# Optimizing a Trainium2 kernel written in Bass

```python
import jax, jax.numpy as jnp
from jax import lax
import numpy as np

D_MODEL = 1024
BATCH = 1
SEQ = 512
DEPTH = 1

GRID_W = 64
CTX_LEN = 256
NA_HEADS = 8
NA_HEAD_DIM = 64
NA_WIN_ROWS = 8
NA_WIN_COLS = 16
GLA_HEADS = 4
GLA_DK = 64
GLA_DV = 128
GLA_GATE_RANK = 16
GLA_GATE_TAU = 16.0
GLA_LOG_ALPHA_MIN = -1.0
GLA_CHUNK = 64
ROPE_THETA = 10000.0
D_FF = ((8 * D_MODEL + 3 * 256 - 1) // (3 * 256)) * 256
N_MOD = 6
NORM_EPS = 1e-6
NEG_INF = -1e30
NA_WIDTH = NA_HEADS * NA_HEAD_DIM
GLA_QK_WIDTH = GLA_HEADS * GLA_DK
GLA_V_WIDTH = GLA_HEADS * GLA_DV
IN_SPLITS = (NA_WIDTH, NA_WIDTH, NA_WIDTH, GLA_QK_WIDTH, GLA_QK_WIDTH, GLA_V_WIDTH, GLA_V_WIDTH,
             2 * GLA_GATE_RANK, D_MODEL, D_MODEL)
IN_OFFSETS = tuple(int(o) for o in np.cumsum(IN_SPLITS)[:-1])
D_IN = sum(IN_SPLITS)


def rmsnorm(x, g):
    xf = x.astype(jnp.float32)
    y = xf * lax.rsqrt(jnp.mean(xf * xf, axis=-1, keepdims=True) + NORM_EPS)
    return (y * g.astype(jnp.float32)).astype(x.dtype)

def modulate(h, shift, scale):
    return h * (1 + scale) + shift

def heads(t, n):
    return t.reshape(*t.shape[:-1], n, -1)

def flip(t):
    return jnp.flip(t, axis=1)

def axial_rope(x, row_pos, col_pos):
    half = x.shape[-1] // 2
    n = half // 2
    freqs = ROPE_THETA ** (-jnp.arange(n, dtype=jnp.float32) / n)

    def rotate(xa, pos):
        ang = pos.astype(jnp.float32)[:, None] * freqs
        cos = jnp.cos(ang)[None, :, None, :]
        sin = jnp.sin(ang)[None, :, None, :]
        x1 = xa[..., :n].astype(jnp.float32)
        x2 = xa[..., n:].astype(jnp.float32)
        return jnp.concatenate([x1 * cos - x2 * sin, x1 * sin + x2 * cos], axis=-1)

    out = jnp.concatenate([rotate(x[..., :half], row_pos), rotate(x[..., half:], col_pos)], axis=-1)
    return out.astype(x.dtype)

def log_decay(z_lr, w_alpha, b_alpha):
    B, L, _ = z_lr.shape
    z = jnp.einsum('bldr,drk->bldk', z_lr.reshape(B, L, 2, GLA_GATE_RANK), w_alpha) + b_alpha
    la = jnp.maximum(jax.nn.log_sigmoid(z.astype(jnp.float32)) / GLA_GATE_TAU, GLA_LOG_ALPHA_MIN)
    la = la.reshape(B, L, 2, GLA_HEADS, GLA_DK)
    return la[:, :, 0], la[:, :, 1]

def gla_chunked(q, k, v, log_a, s0):
    B, L, H, dk = q.shape
    dv = v.shape[-1]
    n = L // GLA_CHUNK
    f32 = jnp.float32
    qc = q.astype(f32).reshape(B, n, GLA_CHUNK, H, dk)
    kc = k.astype(f32).reshape(B, n, GLA_CHUNK, H, dk)
    vc = v.astype(f32).reshape(B, n, GLA_CHUNK, H, dv)
    b = jnp.cumsum(log_a.astype(f32).reshape(B, n, GLA_CHUNK, H, dk), axis=2)
    b_last = b[:, :, -1:]
    q_dec = qc * jnp.exp(b)
    k_inv = kc * jnp.exp(-b)
    k_end = kc * jnp.exp(b_last - b)
    incl = jnp.tril(jnp.ones((GLA_CHUNK, GLA_CHUNK), dtype=bool))
    att = jnp.where(incl, jnp.einsum('bnihd,bnjhd->bnhij', q_dec, k_inv), 0.0)
    o_intra = jnp.einsum('bnhij,bnjhv->bnihv', att, vc)
    u = jnp.einsum('bnjhd,bnjhv->bnhdv', k_end, vc)
    decay = jnp.exp(b_last[:, :, 0])

    def step(s, inp):
        d_n, u_n = inp
        return d_n[..., None] * s + u_n, s

    _, s_prev = lax.scan(step, s0.astype(f32), (jnp.moveaxis(decay, 1, 0), jnp.moveaxis(u, 1, 0)))
    o_inter = jnp.einsum('bnihd,nbhdv->bnihv', q_dec, s_prev)
    return (o_intra + o_inter).reshape(B, L, H, dv)

def gla_final_state(k, v, log_a):
    b = jnp.cumsum(log_a.astype(jnp.float32), axis=1)
    w = jnp.exp(b[:, -1:] - b)
    return jnp.einsum('blhd,blhv->bhdv', k.astype(jnp.float32) * w, v.astype(jnp.float32))

def gla_bidir(q, k, v, la_f, la_b, s0_f, s0_b):
    o_f = gla_chunked(q, k, v, la_f, s0_f)
    o_b = flip(gla_chunked(flip(q), flip(k), flip(v), flip(la_b), s0_b))
    return o_f + o_b

def neighborhood_attention(q, k, v, k_ctx, v_ctx, rpb):
    B, L, H, Dh = q.shape
    rows = L // GRID_W
    kh = min(NA_WIN_ROWS, rows)
    kw = NA_WIN_COLS
    r = jnp.arange(rows)
    row_start = jnp.clip(r - kh // 2, 0, rows - kh)
    key_rows = row_start[:, None] + jnp.arange(kh)[None, :]
    cidx = jnp.arange(GRID_W)
    col_start = jnp.clip(cidx - kw // 2, 0, GRID_W - kw)
    in_win = (cidx[None, :] >= col_start[:, None]) & (cidx[None, :] < col_start[:, None] + kw)
    mask = jnp.broadcast_to(in_win[:, None, :], (GRID_W, kh, GRID_W)).reshape(GRID_W, kh * GRID_W)
    dr = key_rows - r[:, None]
    dc = jnp.clip(cidx[None, :] - cidx[:, None], -(kw - 1), kw - 1)
    bias = rpb.astype(jnp.float32)[:, dr[:, None, :, None] + NA_WIN_ROWS - 1,
                                   dc[None, :, None, :] + kw - 1]
    bias = bias.reshape(H, rows, GRID_W, kh * GRID_W)

    qg = q.reshape(B, rows, GRID_W, H, Dh)
    kb = k.reshape(B, rows, GRID_W, H, Dh)[:, key_rows].reshape(B, rows, kh * GRID_W, H, Dh)
    vb = v.reshape(B, rows, GRID_W, H, Dh)[:, key_rows].reshape(B, rows, kh * GRID_W, H, Dh)
    scale = NA_HEAD_DIM ** -0.5
    s_loc = jnp.einsum('brqhd,brkhd->bhrqk', qg, kb).astype(jnp.float32) * scale + bias
    s_loc = jnp.where(mask, s_loc, NEG_INF)
    s_ctx = jnp.einsum('brqhd,bkhd->bhrqk', qg, k_ctx).astype(jnp.float32) * scale
    p = jax.nn.softmax(jnp.concatenate([s_loc, s_ctx], axis=-1), axis=-1).astype(v.dtype)
    n_loc = kh * GRID_W
    o = (jnp.einsum('bhrqk,brkhd->brqhd', p[..., :n_loc], vb)
         + jnp.einsum('bhrqk,bkhd->brqhd', p[..., n_loc:], v_ctx))
    return o.reshape(B, L, H * Dh)

def context_attention(q, k, v):
    s = jnp.einsum('bqhd,bkhd->bhqk', q, k).astype(jnp.float32) * NA_HEAD_DIM ** -0.5
    p = jax.nn.softmax(s, axis=-1).astype(v.dtype)
    o = jnp.einsum('bhqk,bkhd->bqhd', p, v)
    return o.reshape(*o.shape[:2], -1)

def merge_branches(o_na, o_gla, og, m_a, m_b, gla_norm_g, w_br_na, w_br_gla, w_o):
    o_gla = rmsnorm(o_gla, gla_norm_g)
    o_gla = o_gla.reshape(*o_gla.shape[:2], -1).astype(og.dtype) * jax.nn.silu(og)
    y = jax.nn.sigmoid(m_a) * (o_na @ w_br_na) + jax.nn.sigmoid(m_b) * (o_gla @ w_br_gla)
    return y @ w_o

def swiglu(h, w_gate, w_up, w_down):
    return (jax.nn.silu(h @ w_gate) * (h @ w_up)) @ w_down

def first_inputs(seed: int = 0) -> dict:
    key = jax.random.key(seed)
    ks = jax.random.split(key, 21)

    def nrm(k, shape, s):
        return jax.random.normal(k, shape, jnp.float32) * s

    L = DEPTH
    return {
        "x": nrm(ks[0], (BATCH, SEQ, D_MODEL), 1.0),
        "c": nrm(ks[1], (BATCH, D_MODEL), 1.0),
        "ctx": nrm(ks[2], (BATCH, CTX_LEN, D_MODEL), 1.0),
        "c_ctx": nrm(ks[3], (D_MODEL,), 1.0),
        "w_mod": nrm(ks[4], (L, D_MODEL, N_MOD * D_MODEL), 0.5 * D_MODEL ** -0.5),
        "b_mod": nrm(ks[5], (L, N_MOD * D_MODEL), 0.02),
        "norm1_g": 1.0 + nrm(ks[6], (L, D_MODEL), 0.05),
        "norm2_g": 1.0 + nrm(ks[7], (L, D_MODEL), 0.05),
        "w_in": nrm(ks[8], (L, D_MODEL, D_IN), D_MODEL ** -0.5),
        "na_q_norm_g": 1.0 + nrm(ks[9], (L, NA_HEAD_DIM), 0.05),
        "na_k_norm_g": 1.0 + nrm(ks[10], (L, NA_HEAD_DIM), 0.05),
        "na_rpb": nrm(ks[11], (L, NA_HEADS, 2 * NA_WIN_ROWS - 1, 2 * NA_WIN_COLS - 1), 0.5),
        "gla_w_alpha": nrm(ks[12], (L, 2, GLA_GATE_RANK, GLA_QK_WIDTH), GLA_GATE_RANK ** -0.5),
        "gla_b_alpha": 1.0 + nrm(ks[13], (L, 2, GLA_QK_WIDTH), 0.5),
        "gla_norm_g": 1.0 + nrm(ks[14], (L, GLA_DV), 0.05),
        "w_branch_na": nrm(ks[15], (L, NA_WIDTH, D_MODEL), NA_WIDTH ** -0.5),
        "w_branch_gla": nrm(ks[16], (L, GLA_V_WIDTH, D_MODEL), GLA_V_WIDTH ** -0.5),
        "w_out": nrm(ks[17], (L, D_MODEL, D_MODEL), D_MODEL ** -0.5),
        "w_ffn_gate": nrm(ks[18], (L, D_MODEL, D_FF), D_MODEL ** -0.5),
        "w_ffn_up": nrm(ks[19], (L, D_MODEL, D_FF), D_MODEL ** -0.5),
        "w_ffn_down": nrm(ks[20], (L, D_FF, D_MODEL), D_FF ** -0.5),
    }

def first_block(x, c, ctx, c_ctx, w_mod, b_mod, norm1_g, norm2_g, w_in, na_q_norm_g, na_k_norm_g, na_rpb,
              gla_w_alpha, gla_b_alpha, gla_norm_g, w_branch_na, w_branch_gla, w_out,
              w_ffn_gate, w_ffn_up, w_ffn_down):
    B, L, _ = x.shape
    t = jnp.arange(L)
    row_pos, col_pos = t // GRID_W, t % GRID_W
    for layer in range(DEPTH):
        mod = jax.nn.silu(c) @ w_mod[layer] + b_mod[layer]
        mod_c = jax.nn.silu(c_ctx) @ w_mod[layer] + b_mod[layer]
        sh1, sc1, g1, sh2, sc2, g2 = jnp.split(mod[:, None, :], N_MOD, axis=-1)
        sh1c, sc1c, g1c, sh2c, sc2c, g2c = jnp.split(mod_c, N_MOD, axis=-1)
        (wq_na, wk_na, wv_na, wq_g, wk_g, wv_g, w_og, w_lr, w_ma, w_mb) = jnp.split(w_in[layer], IN_OFFSETS, axis=1)

        h = modulate(rmsnorm(x, norm1_g[layer]), sh1, sc1)
        hc = modulate(rmsnorm(ctx, norm1_g[layer]), sh1c, sc1c)

        k_na_c = rmsnorm(heads(hc @ wk_na, NA_HEADS), na_k_norm_g[layer])
        v_na_c = heads(hc @ wv_na, NA_HEADS)
        k_g_c = heads(hc @ wk_g, GLA_HEADS)
        v_g_c = heads(hc @ wv_g, GLA_HEADS)
        la_f_c, la_b_c = log_decay(hc @ w_lr, gla_w_alpha[layer], gla_b_alpha[layer])
        s_ctx_f = gla_final_state(k_g_c, v_g_c, la_f_c)
        s_ctx_b = gla_final_state(flip(k_g_c), flip(v_g_c), flip(la_b_c))

        (q_na, k_na, v_na, q_g, k_g, v_g, og, z_lr, m_a, m_b) = jnp.split(h @ w_in[layer], IN_OFFSETS, axis=-1)
        q_na = rmsnorm(heads(q_na, NA_HEADS), na_q_norm_g[layer])
        k_na = rmsnorm(heads(k_na, NA_HEADS), na_k_norm_g[layer])
        o_na = neighborhood_attention(q_na, k_na, heads(v_na, NA_HEADS), k_na_c, v_na_c, na_rpb[layer])
        q_g = axial_rope(heads(q_g, GLA_HEADS), row_pos, col_pos) * GLA_DK ** -0.5
        k_g = axial_rope(heads(k_g, GLA_HEADS), row_pos, col_pos)
        la_f, la_b = log_decay(z_lr, gla_w_alpha[layer], gla_b_alpha[layer])
        o_g = gla_bidir(q_g, k_g, heads(v_g, GLA_HEADS), la_f, la_b, s_ctx_f, s_ctx_b)
        mix = merge_branches(o_na, o_g, og, m_a, m_b, gla_norm_g[layer],
                             w_branch_na[layer], w_branch_gla[layer], w_out[layer])

        if layer + 1 < DEPTH:
            q_na_c = rmsnorm(heads(hc @ wq_na, NA_HEADS), na_q_norm_g[layer])
            o_na_c = context_attention(q_na_c, k_na_c, v_na_c)
            s_zero = jnp.zeros((B, GLA_HEADS, GLA_DK, GLA_DV), jnp.float32)
            q_g_c = heads(hc @ wq_g, GLA_HEADS) * GLA_DK ** -0.5
            o_g_c = gla_bidir(q_g_c, k_g_c, v_g_c, la_f_c, la_b_c, s_zero, s_zero)
            mix_c = merge_branches(o_na_c, o_g_c, hc @ w_og, hc @ w_ma, hc @ w_mb, gla_norm_g[layer],
                                   w_branch_na[layer], w_branch_gla[layer], w_out[layer])
            ctx = ctx + g1c * mix_c
            hc2 = modulate(rmsnorm(ctx, norm2_g[layer]), sh2c, sc2c)
            ctx = ctx + g2c * swiglu(hc2, w_ffn_gate[layer], w_ffn_up[layer], w_ffn_down[layer])

        x = x + g1 * mix
        h2 = modulate(rmsnorm(x, norm2_g[layer]), sh2, sc2)
        x = x + g2 * swiglu(h2, w_ffn_gate[layer], w_ffn_up[layer], w_ffn_down[layer])
    return x


DEPTH_2 = 2

MLA_HEADS = 8
MLA_NOPE = 64
MLA_ROPE = 32
MLA_V = 64
MLA_Q_RANK = 256
MLA_KV_RANK = 128
Q_BLOCK = 128
CONV_CH = 512
CONV_WIDTH = 31
RET_HEADS = 4
RET_DK = 128
RET_DV = 256
RET_CHUNK = 128
FFN_HIDDEN = -(-8 * D_MODEL // (3 * 256)) * 256
N_BRANCH = 3
ROPE_BASE = 10000.0
EPS = 1e-6

IN_SPLITS_2 = (MLA_Q_RANK, MLA_KV_RANK, MLA_ROPE, 2 * CONV_CH,
             RET_HEADS * RET_DK, RET_HEADS * RET_DK, RET_HEADS * RET_DV, RET_HEADS * RET_DV,
             N_BRANCH * D_MODEL)
IN_COLS = (MLA_Q_RANK + MLA_KV_RANK + MLA_ROPE + 2 * CONV_CH + 2 * RET_HEADS * RET_DK
           + 2 * RET_HEADS * RET_DV + N_BRANCH * D_MODEL)


def rms_norm(x, g):
    xf = x.astype(jnp.float32)
    y = xf * lax.rsqrt(jnp.mean(xf * xf, -1, keepdims=True) + EPS)
    return (y * g.astype(jnp.float32)).astype(x.dtype)

def layer_norm(x, g, b):
    xf = x.astype(jnp.float32)
    mu = jnp.mean(xf, -1, keepdims=True)
    var = jnp.mean(jnp.square(xf - mu), -1, keepdims=True)
    y = (xf - mu) * lax.rsqrt(var + EPS)
    return (y * g.astype(jnp.float32) + b.astype(jnp.float32)).astype(x.dtype)

def rope_tables(positions, dim):
    inv = ROPE_BASE ** (-jnp.arange(0, dim, 2, dtype=jnp.float32) / dim)
    ang = positions.astype(jnp.float32)[..., None] * inv
    return jnp.cos(ang), jnp.sin(ang)

def apply_rope(x, cos, sin):
    if x.ndim == 4:
        cos, sin = cos[:, :, None, :], sin[:, :, None, :]
    cos, sin = cos.astype(x.dtype), sin.astype(x.dtype)
    x1, x2 = jnp.split(x, 2, axis=-1)
    return jnp.concatenate([x1 * cos - x2 * sin, x2 * cos + x1 * sin], axis=-1)

def mla_branch(c_q, c_kv, k_pe, cos, sin, q_norm, w_uq, kv_norm, w_ukv, w_o):
    B, S, _ = c_q.shape
    q = (rms_norm(c_q, q_norm) @ w_uq).reshape(B, S, MLA_HEADS, MLA_NOPE + MLA_ROPE)
    q_nope = q[..., :MLA_NOPE]
    q_pe = apply_rope(q[..., MLA_NOPE:], cos, sin)
    kv = (rms_norm(c_kv, kv_norm) @ w_ukv).reshape(B, S, MLA_HEADS, MLA_NOPE + MLA_V)
    k_nope, v = kv[..., :MLA_NOPE], kv[..., MLA_NOPE:]
    k_pe = apply_rope(k_pe, cos, sin)
    scale = (MLA_NOPE + MLA_ROPE) ** -0.5
    nq = S // Q_BLOCK
    qn_b = q_nope.reshape(B, nq, Q_BLOCK, MLA_HEADS, MLA_NOPE).swapaxes(0, 1)
    qp_b = q_pe.reshape(B, nq, Q_BLOCK, MLA_HEADS, MLA_ROPE).swapaxes(0, 1)

    def block(args):
        qn, qp = args
        s = (jnp.einsum('bqhd,bkhd->bhqk', qn, k_nope)
             + jnp.einsum('bqhr,bkr->bhqk', qp, k_pe))
        p = jax.nn.softmax(s.astype(jnp.float32) * scale, axis=-1).astype(v.dtype)
        return jnp.einsum('bhqk,bkhd->bqhd', p, v)

    o = lax.map(block, (qn_b, qp_b))
    o = o.swapaxes(0, 1).reshape(B, S, MLA_HEADS * MLA_V)
    return o @ w_o

def conv_branch(u, w_dw, b_dw, ln_g, ln_b, w_pw):
    a, gate = jnp.split(u, 2, axis=-1)
    a = a * jax.nn.sigmoid(gate)
    y = lax.conv_general_dilated(
        a, w_dw[:, None, :].astype(a.dtype), window_strides=(1,),
        padding=[(CONV_WIDTH // 2, CONV_WIDTH // 2)],
        dimension_numbers=('NWC', 'WIO', 'NWC'), feature_group_count=CONV_CH) + b_dw
    y = jax.nn.silu(layer_norm(y, ln_g, ln_b))
    return y @ w_pw

def retention_direction(q, k, v, log_gamma, strict):
    C = q.shape[3]
    idx = jnp.arange(C, dtype=jnp.float32)
    diff = idx[:, None] - idx[None, :]
    mask = (diff > 0) if strict else (diff >= 0)
    lg = log_gamma[:, None, None]
    decay = jnp.where(mask, jnp.exp(jnp.where(mask, diff, 0.0) * lg), 0.0).astype(q.dtype)
    scores = jnp.einsum('bhnqd,bhnkd->bhnqk', q, k) * decay[None, :, None]
    inner = jnp.einsum('bhnqk,bhnke->bhnqe', scores, v)
    k_dec = k * jnp.exp((C - 1 - idx)[None, :] * log_gamma[:, None]).astype(k.dtype)[None, :, None, :, None]
    u = jnp.einsum('bhnkd,bhnke->nbhde', k_dec, v)
    chunk_decay = jnp.exp(C * log_gamma).astype(u.dtype)[None, :, None, None]

    def step(state, xs):
        q_c, u_c = xs
        out = jnp.einsum('bhqd,bhde->bhqe', q_c, state)
        return chunk_decay * state + u_c, out

    state0 = jnp.zeros(u.shape[1:], u.dtype)
    _, cross = lax.scan(step, state0, (jnp.moveaxis(q, 2, 0), u))
    cross = jnp.moveaxis(cross, 0, 2) * jnp.exp((idx + 1)[None, :] * log_gamma[:, None]).astype(q.dtype)[None, :, None, :, None]
    return inner + cross

def retention_branch(q, k, v, g, cos, sin, decay_logits, gn_g, w_o):
    B, S, _ = q.shape
    nc = S // RET_CHUNK
    q = apply_rope(q.reshape(B, S, RET_HEADS, RET_DK), cos, sin)
    k = apply_rope(k.reshape(B, S, RET_HEADS, RET_DK), cos, sin) * (RET_DK ** -0.5)
    v = v.reshape(B, S, RET_HEADS, RET_DV)

    def chunked(t):
        return t.reshape(B, nc, RET_CHUNK, RET_HEADS, -1).transpose(0, 3, 1, 2, 4)

    def unchunk(t):
        return t.transpose(0, 2, 3, 1, 4).reshape(B, S, RET_HEADS, -1)

    def flip(t):
        return jnp.flip(t, axis=1)

    log_gamma = jax.nn.log_sigmoid(decay_logits.astype(jnp.float32))
    fwd = retention_direction(chunked(q), chunked(k), chunked(v), log_gamma[0], False)
    bwd = retention_direction(chunked(flip(q)), chunked(flip(k)), chunked(flip(v)), log_gamma[1], True)
    o = unchunk(fwd) + flip(unchunk(bwd))
    of = o.astype(jnp.float32)
    mu = jnp.mean(of, -1, keepdims=True)
    var = jnp.mean(jnp.square(of - mu), -1, keepdims=True)
    on = ((of - mu) * lax.rsqrt(var + EPS)).reshape(B, S, RET_HEADS * RET_DV)
    on = (on * gn_g.astype(jnp.float32)).astype(g.dtype)
    return (jax.nn.silu(g) * on) @ w_o

def second_inputs(seed: int = 0) -> dict:
    key = jax.random.key(seed)
    ks = jax.random.split(key, 32)
    f32 = jnp.float32

    def w(k, shape, fan_in):
        return jax.random.normal(k, shape, f32) * (fan_in ** -0.5)

    def gain(k, shape):
        return 1.0 + 0.02 * jax.random.normal(k, shape, f32)

    def bias(k, shape):
        return 0.02 * jax.random.normal(k, shape, f32)

    L = DEPTH_2
    x = jax.random.normal(ks[0], (BATCH, SEQ, D_MODEL), f32)
    offset = jax.random.randint(ks[1], (BATCH, 1), 0, SEQ, dtype=jnp.int32)
    positions = offset + jnp.arange(SEQ, dtype=jnp.int32)[None, :]
    k_exp = 5.0 + jnp.arange(RET_HEADS, dtype=f32)
    base_logit = jnp.log(jnp.exp2(k_exp) - 1.0)
    ret_decay_logits = base_logit[None, None, :] + 0.1 * jax.random.normal(ks[2], (L, 2, RET_HEADS), f32)
    return {
        "x": x,
        "positions": positions,
        "ln_mix_pre": gain(ks[3], (L, D_MODEL)),
        "ln_mix_post": gain(ks[4], (L, D_MODEL)),
        "ln_ffn_pre": gain(ks[5], (L, D_MODEL)),
        "ln_ffn_post": gain(ks[6], (L, D_MODEL)),
        "w_in": w(ks[7], (L, D_MODEL, IN_COLS), D_MODEL),
        "mla_q_norm": gain(ks[8], (L, MLA_Q_RANK)),
        "mla_w_uq": w(ks[9], (L, MLA_Q_RANK, MLA_HEADS * (MLA_NOPE + MLA_ROPE)), MLA_Q_RANK),
        "mla_kv_norm": gain(ks[10], (L, MLA_KV_RANK)),
        "mla_w_ukv": w(ks[11], (L, MLA_KV_RANK, MLA_HEADS * (MLA_NOPE + MLA_V)), MLA_KV_RANK),
        "mla_w_o": w(ks[12], (L, MLA_HEADS * MLA_V, D_MODEL), MLA_HEADS * MLA_V),
        "conv_w_dw": w(ks[13], (L, CONV_WIDTH, CONV_CH), CONV_WIDTH),
        "conv_b_dw": bias(ks[14], (L, CONV_CH)),
        "conv_ln_g": gain(ks[15], (L, CONV_CH)),
        "conv_ln_b": bias(ks[16], (L, CONV_CH)),
        "conv_w_pw": w(ks[17], (L, CONV_CH, D_MODEL), CONV_CH),
        "ret_decay_logits": ret_decay_logits,
        "ret_gn_g": gain(ks[18], (L, RET_HEADS * RET_DV)),
        "ret_w_o": w(ks[19], (L, RET_HEADS * RET_DV, D_MODEL), RET_HEADS * RET_DV),
        "w_out": w(ks[20], (L, D_MODEL, D_MODEL), D_MODEL),
        "ffn_w_gate": w(ks[21], (L, D_MODEL, FFN_HIDDEN), D_MODEL),
        "ffn_w_up": w(ks[22], (L, D_MODEL, FFN_HIDDEN), D_MODEL),
        "ffn_w_down": w(ks[23], (L, FFN_HIDDEN, D_MODEL), FFN_HIDDEN),
    }

def second_block(x, positions, ln_mix_pre, ln_mix_post, ln_ffn_pre, ln_ffn_post, w_in,
              mla_q_norm, mla_w_uq, mla_kv_norm, mla_w_ukv, mla_w_o,
              conv_w_dw, conv_b_dw, conv_ln_g, conv_ln_b, conv_w_pw,
              ret_decay_logits, ret_gn_g, ret_w_o, w_out,
              ffn_w_gate, ffn_w_up, ffn_w_down):
    B, S, _ = x.shape
    points = np.cumsum(IN_SPLITS_2)[:-1].tolist()
    cos_m, sin_m = rope_tables(positions, MLA_ROPE)
    cos_r, sin_r = rope_tables(positions, RET_DK)
    for l in range(DEPTH_2):
        h = rms_norm(x, ln_mix_pre[l])
        proj = h @ w_in[l]
        c_q, c_kv, k_pe, conv_u, r_q, r_k, r_v, r_g, gate_logits = jnp.split(proj, points, axis=-1)
        y_mla = mla_branch(c_q, c_kv, k_pe, cos_m, sin_m, mla_q_norm[l], mla_w_uq[l],
                           mla_kv_norm[l], mla_w_ukv[l], mla_w_o[l])
        y_conv = conv_branch(conv_u, conv_w_dw[l], conv_b_dw[l], conv_ln_g[l], conv_ln_b[l], conv_w_pw[l])
        y_ret = retention_branch(r_q, r_k, r_v, r_g, cos_r, sin_r, ret_decay_logits[l],
                                 ret_gn_g[l], ret_w_o[l])
        gates = jax.nn.sigmoid(gate_logits).reshape(B, S, N_BRANCH, D_MODEL)
        merged = gates[:, :, 0] * y_mla + gates[:, :, 1] * y_conv + gates[:, :, 2] * y_ret
        x = x + rms_norm(merged @ w_out[l], ln_mix_post[l])
        h = rms_norm(x, ln_ffn_pre[l])
        f = (jax.nn.silu(h @ ffn_w_gate[l]) * (h @ ffn_w_up[l])) @ ffn_w_down[l]
        x = x + rms_norm(f, ln_ffn_post[l])
    return x


def setup_inputs(seed=0):
    out = dict(first_inputs(seed))
    for name, value in second_inputs(seed + 1).items():
        if name != "x":
            out[name + "_2"] = value
    return out


def reference(
    x, c, ctx, c_ctx, w_mod, b_mod, norm1_g, norm2_g, w_in, na_q_norm_g, na_k_norm_g, na_rpb,
    gla_w_alpha, gla_b_alpha, gla_norm_g, w_branch_na, w_branch_gla, w_out, w_ffn_gate,
    w_ffn_up, w_ffn_down, positions_2, ln_mix_pre_2, ln_mix_post_2, ln_ffn_pre_2, ln_ffn_post_2,
    w_in_2, mla_q_norm_2, mla_w_uq_2, mla_kv_norm_2, mla_w_ukv_2, mla_w_o_2, conv_w_dw_2,
    conv_b_dw_2, conv_ln_g_2, conv_ln_b_2, conv_w_pw_2, ret_decay_logits_2, ret_gn_g_2,
    ret_w_o_2, w_out_2, ffn_w_gate_2, ffn_w_up_2, ffn_w_down_2,
):
    x = first_block(
        x, c, ctx, c_ctx, w_mod, b_mod, norm1_g, norm2_g, w_in, na_q_norm_g, na_k_norm_g,
        na_rpb, gla_w_alpha, gla_b_alpha, gla_norm_g, w_branch_na, w_branch_gla, w_out,
        w_ffn_gate, w_ffn_up, w_ffn_down,
    )
    return second_block(
        x, positions_2, ln_mix_pre_2, ln_mix_post_2, ln_ffn_pre_2, ln_ffn_post_2, w_in_2,
        mla_q_norm_2, mla_w_uq_2, mla_kv_norm_2, mla_w_ukv_2, mla_w_o_2, conv_w_dw_2,
        conv_b_dw_2, conv_ln_g_2, conv_ln_b_2, conv_w_pw_2, ret_decay_logits_2, ret_gn_g_2,
        ret_w_o_2, w_out_2, ffn_w_gate_2, ffn_w_up_2, ffn_w_down_2,
    )


_drawn_inputs = setup_inputs


def setup_inputs(seed=0):
    import zlib

    import numpy as np

    out = dict(_drawn_inputs(seed))
    spreads = {}
    factors = {'na_q_norm_g': 8.0,
     'na_k_norm_g': 8.0,
     'na_rpb': 5.838,
     'gla_norm_g': 4.972,
     'ln_ffn_post_2': 3.261,
     'mla_q_norm_2': 8.0,
     'mla_kv_norm_2': 8.0,
     'conv_ln_g_2': 11.345,
     'conv_ln_b_2': 11.568,
     'ret_gn_g_2': 13.002}
    for name, (base, spread) in spreads.items():
        noise = np.random.default_rng([zlib.crc32(name.encode()), seed]).standard_normal(out[name].shape)
        drawn = base * np.exp(spread * noise) if base else spread * noise
        out[name] = __import__('jax').numpy.asarray(drawn.astype(out[name].dtype))
    for name, factor in factors.items():
        out[name] = (out[name] * factor).astype(out[name].dtype)
    return out
```

```python
from contextlib import ExitStack

import numpy as np

import concourse.bass as bass
from concourse import mybir

F32 = mybir.dt.float32
F32R = mybir.dt.float32r
I32 = mybir.dt.int32
ACT = mybir.ActivationFunctionType
ALU = mybir.AluOpType
AX = mybir.AxisListType.X

T = 512
TC = 256
EPS = 1e-6
FT = 22
FH = 11
NB = 429
NPAGE = 72
ROUND = 12582912.0
C1 = 6.28125
C2 = float(np.floor((2 * np.pi - C1) * 2.0**20) / 2.0**20)
C3 = float(2 * np.pi - C1 - C2)
PI_IN = 3.1415925
NA_K0 = [0, 64, 192, 256]

PARAMS = [
    ("eps", 1), ("one", 1), ("halfpi", 1), ("neg20", 1),
    ("b_mod", 48), ("norm1_g", 8), ("norm2_g", 8), ("na_q_g", 1), ("na_k_g", 1), ("b_alpha", 4),
    ("gla_norm_g", 1), ("inv_m", 1), ("sgn_m", 1), ("inv_r", 1), ("sgn_r", 1), ("decay", 16),
]
for _l in range(2):
    PARAMS += [(f"{n}{_l}", c) for n, c in (
        ("mix_pre", 8), ("mix_post", 8), ("ffn_pre", 8), ("ffn_post", 8), ("q_norm", 2), ("kv_norm", 1),
        ("w_dw", 124), ("b_dw", 4), ("cln_g", 4), ("cln_b", 4), ("gn_g", 8))]
PCOL = {}
NPC = 0
for _n, _c in PARAMS:
    PCOL[_n] = (NPC, _c)
    NPC += _c


class Note:

    def activation(self, *a, **k):
        return lambda e: e.activation(*a, **k)

    def tensor_tensor(self, *a, **k):
        return lambda e: e.tensor_tensor(*a, **k)

    def tensor_scalar(self, *a, **k):
        return lambda e: e.tensor_scalar(*a, **k)

    def scalar_tensor_tensor(self, *a, **k):
        return lambda e: e.scalar_tensor_tensor(*a, **k)

    def tensor_tensor_scan(self, *a, **k):
        return lambda e: e.tensor_tensor_scan(*a, **k)

    def tensor_reduce(self, *a, **k):
        return lambda e: e.tensor_reduce(*a, **k)

    def tensor_copy(self, *a, **k):
        return lambda e: e.tensor_copy(*a, **k)

    def reciprocal(self, *a, **k):
        return lambda e: e.reciprocal(*a, **k)

    def matmul(self, *a, **k):
        return lambda e: e.matmul(*a, **k)

    def transpose(self, *a, **k):
        return lambda e: e.transpose(*a, **k)

    def dma_start(self, *a, **k):
        return lambda e: e.dma_start(*a, **k)

    def wait_ge(self, *a, **k):
        return lambda e: e.wait_ge(*a, **k)


NOTE = Note()


class Lane:

    def __init__(self, sem):
        self.sem, self.ops, self.count, self.seen = sem, [], 0, {}

    def wait(self, *tokens):
        for t in tokens:
            if isinstance(t, list):
                self.wait(*t)
                continue
            sem, value = t
            if self.seen.get(id(sem), 0) < value:
                self.seen[id(sem)] = value
                self.ops.append(lambda e, s=sem, v=value: e.wait_ge(s, v))

    def do(self, fn, *tokens):
        self.wait(*tokens)
        self.count += 1
        op = fn(NOTE)
        self.ops.append(lambda e: op(e).then_inc(self.sem, 1))
        return (self.sem, self.count)

    def quiet(self, fn, *tokens):
        self.wait(*tokens)
        self.ops.append(fn(NOTE))

    def dma(self, sem, dst, src, *tokens):
        self.wait(*tokens)
        self.ops.append(lambda e: e.dma_start(dst, src).then_inc(sem, 16))

    def now(self):
        return (self.sem, self.count)

    def play(self, e):
        for op in self.ops:
            op(e)


class Page:
    def __init__(self, f, r):
        self.f, self.r, self.after = f, r, []


class Slots:

    def __init__(self, pages):
        self.free = list(pages)

    def take(self):
        return self.free.pop(0)

    def give(self, page, *tokens):
        page.after = list(tokens)
        self.free.append(page)


def weave(main, sides, every):
    sides = [s for s in sides]
    n = 0
    for _ in main:
        n += 1
        if n % every == 0:
            sides = [s for s in sides if next(s, "end") != "end"]
    for _ in range(100000):
        sides = [s for s in sides if next(s, "end") != "end"]
        if not sides:
            return
    raise ValueError("a side waits for what is never queued")


def program(nc, a, out, order, probe):
    with ExitStack() as ctx:
        def sb(name, shape, dt=F32):
            return ctx.enter_context(nc.sbuf_tensor(name, shape, dt))

        def sem(name):
            return ctx.enter_context(nc.semaphore(name))

        both = []
        for i in range(NPAGE):
            with nc.sbuf_tensor(f"pageF{i}", [128, 512], F32) as pf:
                pass
            both.append((pf, sb(f"pageR{i}", [128, 512], F32R)))
        NR, NH = 4, 3
        wraw = sb("wraw", [128, NR, 8, 128])
        whi = sb("whi", [128, NH, 8, 128], F32R)
        wlo = sb("wlo", [128, NH, 8, 128], F32R)
        prm = sb("prm", [128, NPC])
        cst = sb("cst", [128, 5, 128])
        with nc.sbuf_tensor("tabG", [128, 1792], F32) as tabG:
            pass
        tabA = sb("tabA", [128, 1792])
        wal = sb("wal", [32, 2, 256])
        csil = sb("csil", [128, 8, 2])
        ccol = sb("ccol", [128, 8, 2])
        modc = sb("modc", [128, 16, 2])
        modr = sb("modr", [128, 32])
        A1 = sb("A1", [128, 8, 2])
        A2 = sb("A2", [128, 8])
        smal = sb("smal", [128, 256])
        xcb = sb("xcb", [128, TC])
        banks = [ctx.enter_context(nc.psum_tensor(f"bank{i}", [128, 512], F32)) for i in range(8)]

        pe, act, dve, pool, sp = (Lane(sem(n)) for n in ("s_pe", "s_act", "s_dve", "s_pool", "s_sp"))
        s_w = [sem(f"s_w{i}") for i in range(NR)]
        s_in = sem("s_in")
        s_pg = [sem(f"s_pg{i}") for i in range(132)]
        s_out = sem("s_out")

        pages = Slots([Page(f[:, :], r[:, :]) for f, r in both])
        mb = Slots([Page(b, None) for b in banks[0:4]])
        sbk = Slots([Page(b, None) for b in banks[4:8]])
        for p in mb.free + sbk.free:
            p.f = p.f[:, :]

        ident, ones, bones = cst[:, 0, :], cst[:, 1, :], cst[:, 2, :]
        maskF, maskB = cst[:, 3, :], cst[:, 4, :]
        gcos, gsin, smask = tabG[:, 0:512], tabG[:, 512:1024], tabG[:, 1024:1792]
        rA1, rA2 = tabA[:, 0:896], tabA[:, 896:1792]
        tabD = sb("tabD", [128, 896])[:, :]

        def col(name, i=0, n=1):
            o = PCOL[name][0] + i
            return prm[:, o:o + n]

        def bc(ap):
            return ap.bitcast(F32)

        dma_n = [0]

        def load(dst, src, *tokens):
            n = dma_n[0]
            dma_n[0] += 1
            s = s_pg[n % len(s_pg)]
            sp.dma(s, dst, src, *tokens)
            return (s, 16 * (n // len(s_pg) + 1))

        st = {"n": 0, "dma": 0, "split": 0}
        wtok = {}
        done = {}

        def w_dma(b):
            if b >= NB or b != st["dma"]:
                return
            st["dma"] += 1
            waits = [wtok[b - NR][0], wtok[b - NR][1]] if b >= NR else []
            sp.dma(s_w[b % NR], wraw[:, b % NR, :, :], a["wst"][b], *waits)

        def w_split(b):
            if b >= NB or b != st["split"]:
                return
            st["split"] += 1
            raw, hi, lo = wraw[:, b % NR, :, :], whi[:, b % NH, :, :], wlo[:, b % NH, :, :]
            landed = (s_w[b % NR], 16 * (b // NR + 1))
            waits = [done[b - NH]] if b >= NH else []
            h = act.do(lambda e: e.activation(hi, raw, ACT.Copy), landed, *waits)
            l = pool.do(lambda e: e.tensor_tensor(lo, raw, bc(hi), ALU.subtract), landed, h, *waits)
            wtok[b] = (h, l)
            w_dma(b + NR)

        def w_next(key):
            s = len(order)
            order.append(key)
            b = s // 8
            if s % 8 == 0:
                w_split(b + NH - 1)
                pe.wait(*wtok[b])
            return b, whi[:, b % NH, s % 8, :], wlo[:, b % NH, s % 8, :]

        def mm(o, l, r, start, stop, *tokens, skip=False):
            return pe.do(lambda e: e.matmul(o, l, r, start=start, stop=stop, skip_group_check=skip), *tokens)

        def mmq(o, l, r, start, stop, *tokens, skip=False):
            pe.quiet(lambda e: e.matmul(o, l, r, start=start, stop=stop, skip_group_check=skip), *tokens)

        def linear(name, m, kts, groups, step=2):
            tok = None
            for i, k in enumerate(kts):
                b, hi, lo = w_next((name, m, k))
                for o, xs in groups:
                    xh, xl, need = xs[i]
                    mmq(o, hi, xh, i == 0, False, need)
                    mmq(o, hi, xl, False, False)
                    tok = mm(o, lo, xh, False, i == len(kts) - 1)
                done[b] = tok
                if i % step == step - 1:
                    yield
            return tok

        def split(src, hi, lo, *need):
            h = act.do(lambda e: e.activation(hi, src, ACT.Copy), *need)
            l = dve.do(lambda e: e.tensor_tensor(lo, src, bc(hi), ALU.subtract), h, *need)
            return [h, l]

        def split_pages(src, *need):
            H, L = pages.take(), pages.take()
            t = split(src.f, H.r, L.r, H.after, L.after, *need)
            pages.give(src, *t)
            return (H, L, t)

        def xk(pairs):
            return [(H.r, L.r, t) for H, L, t in pairs]

        def give_pairs(pairs, *tokens):
            for H, L, _ in pairs:
                pages.give(H, *tokens)
                pages.give(L, *tokens)

        def rsqrt(vps, width, scale, *need):
            v, r, t = pages.take(), pages.take(), pages.take()
            vf, rf, tf = v.f[:, 0:width], r.f[:, 0:width], t.f[:, 0:width]
            d0 = dve.do(lambda e: e.tensor_scalar(vf, vps, scale, EPS, ALU.mult, ALU.add), v.after, *need)
            a0 = act.do(lambda e: e.activation(rf, vf, ACT.Ln), d0, r.after)
            a1 = act.do(lambda e: e.activation(rf, rf, ACT.Exp, scale=-0.5), a0)
            d1 = dve.do(lambda e: e.tensor_tensor(tf, rf, rf, ALU.mult), a1, t.after)
            d2 = dve.do(lambda e: e.scalar_tensor_tensor(tf, tf, -0.5, vf, ALU.mult, ALU.mult), d1)
            d3 = dve.do(lambda e: e.scalar_tensor_tensor(rf, tf, 1.5, rf, ALU.add, ALU.mult), d2)
            pages.give(v, d2)
            pages.give(t, d3)
            return r, d3, d0

        def sumsq(tiles, width):
            acc = pages.take()
            tok = None
            for i, (ap, need) in enumerate(tiles):
                if i == 0:
                    tok = act.do(lambda e, ap=ap: e.activation(acc.f[:, 0:width], ap, ACT.Square), acc.after, need)
                else:
                    q = pages.take()
                    s = act.do(lambda e, ap=ap, q=q: e.activation(q.f[:, 0:width], ap, ACT.Square), q.after, need)
                    tok = dve.do(lambda e, q=q: e.tensor_tensor(acc.f[:, 0:width], acc.f[:, 0:width],
                                                                q.f[:, 0:width], ALU.add), s, tok)
                    pages.give(q, tok)
            return acc, tok

        def rstd_of(tiles, width, n, mat, bks):
            acc, tok = sumsq(tiles, width)
            p = bks.take()
            m = mm(p.f[:, 0:width], mat, acc.f[:, 0:width], True, True, tok, p.after)
            pages.give(acc, m)
            r, rt, d0 = rsqrt(p.f[:, 0:width], width, 1.0 / n, m)
            bks.give(p, d0)
            return r, rt

        t_prm = load(prm[:, :], a["prm"])
        t_cc = load(ccol[:, :, :], a["ccol"])
        modp = {}

        def mod_load(m):
            for hf in range(2):
                p = pages.take()
                modp[m, hf] = (p, load(p.f.rearrange("p (k n) -> p k n", k=4), a["wmod"][2 * m + hf], p.after))

        for m in range(8):
            mod_load(m)
        X = []
        for k in range(8):
            p = pages.take()
            p.w = [load(p.f, a["xT"][:, k, :], p.after)]
            p.rd = []
            X.append(p)
        XC = []
        for k in range(4):
            p = pages.take()
            XC.append((p, load(p.f, a["cT"][:, k, :], p.after)))
        for m in range(8, 16):
            mod_load(m)
        t_cst = load(cst[:, :, :], a["cst"])
        t_tab = load(tabG[:, :], a["tabG"])
        t_wal = load(wal[:, :, :], a["wal"])
        for b in range(NR):
            w_dma(b)

        t_cs = act.do(lambda e: e.activation(csil[:, :, :], ccol[:, :, :], ACT.Silu), t_cc)

        def mod_mm(m, o, n, *need):
            tok = None
            for hf in range(2):
                p, land = modp.pop((m, hf))
                pe.wait(land, *need)
                w = p.f.rearrange("p (k n) -> p k n", k=4)
                for k in range(4):
                    tok = mm(o, w[:, k, :], csil[:, 4 * hf + k, 0:n], hf == 0 and k == 0, hf == 1 and k == 3)
                pages.give(p, tok)
            return tok

        bm = mb.take()
        for m in range(16):
            t = mod_mm(m, bm.f[:, 2 * m:2 * m + 2], 2, t_cs, bm.after)
        bcast = col("b_mod", 0, 16).unsqueeze(2).broadcast_to([128, 16, 2])
        t_mod = dve.do(lambda e: e.tensor_tensor(modc[:, :, :], bm.f[:, 0:32].rearrange("p (m c) -> p m c", c=2),
                                                 bcast, ALU.add), t, t_prm)
        mb.give(bm, t_mod)
        n1 = col("norm1_g", 0, 8).unsqueeze(2).broadcast_to([128, 8, 2])
        t_A1 = dve.do(lambda e: e.scalar_tensor_tensor(A1[:, :, :], modc[:, 8:16, :], 1.0, n1, ALU.add, ALU.mult),
                      t_mod)

        def ctx_tile(k):
            p, t = XC[k // 2]
            return p.f[:, 256 * (k % 2):256 * (k % 2) + 256], t

        act.wait(t_prm)
        pe.wait(t_cst)
        rx, rxt = rstd_of([(X[k].f, X[k].w) for k in range(8)], T, 1024, ones, mb)
        rc, rct = rstd_of([ctx_tile(k) for k in range(8)], TC, 1024, ones, mb)
        H, HC = [], []
        for k in range(8):
            t = pages.take()
            d = dve.do(lambda e, k=k, t=t: e.scalar_tensor_tensor(t.f, X[k].f, A1[:, k, 0:1], rx.f, ALU.mult,
                                                                 ALU.mult), t.after, X[k].w, t_A1, rxt)
            d2 = dve.do(lambda e, k=k, t=t: e.tensor_scalar(t.f, t.f, modc[:, k, 0:1], None, ALU.add), d)
            H.append(split_pages(t, d2))
        pages.give(rx, d)
        for k in range(8):
            ap, _ = ctx_tile(k)
            t, h = pages.take(), pages.take()
            d = dve.do(lambda e, k=k, t=t, ap=ap: e.scalar_tensor_tensor(
                t.f[:, 0:256], ap, A1[:, k, 1:2], rc.f[:, 0:256], ALU.mult, ALU.mult), t.after, XC[k // 2][1], rct)
            d2 = dve.do(lambda e, k=k, t=t: e.tensor_scalar(t.f[:, 0:256], t.f[:, 0:256], modc[:, k, 1:2], None,
                                                            ALU.add), d)
            s = split(t.f[:, 0:256], h.r[:, 0:256], h.r[:, 256:512], d2, h.after)
            pages.give(t, *s)
            HC.append((h, s))
        pages.give(rc, d)
        for p, _ in XC:
            pages.give(p, d, act.now())

        w_split(0)
        w_split(1)

        R = {}
        hcur = [None]
        K8 = range(8)

        def proj(name, m, xs, ctx=None, step=2, k0=0):
            o = mb.take()
            pe.wait(o.after)
            groups = [(o.f, xs)]
            oc = None
            if ctx is not None:
                oc = mb.take()
                pe.wait(oc.after)
                groups.append((oc.f[:, 0:256], ctx))
            tok = yield from linear(name, m, range(k0, k0 + len(xs)), groups, step)
            return o, oc, tok

        hx = xk(H)
        hcx = [(h.r[:, 0:256], h.r[:, 256:512], s) for h, s in HC]

        def copy_act(dst, src, *need, **kw):
            return act.do(lambda e: e.activation(dst, src, ACT.Copy, **kw), *need)

        def to_tokens(src, offs, width, bks, *need):
            b = bks.take()
            pe.wait(b.after, *need)
            for j, o in enumerate(offs):
                tok = pe.do(lambda e, j=j, o=o: e.transpose(b.f[:, j * 128:(j + 1) * 128], src[:, o:o + 128], ident))
            p = pages.take()
            w = 128 * len(offs)
            c = copy_act(p.f[:, 0:w], b.f[:, 0:w], tok, p.after)
            bks.give(b, c)
            return p, c, tok

        def main_gla():
            o, oc, t = yield from proj("w_lr", 0, hx, hcx)
            z = pages.take()
            zc = pages.take()
            c1 = copy_act(z.f[0:32, :], o.f[0:32, :], t, z.after)
            c2 = copy_act(zc.f[0:32, 0:256], oc.f[0:32, 0:256], t, zc.after)
            mb.give(o, c1)
            mb.give(oc, c2)
            R["z"] = (z, zc, [c1, c2])
            for m in range(2):
                o, oc, t = yield from proj("wk_g", m, hx, hcx)
                R["kg", m] = rope_gla(o, t)
                kc = pages.take()
                c = copy_act(kc.f[:, 0:256], oc.f[:, 0:256], t, kc.after)
                mb.give(oc, c)
                R["kgc", m] = (kc, c)
                o, oc, t = yield from proj("wq_g", m, hx)
                R["qg", m] = rope_gla(o, t)
                for h in (2 * m, 2 * m + 1):
                    o, oc, t = yield from proj("wv_g", h, hx, hcx)
                    v, vc = pages.take(), pages.take()
                    c1 = copy_act(v.f, o.f, t, v.after)
                    c2 = copy_act(vc.f[:, 0:256], oc.f[:, 0:256], t, vc.after)
                    mb.give(o, c1)
                    mb.give(oc, c2)
                    V, tv, r1 = to_tokens(v.f, [0, 128, 256, 384], 512, mb, c1)
                    VC, tvc, r2 = to_tokens(vc.f, [0, 128], 256, mb, c2)
                    pages.give(v, r1)
                    pages.give(vc, r2)
                    R["vg", h] = (V, VC, [tv, tvc])

        def rope_gla(o, t):
            p, q = pages.take(), pages.take()
            d1 = dve.do(lambda e: e.tensor_tensor(p.f, o.f, gcos, ALU.mult), t, p.after, t_tab)
            dve.wait(q.after)
            for a_ in range(4):
                s, d = 32 * (a_ ^ 1), 32 * a_
                d2 = dve.do(lambda e, s=s, d=d: e.tensor_tensor(q.f[d:d + 32, :], o.f[s:s + 32, :],
                                                                gsin[s:s + 32, :], ALU.mult))
            d3 = dve.do(lambda e: e.tensor_tensor(p.f, p.f, q.f, ALU.add), d1, d2)
            mb.give(o, d2)
            pages.give(q, d3)
            return (p, d3)

        def side_gla():
            while "z" not in R:
                yield
            z, zc, tz = R["z"]
            for m in range(2):
                while ("kg", m) not in R:
                    yield
                dirs = []
                for dr in range(2):
                    b1, b2 = sbk.take(), sbk.take()
                    lh = wal[:, dr, 128 * m:128 * m + 128]
                    mmq(b1.f, lh, z.f[0:32, :], True, True, tz, b1.after, t_wal)
                    t = mm(b2.f[:, 0:256], lh, zc.f[0:32, 0:256], True, True, b2.after)
                    la, lac = pages.take(), pages.take()
                    bcol = col("b_alpha", 2 * dr + m)
                    d1 = dve.do(lambda e, la=la, b1=b1, bcol=bcol: e.tensor_scalar(
                        la.f, b1.f, bcol, -20.0, ALU.add, ALU.max), t, la.after)
                    d2 = dve.do(lambda e, lac=lac, b2=b2, bcol=bcol: e.tensor_scalar(
                        lac.f[:, 0:256], b2.f[:, 0:256], bcol, -20.0, ALU.add, ALU.max), lac.after)
                    sbk.give(b1, d1)
                    sbk.give(b2, d2)
                    e1 = act.do(lambda e, la=la: e.activation(la.f, la.f, ACT.Exp, scale=-1.0), d1)
                    e2 = act.do(lambda e, lac=lac: e.activation(lac.f[:, 0:256], lac.f[:, 0:256], ACT.Exp,
                                                                scale=-1.0), d2)
                    dirs.append([la, lac, e1, e2])
                yield
                for dr in range(2):
                    la, lac, e1, e2 = dirs[dr]
                    l1 = act.do(lambda e, la=la: e.activation(la.f, la.f, ACT.Ln, bias=col("one")), e1)
                    l2 = act.do(lambda e, lac=lac: e.activation(lac.f[:, 0:256], lac.f[:, 0:256], ACT.Ln,
                                                                bias=col("one")), e2)
                    d1 = dve.do(lambda e, la=la: e.tensor_scalar(la.f, la.f, -1.0 / 16, -1.0, ALU.mult, ALU.max),
                                l1)
                    d2 = dve.do(lambda e, lac=lac: e.tensor_scalar(lac.f[:, 0:256], lac.f[:, 0:256], -1.0 / 16,
                                                                   -1.0, ALU.mult, ALU.max), l2)
                    P, PC = pages.take(), pages.take()
                    d3 = dve.do(lambda e, la=la, P=P: e.tensor_tensor_scan(P.f, smask[:, 0:512], la.f, 0.0,
                                                                           ALU.mult, ALU.add), d1, P.after, t_tab)
                    d4 = dve.do(lambda e, lac=lac, PC=PC: e.tensor_tensor_scan(
                        PC.f[:, 0:256], smask[:, 512:768], lac.f[:, 0:256], 0.0, ALU.mult, ALU.add), d2, PC.after)
                    dirs[dr] = [la, lac, P, PC, d3, d4]
                yield
                k, tk = R["kg", m]
                q, tq = R["qg", m] if ("qg", m) in R else (None, None)
                while q is None:
                    yield
                    if ("qg", m) in R:
                        q, tq = R["qg", m]
                kc, tkc = R["kgc", m]
                work = []
                for dr in range(2):
                    la, lac, P, PC, d3, d4 = dirs[dr]
                    v3 = P.f.rearrange("p (c t) -> p c t", t=64)
                    o8 = 8 * (2 * m + dr)
                    dec = smal[:, o8:o8 + 8]
                    te = act.do(lambda e, dec=dec, v3=v3: e.activation(dec, v3[:, :, 63], ACT.Exp), d3)
                    if dr == 0:
                        aw = act.do(lambda e, lac=lac, PC=PC: e.activation(
                            lac.f[:, 0:256], PC.f[:, 0:256], ACT.Exp, scale=-1.0, bias=PC.f[:, 255:256]), d4)
                        B, tB = P, d3
                        pages.give(la, d3)
                    else:
                        x1 = dve.do(lambda e, la=la, P=P: e.tensor_tensor(la.f, la.f, P.f, ALU.subtract), d3)
                        tot = v3[:, :, 63:64].broadcast_to([128, 8, 64])
                        tB = dve.do(lambda e, la=la, tot=tot: e.tensor_tensor(
                            la.f.rearrange("p (c t) -> p c t", t=64), la.f.rearrange("p (c t) -> p c t", t=64),
                            tot, ALU.add), x1)
                        x2 = dve.do(lambda e, lac=lac, PC=PC: e.tensor_tensor(
                            lac.f[:, 0:256], PC.f[:, 0:256], lac.f[:, 0:256], ALU.subtract), d4)
                        aw = act.do(lambda e, lac=lac: e.activation(lac.f[:, 0:256], lac.f[:, 0:256], ACT.Exp), x2)
                        pages.give(P, tB, te)
                        B = la
                    E1 = pages.take()
                    a1 = act.do(lambda e, E1=E1, B=B: e.activation(E1.f, B.f, ACT.Exp), tB, E1.after)
                    a2 = act.do(lambda e, B=B: e.activation(B.f, B.f, ACT.Exp, scale=-1.0), a1, te)
                    qd = dve.do(lambda e, E1=E1: e.scalar_tensor_tensor(E1.f, q.f, 0.125, E1.f, ALU.mult,
                                                                        ALU.mult), a1, tq)
                    ki = dve.do(lambda e, B=B: e.tensor_tensor(B.f, k.f, B.f, ALU.mult), a2, tk)
                    KE = pages.take()
                    ke = dve.do(lambda e, KE=KE, B=B, dec=dec: e.tensor_tensor(
                        KE.f.rearrange("p (c t) -> p c t", t=64), B.f.rearrange("p (c t) -> p c t", t=64),
                        dec.unsqueeze(2).broadcast_to([128, 8, 64]), ALU.mult), ki, te, KE.after)
                    kw = dve.do(lambda e, lac=lac: e.tensor_tensor(lac.f[:, 0:256], kc.f[:, 0:256],
                                                                   lac.f[:, 0:256], ALU.mult), aw, tkc)
                    pages.give(PC, aw, x2 if dr else aw)
                    work.append((E1, qd, B, ki, KE, ke, lac, kw, dec, te))
                    yield
                pages.give(k, dve.now())
                pages.give(q, dve.now())
                pages.give(kc, dve.now())
                while ("vg", 2 * m + 1) not in R:
                    yield
                states = []
                for dr in range(2):
                    E1, qd, B, ki, KE, ke, lac, kw, dec, te = work[dr]
                    KT, tkt, r1 = to_tokens(KE.f, [0, 128, 256, 384], 512, sbk, ke)
                    pages.give(KE, r1)
                    WT, twt, r2 = to_tokens(lac.f, [0, 128], 256, sbk, kw)
                    pages.give(lac, r2)
                    yield
                    S = [pages.take(), pages.take()]

                    def sview(c, S=S):
                        return S[c // 4].f[:, 128 * (c % 4):128 * (c % 4) + 128]

                    b0 = sbk.take()
                    for hp in range(2):
                        V, VC, tv = R["vg", 2 * m + hp]
                        for j in range(2):
                            t = mm(b0.f[64 * hp:64 * hp + 64, 0:128], WT.f[:, 128 * j + 64 * hp:128 * j + 64 * hp + 64],
                                   VC.f[:, 128 * j:128 * j + 128], j == 0, j == 1, twt, tv, b0.after)
                    pages.give(WT, t)
                    c0 = 7 if dr else 0
                    s_t = dve.do(lambda e, c0=c0, sview=sview, b0=b0: e.tensor_copy(sview(c0), b0.f[:, 0:128]), t,
                                 S[0].after, S[1].after)
                    sbk.give(b0, s_t)
                    yield
                    ub = [sbk.take(), sbk.take()]
                    for par in range(2):
                        pe.wait(ub[par].after)
                        for i in range(4):
                            for hp in range(2):
                                V, _, tv = R["vg", 2 * m + hp]
                                l = KT.f[64 * par:64 * par + 64, 128 * i + 64 * hp:128 * i + 64 * hp + 64]
                                r = V.f[64 * par:64 * par + 64, 128 * i:128 * i + 128]
                                t = mm(ub[par].f[64 * hp:64 * hp + 64, 128 * i:128 * i + 128], l, r, True, True,
                                       tkt, tv)
                    pages.give(KT, t)
                    dve.wait(t)
                    for i in range(7):
                        c = 7 - i if dr else i
                        n = c - 1 if dr else c + 1
                        u = ub[c % 2].f[:, 128 * (c // 2):128 * (c // 2) + 128]
                        s_t = dve.do(lambda e, c=c, n=n, u=u, dec=dec, sview=sview: e.scalar_tensor_tensor(
                            sview(n), sview(c), dec[:, c:c + 1], u, ALU.mult, ALU.add), s_t)
                    sbk.give(ub[0], s_t)
                    sbk.give(ub[1], s_t)
                    states.append((S, sview, s_t))
                    yield
                for hp in range(2):
                    rows = slice(64 * hp, 64 * hp + 64)
                    V, VC, tv = R["vg", 2 * m + hp]
                    atts = []
                    for dr in range(2):
                        E1, qd, B, ki, *_ = work[dr]
                        ab = sbk.take()
                        pe.wait(ab.after, qd, ki)
                        for j in range(4):
                            sl = slice(128 * j, 128 * j + 128)
                            t = mm(ab.f[:, sl], B.f[rows, sl], E1.f[rows, sl], True, True)
                        am = pages.take()
                        msk = (maskF, maskB)[dr].unsqueeze(1).broadcast_to([128, 4, 128])
                        d = dve.do(lambda e, am=am, ab=ab, msk=msk: e.tensor_tensor(
                            am.f.rearrange("p (j n) -> p j n", j=4), ab.f.rearrange("p (j n) -> p j n", j=4), msk,
                            ALU.mult), t, am.after)
                        sbk.give(ab, d)
                        atts.append((am, d))
                    yield
                    ob = sbk.take()
                    pe.wait(ob.after, tv)
                    for dr in range(2):
                        am, d = atts[dr]
                        for j in range(4):
                            sl = slice(128 * j, 128 * j + 128)
                            t = mm(ob.f[:, sl], V.f[:, sl], am.f[:, sl], dr == 0 and j == 0, False, d, skip=True)
                        pages.give(am, t)
                    for dr in range(2):
                        E1 = work[dr][0]
                        S, sview, s_t = states[dr]
                        for c in range(8):
                            t = mm(ob.f[:, 64 * c:64 * c + 64], sview(c)[rows, :], E1.f[rows, 64 * c:64 * c + 64],
                                   False, dr == 1 and c == 7, s_t, skip=True)
                    og = pages.take()
                    c = copy_act(og.f, ob.f, t, og.after)
                    sbk.give(ob, c)
                    pages.give(V, t)
                    pages.give(VC, t)
                    R["og_raw", 2 * m + hp] = (og, c)
                    yield
                for dr in range(2):
                    pages.give(work[dr][0], t)
                    pages.give(work[dr][2], t)
                    pages.give(states[dr][0][0], t)
                    pages.give(states[dr][0][1], t)
            pages.give(z, pe.now())
            pages.give(zc, pe.now())
            for h in range(4):
                while ("og", h) not in R:
                    yield
                o, to = R["og_raw", h]
                r, rt = rstd_of([(o.f, to)], T, 128, ones, sbk)
                yield
                d = dve.do(lambda e, o=o, r=r: e.scalar_tensor_tensor(o.f, o.f, col("gla_norm_g"), r.f, ALU.mult,
                                                                     ALU.mult), rt, to, act.now())
                g, tg = R["og", h]
                d2 = dve.do(lambda e, o=o, g=g: e.scalar_tensor_tensor(o.f, o.f, 0.5, g.f, ALU.mult, ALU.mult),
                            d, tg)
                pages.give(r, d)
                pages.give(g, d2)
                R["o_gla", h] = split_pages(o, d2)
                yield

        def perm(ap):
            return ap.rearrange("p (r c) -> p c r", c=64)

        def inperm(ap):
            return ap.rearrange("p (c r) -> p c r", r=8)

        def na_norm(o, t, g, width, tag, natural):
            raw = pages.take()
            c = copy_act(raw.f[:, 0:width], o.f[:, 0:width], t, raw.after)
            mb.give(o, c)
            r, rt = rstd_of([(raw.f[:, 0:width], c)], width, 64, bones, mb)
            q = pages.take()
            if natural:
                d = dve.do(lambda e: e.scalar_tensor_tensor(q.f[:, 0:width], raw.f[:, 0:width], g,
                                                            r.f[:, 0:width], ALU.mult, ALU.mult), rt, q.after)
            else:
                d = dve.do(lambda e: e.scalar_tensor_tensor(perm2(q.f), rc3(raw.f), g, rc3(r.f), ALU.mult,
                                                            ALU.mult), rt, q.after)
            pages.give(raw, d)
            pages.give(r, d)
            R[tag] = (q, d)

        def rc3(ap):
            return ap.rearrange("p (r c) -> p r c", c=64)

        def perm2(ap):
            return ap.rearrange("p (c r) -> p r c", r=8)

        gq = smal[:, 64:65]
        t_gq = dve.do(lambda e: e.tensor_scalar(gq, col("na_q_g"), 0.125, None, ALU.mult), t_prm)

        def main_na():
            dve.wait(t_gq)
            for m in range(4):
                o, oc, t = yield from proj("wk_na", m, hx, hcx)
                na_norm(o, t, col("na_k_g"), 512, ("kn", m), False)
                na_norm(oc, t, col("na_k_g"), 256, ("knc", m), True)
                o, oc, t = yield from proj("wv_na", m, hx, hcx)
                v, vc = pages.take(), pages.take()
                c1 = copy_act(perm2(v.f), rc3(o.f), t, v.after)
                c2 = copy_act(vc.f[:, 0:256], oc.f[:, 0:256], t, vc.after)
                mb.give(o, c1)
                mb.give(oc, c2)
                V, tv, r0 = to_tokens(v.f, [0, 128, 256, 384], 512, mb, c1)
                VS, ts, r1 = to_tokens(v.f, [64, 192, 320], 384, mb, c1)
                VC, tc, r2 = to_tokens(vc.f, [0, 128], 256, mb, c2)
                pages.give(v, r1)
                pages.give(vc, r2)
                R["vn", m] = (V, VS, VC, [tv, ts, tc])
                o, oc, t = yield from proj("wq_na", m, hx)
                na_norm(o, t, gq, 512, ("qn", m), False)

        def softmax(b, t, col0):
            nm, sm, rc_ = smal[:, col0:col0 + 1], smal[:, col0 + 1:col0 + 2], smal[:, col0 + 2:col0 + 3]
            d = dve.do(lambda e: e.tensor_reduce(nm, b.f, AX, ALU.max, negate=True), t)
            P = pages.take()
            x = act.do(lambda e: e.activation(P.f, b.f, ACT.Exp, bias=nm, accum_out=sm), d, P.after)
            sbk.give(b, x)
            d2 = dve.do(lambda e: e.reciprocal(rc_, sm), x)
            d3 = dve.do(lambda e: e.tensor_scalar(P.f, P.f, rc_, None, ALU.mult), d2)
            return P, d3

        def attention(jobs, scores, values, finish, ready):
            a_, b_ = {}, {}
            n = len(jobs)
            for i in range(n + 2):
                if i < n:
                    while not ready(jobs[i]):
                        yield
                    b = sbk.take()
                    t = scores(jobs[i], b)
                    a_[i] = softmax(b, t, 80 + 4 * (i % 8))
                    yield
                if 1 <= i <= n:
                    P, d = a_.pop(i - 1)
                    PT, tp, r = to_tokens(P.f, [0, 128, 256, 384], 512, sbk, d)
                    pages.give(P, r)
                    b_[i - 1] = (PT, tp)
                    yield
                if i >= 2:
                    PT, tp = b_.pop(i - 2)
                    t = values(jobs[i - 2], PT, tp)
                    pages.give(PT, t)
                    finish(jobs[i - 2], t)
                    yield

        def side_na():
            cur = {}
            bias = {}

            def bias_load(h, hf):
                if h < 8 and (h, hf) not in bias:
                    p = pages.take()
                    bias[h, hf] = (p, load(p.f.rearrange("p (q k) -> p q k", q=2), a["bias"][2 * h + hf], p.after))

            bias_load(0, 0)
            bias_load(0, 1)

            def scores(job, b):
                h, qt = job
                m, hp = h // 2, h % 2
                if qt % 2 == 0:
                    nh, nf = (h, 1) if qt == 0 else (h + 1, 0)
                    bias_load(nh, nf)
                q, tq = R["qn", m]
                k, tk = R["kn", m]
                kc, tkc = R["knc", m]
                rows = slice(64 * hp, 64 * hp + 64)
                k0 = NA_K0[qt]
                ql = q.f[rows, 128 * qt:128 * qt + 128]
                pe.wait(b.after, tq, tk, tkc)
                mmq(b.f[:, 0:256], ql, k.f[rows, k0:k0 + 256], True, False, skip=True)
                mmq(b.f[:, 256:512], ql, kc.f[rows, 0:256], False, False, skip=True)
                p, tb = bias[h, qt // 2]
                t = mm(b.f[:, 0:256], ident, p.f[:, 256 * (qt % 2):256 * (qt % 2) + 256], False, True, tb, skip=True)
                if qt % 2 == 1:
                    pages.give(p, t)
                return t

            def values(job, PT, tp):
                h, qt = job
                m, hp = h // 2, h % 2
                if m not in cur:
                    cur[m] = sbk.take()
                    pe.wait(cur[m].after)
                V, VS, VC, tv = R["vn", m]
                f = slice(64 * hp, 64 * hp + 64)

                def vt(page, j):
                    return page.f[:, 128 * j + 64 * hp:128 * j + 64 * hp + 64]

                loc = {0: (V, 0), 1: (VS, 0), 2: (VS, 1), 3: (V, 2)}[qt]
                ls = [vt(loc[0], loc[1]), vt(loc[0], loc[1] + 1), vt(VC, 0), vt(VC, 1)]
                for j in range(4):
                    t = mm(cur[m].f[f, 128 * qt:128 * qt + 128], ls[j], PT.f[:, 128 * j:128 * j + 128], j == 0,
                           j == 3, tp, tv)
                return t

            def finish(job, t):
                h, qt = job
                m = h // 2
                if h % 2 == 1 and qt == 3:
                    o = pages.take()
                    b = cur.pop(m)
                    c = act.do(lambda e: e.activation(rc3(o.f), perm2(b.f), ACT.Copy), t, o.after)
                    sbk.give(b, c)
                    R["o_na", m] = split_pages(o, c)
                    for key in (("qn", m), ("kn", m), ("knc", m)):
                        pages.give(R[key][0], pe.now())
                    for p in R["vn", m][0:3]:
                        pages.give(p, pe.now())

            jobs = [(h, qt) for h in range(8) for qt in range(4)]
            yield from attention(jobs, scores, values, finish, lambda job: ("qn", job[0] // 2) in R)

        def tanh_gate(o, t, bks):
            g = pages.take()
            c = act.do(lambda e: e.activation(g.f, o.f, ACT.Tanh, scale=0.5), t, g.after)
            bks.give(o, c)
            return g, c

        def main_og():
            for h in range(4):
                o, _, t = yield from proj("w_og", h, hx)
                g = pages.take()
                c = act.do(lambda e, g=g, o=o: e.activation(g.f, o.f, ACT.Tanh, scale=0.5), t, g.after)
                d = dve.do(lambda e, g=g, o=o: e.scalar_tensor_tensor(g.f, g.f, 1.0, o.f, ALU.add, ALU.mult), c)
                mb.give(o, d)
                R["og", h] = (g, d)

        def main_mod():
            b = mb.take()
            for m in range(16, 19):
                mod_load(m)
            for m in range(16, 48):
                if m + 3 < 48:
                    mod_load(m + 3)
                t = mod_mm(m, b.f[:, m - 16:m - 15], 1, b.after)
                yield
            d = dve.do(lambda e: e.tensor_tensor(modr[:, :], b.f[:, 0:32], col("b_mod", 16, 32), ALU.add), t)
            mb.give(b, d)
            d = dve.do(lambda e: e.scalar_tensor_tensor(A2[:, :], modr[:, 16:24], 1.0, col("norm2_g", 0, 8),
                                                        ALU.add, ALU.mult), d)
            d = dve.do(lambda e: e.tensor_scalar(modr[:, 0:8], modr[:, 0:8], 0.5, None, ALU.mult), d)
            R["mod"] = d

        def main_gates1():
            for m in range(8):
                for nm in ("w_ma", "w_mb"):
                    o, _, t = yield from proj(nm, m, hx)
                    R[nm, m] = tanh_gate(o, t, mb)

        def chain(*gens):
            for g in gens:
                yield from g

        def room(n):
            for _ in range(1000):
                if len(pages.free) >= n:
                    return
                yield
            raise ValueError("no room")

        def ready(*keys):
            for _ in range(1000):
                if all(k in R for k in keys):
                    return
                yield
            raise ValueError(f"never ready: {keys}")

        def branch(merged, gate, gm, w, xs, gates=None):
            for m in range(8):
                if gates is None:
                    yield from room(3)
                    o, _, t = yield from proj(gate, gm + m, hcur[0])
                    g, tg = tanh_gate(o, t, mb)
                else:
                    g, tg = gates[m]
                o, _, t = yield from proj(w, m, xs)
                d = dve.do(lambda e, g=g, o=o: e.scalar_tensor_tensor(g.f, g.f, 1.0, o.f, ALU.add, ALU.mult), tg, t)
                mb.give(o, d)
                if m not in merged:
                    merged[m] = (g, d)
                else:
                    acc, tok = merged[m]
                    tok = pool.do(lambda e, g=g, acc=acc: e.tensor_tensor(acc.f, acc.f, g.f, ALU.add), d, tok)
                    pages.give(g, tok)
                    merged[m] = (acc, tok)

        def free_context():
            for h, _ in HC:
                pages.give(h, pe.now())
            yield

        mains1 = chain(main_gla(), main_og(), main_na(), free_context(), main_mod(), main_gates1())
        weave(mains1, [chain(side_gla(), side_na())], 1)
        give_pairs(H, pe.now())

        def run(gen):
            for _ in gen:
                pass

        def split_all(ps):
            return [split_pages(p, t) for p, t in ps]

        def main_merge1():
            merged = {}
            for key, w in (("o_gla", "w_branch_gla"), ("o_na", "w_branch_na")):
                pairs = [R.pop((key, m)) for m in range(4)]
                gates = [R.pop(({"o_na": "w_ma", "o_gla": "w_mb"}[key], m)) for m in range(8)]
                yield from branch(merged, None, 0, w, xk(pairs), gates)
                give_pairs(pairs, pe.now())
            R["merged"] = [merged[m] for m in range(8)]

        run(main_merge1())
        M = split_all(R["merged"])

        def main_out1():
            xm = xk(M)
            for m in range(8):
                o, _, t = yield from proj("w_out", m, xm)
                d = dve.do(lambda e, m=m, o=o: e.scalar_tensor_tensor(X[m].f, o.f, modr[:, m:m + 1], X[m].f, ALU.mult,
                                                                      ALU.add), t, X[m].rd, R["mod"])
                mb.give(o, d)
                X[m].w, X[m].rd = [d], []

        run(main_out1())
        give_pairs(M, pe.now())

        def norm_x(gain, shift):
            r, rt = rstd_of([(X[k].f, X[k].w) for k in range(8)], T, 1024, ones, mb)
            res = []
            for k in range(8):
                t = pages.take()
                d = dve.do(lambda e, k=k, t=t: e.scalar_tensor_tensor(t.f, X[k].f, gain(k), r.f, ALU.mult, ALU.mult),
                           t.after, rt)
                X[k].rd = [d]
                if shift is not None:
                    d = dve.do(lambda e, k=k, t=t: e.tensor_scalar(t.f, t.f, shift(k), None, ALU.add), d)
                res.append(split_pages(t, d))
            pages.give(r, d)
            return res

        def main_ffn(sfx, Hf, on_out):
            xh = xk(Hf)
            for hf in range(2):
                pairs = []
                for j in range(FH * hf, FH * hf + FH):
                    og, _, tg = yield from proj("ffn_gate" + sfx, j, xh)
                    ou, _, tu = yield from proj("ffn_up" + sfx, j, xh)
                    s = pages.take()
                    c = act.do(lambda e, s=s, og=og: e.activation(s.f, og.f, ACT.Silu), tg, s.after)
                    mb.give(og, c)
                    d = dve.do(lambda e, s=s, ou=ou: e.tensor_tensor(s.f, s.f, ou.f, ALU.mult), c, tu)
                    mb.give(ou, d)
                    pairs.append(split_pages(s, d))
                if hf == 1:
                    give_pairs(Hf, pe.now())
                for m in range(8):
                    o, _, t = yield from proj("ffn_down" + sfx, m, xk(pairs), None, 2, FH * hf)
                    on_out(hf, m, o, t)
                give_pairs(pairs, pe.now())

        H2 = norm_x(lambda k: A2[:, k:k + 1], lambda k: modr[:, 8 + k:9 + k])

        def out_x(hf, m, o, t):
            d = dve.do(lambda e: e.scalar_tensor_tensor(X[m].f, o.f, modr[:, 24 + m:25 + m], X[m].f, ALU.mult,
                                                        ALU.add), t, X[m].rd, X[m].w)
            mb.give(o, d)
            X[m].w, X[m].rd = [d], []

        lg = smal[:, 128:144]

        def side_tables():
            R["tabA"] = load(tabA[:, :], a["tabA"], dve.now())
            pi = pages.take()
            tp = load(pi.f.bitcast(I32), a["pos"], pi.after)
            pf = pages.take()
            d0 = dve.do(lambda e: e.tensor_copy(pf.f, pi.f.bitcast(I32)), tp, pf.after)
            pages.give(pi, d0)
            yield
            for key, inv, sgn in (("m", "inv_m", "sgn_m"), ("r", "inv_r", "sgn_r")):
                an, kk = pages.take(), pages.take()
                d = dve.do(lambda e, an=an, inv=inv: e.tensor_scalar(an.f, pf.f, col(inv), None, ALU.mult), d0,
                           an.after)
                d = dve.do(lambda e, an=an, kk=kk: e.tensor_scalar(kk.f, an.f, 1 / (2 * np.pi), ROUND, ALU.mult,
                                                                   ALU.add), d, kk.after)
                d = dve.do(lambda e, kk=kk: e.tensor_scalar(kk.f, kk.f, -ROUND, None, ALU.add), d)
                for cc in (C1, C2, C3):
                    d = dve.do(lambda e, an=an, kk=kk, cc=cc: e.scalar_tensor_tensor(an.f, kk.f, -cc, an.f, ALU.mult,
                                                                                    ALU.add), d)
                d = dve.do(lambda e, an=an: e.tensor_scalar(an.f, an.f, -PI_IN, PI_IN, ALU.max, ALU.min), d)
                s1 = act.do(lambda e, an=an, kk=kk: e.activation(kk.f, an.f, ACT.Sin), d)
                d = act.do(lambda e, an=an: e.activation(an.f, an.f, ACT.Abs), s1)
                s2 = act.do(lambda e, an=an: e.activation(an.f, an.f, ACT.Sin, scale=-1.0, bias=col("halfpi")), d)
                d = dve.do(lambda e, kk=kk, sgn=sgn: e.tensor_scalar(kk.f, kk.f, col(sgn), None, ALU.mult), s1)
                R["cos", key], R["sin", key] = an, kk
                R["trig", key] = [s2, d]
                yield
            pages.give(pf, d)
            x = col("decay", 0, 16)
            s = [smal[:, 144 + 16 * i:160 + 16 * i] for i in range(2)]
            d = act.do(lambda e: e.activation(s[0], x, ACT.Abs))
            t = act.do(lambda e: e.activation(s[0], s[0], ACT.Exp, scale=-1.0), d)
            t = act.do(lambda e: e.activation(s[0], s[0], ACT.Ln, bias=col("one")), t)
            d = dve.do(lambda e: e.tensor_scalar(s[1], x, 0.0, None, ALU.min))
            R["lg"] = dve.do(lambda e: e.tensor_tensor(lg, s[1], s[0], ALU.subtract), t, d)
            yield

        weave(main_ffn("", H2, out_x), [side_tables()], 4)

        MSC = float(96 ** -0.5)
        RSC = float(128 ** -0.5)

        def layer(l):
            L = str(l)
            Hl = norm_x(lambda k: col("mix_pre" + L, k), None)
            xh = xk(Hl)
            qns = smal[:, 176 + 2 * l:178 + 2 * l]
            t_qn = dve.do(lambda e: e.tensor_scalar(qns, col("q_norm" + L, 0, 2), MSC, None, ALU.mult))
            cosM, sinM, trM = R["cos", "m"], R["sin", "m"], R["trig", "m"]
            cosR, sinR, trR = R["cos", "r"], R["sin", "r"], R["trig", "r"]

            def rope96(o, dst, t, *need):
                q = pages.take()
                d1 = dve.do(lambda e: e.tensor_tensor(dst.f[64:96, :], o.f[64:96, :], cosM.f[64:96, :], ALU.mult),
                            t, trM, dst.after, *need)
                d2 = dve.do(lambda e: e.tensor_tensor(q.f[64:96, :], o.f[96:128, :], sinM.f[96:128, :], ALU.mult),
                            q.after)
                d3 = dve.do(lambda e: e.tensor_tensor(dst.f[64:96, :], dst.f[64:96, :], q.f[64:96, :], ALU.add),
                            d1, d2)
                pages.give(q, d3)
                return d3

            def rope128(o, t):
                p, q = pages.take(), pages.take()
                d1 = dve.do(lambda e: e.tensor_tensor(p.f, o.f, cosR.f, ALU.mult), t, trR, p.after)
                dve.wait(q.after)
                for s, d in ((0, 64), (64, 0)):
                    d2 = dve.do(lambda e, s=s, d=d: e.tensor_tensor(q.f[d:d + 64, :], o.f[s:s + 64, :],
                                                                    sinR.f[s:s + 64, :], ALU.mult))
                d3 = dve.do(lambda e: e.tensor_tensor(p.f, p.f, q.f, ALU.add), d1, d2)
                mb.give(o, d2)
                pages.give(q, d3)
                return p, d3

            def main_mla():
                o, _, t = yield from proj("w_kv" + L, 0, xh)
                kv = pages.take()
                c = copy_act(kv.f, o.f, t, kv.after)
                mb.give(o, c)
                r, rt = rstd_of([(kv.f, c)], T, 128, ones, mb)
                d = dve.do(lambda e: e.scalar_tensor_tensor(kv.f, kv.f, col("kv_norm" + L), r.f, ALU.mult, ALU.mult),
                           rt)
                pages.give(r, d)
                R["xkv"] = [split_pages(kv, d)]
                o, _, t = yield from proj("w_kpe" + L, 0, xh)
                kp = pages.take()
                d = rope96(o, kp, t)
                mb.give(o, d)
                R["kpe"] = (kp, d)
                cq = []
                for m in range(2):
                    o, _, t = yield from proj("w_cq" + L, m, xh)
                    p = pages.take()
                    c = copy_act(p.f, o.f, t, p.after)
                    mb.give(o, c)
                    cq.append((p, c))
                r, rt = rstd_of([(p.f, c) for p, c in cq], T, 256, ones, mb)
                res = []
                for m, (p, c) in enumerate(cq):
                    d = dve.do(lambda e, p=p, m=m: e.scalar_tensor_tensor(p.f, p.f, qns[:, m:m + 1], r.f, ALU.mult,
                                                                         ALU.mult), rt, t_qn)
                    res.append(split_pages(p, d))
                pages.give(r, d)
                R["xq"] = res

            def side_mla():
                while "xq" not in R:
                    yield
                xq, xkv, (kp, tkp) = R.pop("xq"), R.pop("xkv"), R.pop("kpe")
                made = {}

                def make(j):
                    o, _, t = yield from proj("w_kn" + L, j, xk(xkv))
                    ks = []
                    for hp in range(2):
                        p = pages.take()
                        c1 = copy_act(p.f[0:64, :], o.f[64 * hp:64 * hp + 64, :], t, p.after)
                        c2 = dve.do(lambda e, p=p: e.tensor_copy(p.f[64:96, :], kp.f[64:96, :]), tkp, p.after)
                        ks.append((p, [c1, c2]))
                    mb.give(o, c1)
                    yield
                    o, _, t = yield from proj("w_v" + L, j, xk(xkv))
                    v = pages.take()
                    c = copy_act(v.f, o.f, t, v.after)
                    mb.give(o, c)
                    yield
                    qs = []
                    for hp in range(2):
                        o, _, t = yield from proj("w_uq" + L, 2 * j + hp, xk(xq))
                        p = pages.take()
                        d = rope96(o, p, t)
                        c1 = copy_act(p.f[0:64, :], o.f[0:64, :], t, p.after, d)
                        mb.give(o, c1)
                        qs.append((p, [c1, d]))
                        yield
                    V, tv, r = to_tokens(v.f, [0, 128, 256, 384], 512, mb, c)
                    pages.give(v, r)
                    made[j] = (ks, qs, V, tv)

                yield from make(0)
                cur = {}

                def scores(job, b):
                    h, qt = job
                    ks, qs, V, tv = made[h // 2]
                    (q, tq), (k, tk) = qs[h % 2], ks[h % 2]
                    return mm(b.f, q.f[0:96, 128 * qt:128 * qt + 128], k.f[0:96, :], True, True, b.after, tq, tk)

                def values(job, PT, tp):
                    h, qt = job
                    j, hp = h // 2, h % 2
                    if j not in cur:
                        cur[j] = sbk.take()
                        pe.wait(cur[j].after)
                    V, tv = made[j][2:4]
                    for i in range(4):
                        t = mm(cur[j].f[64 * hp:64 * hp + 64, 128 * qt:128 * qt + 128],
                               V.f[:, 128 * i + 64 * hp:128 * i + 64 * hp + 64], PT.f[:, 128 * i:128 * i + 128],
                               i == 0, i == 3, tp, tv)
                    return t

                def finish(job, t):
                    h, qt = job
                    j = h // 2
                    if h % 2 == 1 and qt == 3:
                        o, b = pages.take(), cur.pop(j)
                        c = copy_act(o.f, b.f, t, o.after)
                        sbk.give(b, c)
                        R["o_mla", j] = split_pages(o, c)
                        ks, qs, V, tv = made.pop(j)
                        for p, _ in ks + qs:
                            pages.give(p, pe.now())
                        pages.give(V, pe.now())

                def maker():
                    for j in range(1, 4):
                        yield from make(j)
                        while j in made and len(made) > 1:
                            yield
                    give_pairs(xq, pe.now())
                    give_pairs(xkv, pe.now())
                    pages.give(kp, dve.now())

                mk = maker()
                jobs = [(h, qt) for h in range(8) for qt in range(4)]
                n = 0
                att = attention(jobs, scores, values, finish, lambda job: job[0] // 2 in made)
                started = {0}
                for _ in att:
                    n += 1
                    next(mk, None)
                    yield
                for _ in mk:
                    yield

            def main_conv():
                for m in range(4):
                    o1, _, t1 = yield from proj("w_cg" + L, m, xh)
                    g, tg = tanh_gate(o1, t1, mb)
                    o2, _, t2 = yield from proj("w_ca" + L, m, xh)
                    d = dve.do(lambda e, g=g, o2=o2: e.scalar_tensor_tensor(g.f, g.f, 1.0, o2.f, ALU.add, ALU.mult),
                               tg, t2)
                    mb.give(o2, d)
                    R["ca", m] = (g, d)

            def side_conv():
                while ("ca", 3) not in R:
                    yield
                ca = [R.pop(("ca", m)) for m in range(4)]
                acc = [pages.take() for _ in range(4)]
                tok = [None] * 4
                for j in [15] + [i for i in range(31) if i != 15]:
                    s = j - 15
                    lo, hi = max(0, -s), min(T, T - s)
                    for m in range(4):
                        w = col("w_dw" + L, 31 * m + j)
                        src, A = ca[m][0].f[:, lo + s:hi + s], acc[m].f[:, lo:hi]
                        if j == 15:
                            tok[m] = dve.do(lambda e, A=A, src=src, w=w: e.tensor_scalar(A, src, w, None, ALU.mult),
                                            ca[m][1], acc[m].after)
                        else:
                            tok[m] = dve.do(lambda e, A=A, src=src, w=w: e.scalar_tensor_tensor(
                                A, src, w, A, ALU.mult, ALU.add), tok[m])
                    yield
                for m in range(4):
                    pages.give(ca[m][0], tok[m])
                    tok[m] = dve.do(lambda e, m=m: e.tensor_scalar(acc[m].f, acc[m].f, 0.5, col("b_dw" + L, m),
                                                                   ALU.mult, ALU.add), tok[m])
                R["conv"] = (acc, tok)
                yield

            def centred(ps, toks, n):
                b = sbk.take()
                pe.wait(b.after)
                for i, (p, t) in enumerate(zip(ps, toks)):
                    mt = mm(b.f, ones, p.f, i == 0, i == len(ps) - 1, t)
                ds = []
                for p in ps:
                    ds.append(dve.do(lambda e, p=p: e.scalar_tensor_tensor(p.f, b.f, -1.0 / n, p.f, ALU.mult,
                                                                           ALU.add), mt))
                sbk.give(b, ds[-1])
                return ds

            def side_conv_norm():
                while "conv" not in R:
                    yield
                acc, tok = R.pop("conv")
                ds = centred(acc, tok, 512)
                yield
                r, rt = rstd_of([(p.f, d) for p, d in zip(acc, ds)], T, 512, ones, sbk)
                yield
                for m in range(4):
                    d = dve.do(lambda e, m=m: e.scalar_tensor_tensor(acc[m].f, acc[m].f, col("cln_g" + L, m), r.f,
                                                                     ALU.mult, ALU.mult), rt)
                    c = act.do(lambda e, m=m: e.activation(acc[m].f, acc[m].f, ACT.Silu, bias=col("cln_b" + L, m)),
                               d)
                    R["o_conv", m] = split_pages(acc[m], c)
                    yield
                pages.give(r, d)

            def main_ret(h):
                for _ in range(1):
                    yield from room(12)
                    for e_ in range(2):
                        o, _, t = yield from proj("w_rv" + L, 2 * h + e_, xh)
                        v = pages.take()
                        c = copy_act(v.f, o.f, t, v.after)
                        mb.give(o, c)
                        V, tv, r = to_tokens(v.f, [0, 128, 256, 384], 512, mb, c)
                        pages.give(v, r)
                        R["rv", h, e_] = (V, tv)
                    for nm in ("rk", "rq"):
                        o, _, t = yield from proj("w_" + nm + L, h, xh)
                        R[nm, h] = rope128(o, t)
                    for e_ in range(2):
                        o, _, t = yield from proj("w_rg" + L, 2 * h + e_, xh)
                        g = pages.take()
                        c = act.do(lambda e, g=g, o=o: e.activation(g.f, o.f, ACT.Tanh, scale=0.5), t, g.after)
                        d = dve.do(lambda e, g=g, o=o: e.scalar_tensor_tensor(g.f, g.f, 1.0, o.f, ALU.add, ALU.mult),
                                   c)
                        mb.give(o, d)
                        R["rg", h, e_] = (g, d)

            def side_ret():
                for h in range(4):
                    while ("rg", h, 1) not in R:
                        yield
                    lf, lb = (lg[:, 8 * l + 4 * x + h:8 * l + 4 * x + h + 1] for x in range(2))
                    d = dve.do(lambda e, lf=lf: e.tensor_scalar(tabD, rA1, lf, None, ALU.mult), R["tabA"], R["lg"],
                               R["Dfree"])
                    d = dve.do(lambda e, lb=lb: e.scalar_tensor_tensor(tabD, rA2, lb, tabD, ALU.mult, ALU.add), d)
                    tD = act.do(lambda e: e.activation(tabD, tabD, ACT.Exp), d)
                    yield
                    (q, tq), (k, tk) = R.pop(("rq", h)), R.pop(("rk", h))
                    ats = []
                    for j in range(4):
                        b, at = sbk.take(), pages.take()
                        t = mm(b.f, k.f[:, 128 * j:128 * j + 128], q.f, True, True, b.after, tq, tk)
                        o0 = 384 - 128 * j
                        d = dve.do(lambda e, b=b, at=at, o0=o0: e.scalar_tensor_tensor(
                            at.f, b.f, RSC, tabD[:, o0:o0 + 512], ALU.mult, ALU.mult), t, tD, at.after)
                        sbk.give(b, d)
                        ats.append((at, d))
                        if j % 2:
                            yield
                    R["Dfree"] = [d]
                    pages.give(q, t)
                    pages.give(k, t)
                    os_, ots = [], []
                    for e_ in range(2):
                        V, tv = R.pop(("rv", h, e_))
                        b = sbk.take()
                        pe.wait(b.after, tv)
                        for j, (at, d) in enumerate(ats):
                            t = mm(b.f, V.f[:, 128 * j:128 * j + 128], at.f, j == 0, j == 3, d)
                        pages.give(V, t)
                        o = pages.take()
                        c = copy_act(o.f, b.f, t, o.after)
                        sbk.give(b, c)
                        os_.append(o)
                        ots.append(c)
                        yield
                    for at, _ in ats:
                        pages.give(at, t)
                    ds = centred(os_, ots, 256)
                    yield
                    r, rt = rstd_of([(p.f, d) for p, d in zip(os_, ds)], T, 256, ones, sbk)
                    yield
                    for e_ in range(2):
                        o, (g, tg) = os_[e_], R.pop(("rg", h, e_))
                        d = dve.do(lambda e, o=o, e_=e_, h=h: e.scalar_tensor_tensor(
                            o.f, o.f, col("gn_g" + L, 2 * h + e_), r.f, ALU.mult, ALU.mult), rt)
                        d2 = dve.do(lambda e, o=o, g=g: e.scalar_tensor_tensor(o.f, o.f, 0.5, g.f, ALU.mult,
                                                                               ALU.mult), d, tg)
                        pages.give(g, d2)
                        R["o_ret", 2 * h + e_] = split_pages(o, d2)
                    pages.give(r, d)
                    yield

            merged = {}
            hcur[0] = xh

            def main_branch(i, key, n, w):
                yield from ready(*[(key, m) for m in range(n)])
                pairs = [R.pop((key, m)) for m in range(n)]
                yield from branch(merged, "w_gate" + L, 8 * i, w + L, xk(pairs))
                give_pairs(pairs, pe.now())

            weave(chain(main_mla(), main_conv(), main_ret(0), main_ret(1), main_branch(1, "o_conv", 4, "w_pw"),
                        main_branch(0, "o_mla", 4, "w_mo"), main_ret(2), main_ret(3),
                        main_branch(2, "o_ret", 8, "w_ro")),
                  [chain(side_mla(), side_ret()), side_conv(), side_conv_norm()], 1)
            give_pairs(Hl, pe.now())
            R["merged"] = [merged[m] for m in range(8)]
            M = split_all(R["merged"])
            F = []

            def main_out():
                for m in range(8):
                    o, _, t = yield from proj("w_out" + L, m, xk(M))
                    f = pages.take()
                    c = copy_act(f.f, o.f, t, f.after, scale=0.5)
                    mb.give(o, c)
                    F.append((f, c))

            run(main_out())
            give_pairs(M, pe.now())

            def post_norm(F, g):
                r, rt = rstd_of([(f.f, c) for f, c in F], T, 1024, ones, mb)
                for m, (f, c) in enumerate(F):
                    d = dve.do(lambda e, f=f, m=m: e.scalar_tensor_tensor(f.f, f.f, col(g, m), r.f, ALU.mult,
                                                                         ALU.mult), rt)
                    d = dve.do(lambda e, f=f, m=m: e.tensor_tensor(X[m].f, X[m].f, f.f, ALU.add), d, X[m].rd)
                    X[m].w, X[m].rd = [d], []
                    pages.give(f, d)
                pages.give(r, d)

            post_norm(F, "mix_post" + L)
            Hf = norm_x(lambda k: col("ffn_pre" + L, k), None)
            F2 = []

            def out_f(hf, m, o, t):
                if hf == 0:
                    f = pages.take()
                    c = copy_act(f.f, o.f, t, f.after)
                    F2.append((f, c))
                else:
                    f, c0 = F2[m]
                    c = dve.do(lambda e: e.tensor_tensor(f.f, f.f, o.f, ALU.add), t, c0)
                    F2[m] = (f, c)
                mb.give(o, c)

            run(main_ffn(L, Hf, out_f))
            post_norm(F2, "ffn_post" + L)

        R["Dfree"] = []
        for l in range(2):
            layer(l)

        for k in range(8):
            sp.dma(s_out, out[:, k, :], X[k].f, X[k].w)
        sp.quiet(lambda e: e.wait_ge(s_out, 128))

        while len(order) % 8:
            order.append(None)
        if probe:
            return

        block = ctx.enter_context(nc.Block())

        @block.sync
        def _(e):
            sp.play(e)

        @block.tensor
        def _(e):
            pe.play(e)

        @block.scalar
        def _(e):
            act.play(e)

        @block.vector
        def _(e):
            dve.play(e)

        @block.gpsimd
        def _(e):
            pool.play(e)


def columns(v):
    return np.ascontiguousarray(v.reshape(-1, 128).T)


def tables():
    i = np.arange(128)
    same = (i[:, None] // 64) == (i[None, :] // 64)
    cst = np.zeros((128, 5, 128), np.float32)
    cst[:, 0] = np.eye(128)
    cst[:, 1] = 1.0
    cst[:, 2] = same
    cst[:, 3] = same & (i[:, None] <= i[None, :])
    cst[:, 4] = same & (i[:, None] >= i[None, :])
    freqs = (np.float32(10000.0) ** (-np.arange(16, dtype=np.float32) / np.float32(16))).astype(np.float32)
    t = np.arange(T)
    tabG = np.zeros((128, 1792), np.float32)
    for p in range(128):
        j, second = p % 32, (p % 64) >= 32
        pos = (t // 64 if j < 16 else t % 64).astype(np.float32)
        ang = (pos * freqs[j % 16]).astype(np.float32)
        tabG[p, 0:512] = np.cos(ang)
        tabG[p, 512:1024] = -np.sin(ang) if second else np.sin(ang)
    tabG[:, 1024:1536] = (t % 64 != 0)
    tabG[:, 1536:1792] = (np.arange(256) != 0)
    c = np.arange(896)
    diff = (c[None, :] - 384 - i[:, None]).astype(np.float32)
    tabA = np.concatenate([np.maximum(diff, 0), np.maximum(-diff, 0)], 1).astype(np.float32)
    return cst, tabG, tabA


def na_bias(rpb):
    out = np.full((8, 4, 128, 256), -1e30, np.float32)
    for qt in range(4):
        q = 128 * qt + np.arange(128)
        k = NA_K0[qt] + np.arange(256)
        qc, qr = (q // 8)[:, None], (q % 8)[:, None]
        kc, kr = (k // 8)[None, :], (k % 8)[None, :]
        st = np.clip(qc - 8, 0, 48)
        inside = (kc >= st) & (kc < st + 16)
        dc = np.clip(kc - qc, -15, 15) + 15
        got = rpb[:, kr - qr + 7, dc]
        out[:, qt] = np.where(inside[None], got, out[:, qt])
    return np.ascontiguousarray(out.reshape(16, 2, 128, 256).transpose(0, 2, 1, 3))


def weights(inp):
    w = inp["w_in"][0]
    o = np.cumsum([0, 512, 512, 512, 256, 256, 512, 512, 32, 1024, 1024])
    hp = np.concatenate([np.arange(0, 16), np.arange(32, 48), np.arange(16, 32), np.arange(48, 64)])
    gp = np.concatenate([64 * h + hp for h in range(4)])
    lr = np.zeros((1024, 128), np.float32)
    lr[:, 0:32] = w[:, o[7]:o[8]]
    m = {
        "wq_na": w[:, o[0]:o[1]], "wk_na": w[:, o[1]:o[2]], "wv_na": w[:, o[2]:o[3]],
        "wq_g": w[:, o[3]:o[4]][:, gp], "wk_g": w[:, o[4]:o[5]][:, gp], "wv_g": w[:, o[5]:o[6]],
        "w_og": w[:, o[6]:o[7]], "w_lr": lr, "w_ma": w[:, o[8]:o[9]], "w_mb": w[:, o[9]:o[10]],
        "w_branch_na": inp["w_branch_na"][0], "w_branch_gla": inp["w_branch_gla"][0], "w_out": inp["w_out"][0],
        "ffn_gate": inp["w_ffn_gate"][0], "ffn_up": inp["w_ffn_up"][0], "ffn_down": inp["w_ffn_down"][0],
    }
    o = np.cumsum([0, 256, 128, 32, 1024, 512, 512, 1024, 1024, 3072])
    swap = np.concatenate([np.arange(16, 32), np.arange(0, 16)])
    for l in range(2):
        L = str(l)
        w = inp["w_in_2"][l]
        pe_ = w[:, o[2]:o[3]]
        kpe = np.zeros((1024, 128), np.float32)
        kpe[:, 64:96], kpe[:, 96:128] = pe_, pe_[:, swap]
        uq = inp["mla_w_uq_2"][l].reshape(256, 8, 96)
        uq = np.concatenate([uq, uq[:, :, 64:][:, :, swap]], 2).reshape(256, 1024)
        ukv = inp["mla_w_ukv_2"][l].reshape(128, 8, 128)
        m.update({
            "w_cq" + L: w[:, o[0]:o[1]], "w_kv" + L: w[:, o[1]:o[2]], "w_kpe" + L: kpe,
            "w_ca" + L: w[:, o[3]:o[3] + 512], "w_cg" + L: w[:, o[3] + 512:o[4]],
            "w_rq" + L: w[:, o[4]:o[5]], "w_rk" + L: w[:, o[5]:o[6]], "w_rv" + L: w[:, o[6]:o[7]],
            "w_rg" + L: w[:, o[7]:o[8]], "w_gate" + L: w[:, o[8]:o[9]],
            "w_uq" + L: uq, "w_kn" + L: ukv[:, :, 0:64].reshape(128, 512), "w_v" + L: ukv[:, :, 64:].reshape(128, 512),
            "w_mo" + L: inp["mla_w_o_2"][l], "w_pw" + L: inp["conv_w_pw_2"][l], "w_ro" + L: inp["ret_w_o_2"][l],
            "w_out" + L: inp["w_out_2"][l], "ffn_gate" + L: inp["ffn_w_gate_2"][l],
            "ffn_up" + L: inp["ffn_w_up_2"][l], "ffn_down" + L: inp["ffn_w_down_2"][l],
        })
    return m


def stream(mats, order):
    out = np.zeros((NB, 128, 8, 128), np.float32)
    for s, key in enumerate(order):
        if key is not None:
            name, m, k = key
            out[s // 8, :, s % 8, :] = mats[name][128 * k:128 * k + 128, 128 * m:128 * m + 128]
    return out


def params(inp):
    hp = np.concatenate([np.arange(0, 16), np.arange(32, 48), np.arange(16, 32), np.arange(48, 64)])
    gp = np.concatenate([64 * h + hp for h in range(4)])
    prm = np.zeros((128, NPC), np.float32)

    def put(name, v):
        o, n = PCOL[name]
        prm[:, o:o + n] = v

    put("eps", EPS)
    put("one", 1.0)
    put("halfpi", np.pi / 2)
    put("b_mod", columns(inp["b_mod"][0]))
    put("norm1_g", columns(inp["norm1_g"][0]))
    put("norm2_g", columns(inp["norm2_g"][0]))
    put("na_q_g", columns(np.concatenate([inp["na_q_norm_g"][0]] * 2)))
    put("na_k_g", columns(np.concatenate([inp["na_k_norm_g"][0]] * 2)))
    put("b_alpha", columns(np.ascontiguousarray(inp["gla_b_alpha"][0][:, gp])))
    put("gla_norm_g", columns(inp["gla_norm_g"][0]))
    im = (np.float32(10000.0) ** (-np.arange(0, 32, 2, dtype=np.float32) / np.float32(32))).astype(np.float32)
    ir = (np.float32(10000.0) ** (-np.arange(0, 128, 2, dtype=np.float32) / np.float32(128))).astype(np.float32)
    put("inv_m", np.tile(im, 8)[:, None])
    put("sgn_m", np.tile(np.repeat(np.float32([-1, 1]), 16), 4)[:, None])
    put("inv_r", np.tile(ir, 2)[:, None])
    put("sgn_r", np.repeat(np.float32([1, -1]), 64)[:, None])
    put("decay", np.broadcast_to(inp["ret_decay_logits_2"].reshape(1, 16), (128, 16)))
    for l in range(2):
        L = str(l)
        for n, k in (("mix_pre", "ln_mix_pre_2"), ("mix_post", "ln_mix_post_2"), ("ffn_pre", "ln_ffn_pre_2"),
                     ("ffn_post", "ln_ffn_post_2"), ("q_norm", "mla_q_norm_2"), ("kv_norm", "mla_kv_norm_2"),
                     ("b_dw", "conv_b_dw_2"), ("cln_g", "conv_ln_g_2"), ("cln_b", "conv_ln_b_2"),
                     ("gn_g", "ret_gn_g_2")):
            put(n + L, columns(inp[k][l]))
        put("w_dw" + L, inp["conv_w_dw_2"][l].reshape(31, 4, 128).transpose(2, 1, 0).reshape(128, 124))
    return prm


SHAPES = {
    "wst": ((NB, 128, 8, 128), F32), "prm": ((128, NPC), F32), "ccol": ((128, 8, 2), F32),
    "wmod": ((96, 128, 4, 128), F32), "xT": ((128, 8, 512), F32), "cT": ((128, 4, 512), F32),
    "cst": ((128, 5, 128), F32), "tabG": ((128, 1792), F32), "tabA": ((128, 1792), F32), "wal": ((32, 2, 256), F32),
    "bias": ((16, 128, 2, 256), F32), "pos": ((128, 512), I32),
}


def arrays(inp, order):
    cst, tabG, tabA = tables()
    gp = np.concatenate([64 * h + np.concatenate([np.arange(0, 16), np.arange(32, 48), np.arange(16, 32),
                                                  np.arange(48, 64)]) for h in range(4)])
    wal = np.zeros((32, 2, 256), np.float32)
    wal[0:16, 0] = inp["gla_w_alpha"][0, 0][:, gp]
    wal[16:32, 1] = inp["gla_w_alpha"][0, 1][:, gp]
    wm = inp["w_mod"][0].reshape(2, 4, 128, 48, 128).transpose(3, 0, 2, 1, 4).reshape(96, 128, 4, 128)
    got = {
        "wst": stream(weights(inp), order), "prm": params(inp),
        "ccol": np.stack([columns(inp["c"][0]), columns(inp["c_ctx"])], 2),
        "wmod": wm, "xT": inp["x"][0].T.reshape(8, 128, 512).transpose(1, 0, 2),
        "cT": inp["ctx"][0].T.reshape(4, 2, 128, 256).transpose(2, 0, 1, 3).reshape(128, 4, 512),
        "cst": cst, "tabG": tabG, "tabA": tabA, "wal": wal, "bias": na_bias(inp["na_rpb"][0]),
        "pos": np.repeat(inp["positions_2"][0:1], 128, 0),
    }
    return {k: np.ascontiguousarray(v) for k, v in got.items()}


def kernel(**inputs):
    import concourse.bacc as _bacc
    from concourse.bass_utils import run_bass_kernel_spmd as _run

    inp = {k: np.asarray(v) for k, v in inputs.items()}
    nc = _bacc.Bacc("TRN2", target_bir_lowering=False, num_devices=1)
    aps = {k: nc.dram_tensor(f"in_{k}", s, dt, kind="ExternalInput").ap() for k, (s, dt) in SHAPES.items()}
    out = nc.dram_tensor("out_x", (128, 8, 512), F32, kind="ExternalOutput").ap()
    order = []
    program(nc, aps, out, order, False)
    assert len(order) == 8 * NB, len(order) / 8
    got = arrays(inp, order)
    r = _run(nc, [{f"in_{k}": v for k, v in got.items()}], core_ids=[0])
    y = r.results[0]["out_x"]
    return np.ascontiguousarray(y.transpose(1, 0, 2).reshape(1024, 512).T)[None]
```

```python
from contextlib import ExitStack

import numpy as np

import concourse.bass as bass
from concourse import mybir

F32 = mybir.dt.float32
F32R = mybir.dt.float32r
I32 = mybir.dt.int32
ACT = mybir.ActivationFunctionType
ALU = mybir.AluOpType
AX = mybir.AxisListType.X

T = 512
TC = 256
EPS = 1e-6
FT = 22
FH = 11
NB = 429
NPAGE = 72
ROUND = 12582912.0
C1 = 6.28125
C2 = float(np.floor((2 * np.pi - C1) * 2.0**20) / 2.0**20)
C3 = float(2 * np.pi - C1 - C2)
PI_IN = 3.1415925
NA_K0 = [0, 64, 192, 256]

PARAMS = [
    ("eps", 1), ("one", 1), ("halfpi", 1), ("neg20", 1),
    ("b_mod", 48), ("norm1_g", 8), ("norm2_g", 8), ("na_q_g", 1), ("na_k_g", 1), ("b_alpha", 4),
    ("gla_norm_g", 1), ("inv_m", 1), ("sgn_m", 1), ("inv_r", 1), ("sgn_r", 1), ("decay", 16),
]
for _l in range(2):
    PARAMS += [(f"{n}{_l}", c) for n, c in (
        ("mix_pre", 8), ("mix_post", 8), ("ffn_pre", 8), ("ffn_post", 8), ("q_norm", 2), ("kv_norm", 1),
        ("w_dw", 124), ("b_dw", 4), ("cln_g", 4), ("cln_b", 4), ("gn_g", 8))]
PCOL = {}
NPC = 0
for _n, _c in PARAMS:
    PCOL[_n] = (NPC, _c)
    NPC += _c


class Note:

    def activation(self, *a, **k):
        return lambda e: e.activation(*a, **k)

    def tensor_tensor(self, *a, **k):
        return lambda e: e.tensor_tensor(*a, **k)

    def tensor_scalar(self, *a, **k):
        return lambda e: e.tensor_scalar(*a, **k)

    def scalar_tensor_tensor(self, *a, **k):
        return lambda e: e.scalar_tensor_tensor(*a, **k)

    def tensor_tensor_scan(self, *a, **k):
        return lambda e: e.tensor_tensor_scan(*a, **k)

    def tensor_reduce(self, *a, **k):
        return lambda e: e.tensor_reduce(*a, **k)

    def tensor_copy(self, *a, **k):
        return lambda e: e.tensor_copy(*a, **k)

    def reciprocal(self, *a, **k):
        return lambda e: e.reciprocal(*a, **k)

    def matmul(self, *a, **k):
        return lambda e: e.matmul(*a, **k)

    def transpose(self, *a, **k):
        return lambda e: e.transpose(*a, **k)

    def dma_start(self, *a, **k):
        return lambda e: e.dma_start(*a, **k)

    def wait_ge(self, *a, **k):
        return lambda e: e.wait_ge(*a, **k)


NOTE = Note()


class Lane:

    def __init__(self, sem):
        self.sem, self.ops, self.count, self.seen = sem, [], 0, {}

    def wait(self, *tokens):
        for t in tokens:
            if isinstance(t, list):
                self.wait(*t)
                continue
            sem, value = t
            if self.seen.get(id(sem), 0) < value:
                self.seen[id(sem)] = value
                self.ops.append(lambda e, s=sem, v=value: e.wait_ge(s, v))

    def do(self, fn, *tokens):
        self.wait(*tokens)
        self.count += 1
        op = fn(NOTE)
        self.ops.append(lambda e: op(e).then_inc(self.sem, 1))
        return (self.sem, self.count)

    def quiet(self, fn, *tokens):
        self.wait(*tokens)
        self.ops.append(fn(NOTE))

    def dma(self, sem, dst, src, *tokens):
        self.wait(*tokens)
        self.ops.append(lambda e: e.dma_start(dst, src).then_inc(sem, 16))

    def now(self):
        return (self.sem, self.count)

    def play(self, e):
        for op in self.ops:
            op(e)


class Page:
    def __init__(self, f, r):
        self.f, self.r, self.after = f, r, []


class Slots:

    def __init__(self, pages):
        self.free = list(pages)

    def take(self):
        return self.free.pop(0)

    def give(self, page, *tokens):
        page.after = list(tokens)
        self.free.append(page)


def weave(main, sides, every):
    sides = [s for s in sides]
    n = 0
    for _ in main:
        n += 1
        if n % every == 0:
            sides = [s for s in sides if next(s, "end") != "end"]
    for _ in range(100000):
        sides = [s for s in sides if next(s, "end") != "end"]
        if not sides:
            return
    raise ValueError("a side waits for what is never queued")


def program(nc, a, out, order, probe):
    with ExitStack() as ctx:
        def sb(name, shape, dt=F32):
            return ctx.enter_context(nc.sbuf_tensor(name, shape, dt))

        def sem(name):
            return ctx.enter_context(nc.semaphore(name))

        both = []
        for i in range(NPAGE):
            with nc.sbuf_tensor(f"pageF{i}", [128, 512], F32) as pf:
                pass
            both.append((pf, sb(f"pageR{i}", [128, 512], F32R)))
        NR, NH = 4, 3
        wraw = sb("wraw", [128, NR, 8, 128])
        whi = sb("whi", [128, NH, 8, 128], F32R)
        wlo = sb("wlo", [128, NH, 8, 128], F32R)
        prm = sb("prm", [128, NPC])
        cst = sb("cst", [128, 5, 128])
        with nc.sbuf_tensor("tabG", [128, 1792], F32) as tabG:
            pass
        tabA = sb("tabA", [128, 1792])
        wal = sb("wal", [32, 2, 256])
        csil = sb("csil", [128, 8, 2])
        ccol = sb("ccol", [128, 8, 2])
        modc = sb("modc", [128, 16, 2])
        modr = sb("modr", [128, 32])
        A1 = sb("A1", [128, 8, 2])
        A2 = sb("A2", [128, 8])
        smal = sb("smal", [128, 256])
        xcb = sb("xcb", [128, TC])
        banks = [ctx.enter_context(nc.psum_tensor(f"bank{i}", [128, 512], F32)) for i in range(8)]

        pe, act, dve, pool, sp = (Lane(sem(n)) for n in ("s_pe", "s_act", "s_dve", "s_pool", "s_sp"))
        s_w = [sem(f"s_w{i}") for i in range(NR)]
        s_in = sem("s_in")
        s_pg = [sem(f"s_pg{i}") for i in range(132)]
        s_out = sem("s_out")

        pages = Slots([Page(f[:, :], r[:, :]) for f, r in both])
        mb = Slots([Page(b, None) for b in banks[0:4]])
        sbk = Slots([Page(b, None) for b in banks[4:8]])
        for p in mb.free + sbk.free:
            p.f = p.f[:, :]

        ident, ones, bones = cst[:, 0, :], cst[:, 1, :], cst[:, 2, :]
        maskF, maskB = cst[:, 3, :], cst[:, 4, :]
        gcos, gsin, smask = tabG[:, 0:512], tabG[:, 512:1024], tabG[:, 1024:1792]
        rA1, rA2 = tabA[:, 0:896], tabA[:, 896:1792]
        tabD = sb("tabD", [128, 896])[:, :]

        def col(name, i=0, n=1):
            o = PCOL[name][0] + i
            return prm[:, o:o + n]

        def bc(ap):
            return ap.bitcast(F32)

        dma_n = [0]

        def load(dst, src, *tokens):
            n = dma_n[0]
            dma_n[0] += 1
            s = s_pg[n % len(s_pg)]
            sp.dma(s, dst, src, *tokens)
            return (s, 16 * (n // len(s_pg) + 1))

        st = {"n": 0, "dma": 0, "split": 0}
        wtok = {}
        done = {}

        def w_dma(b):
            if b >= NB or b != st["dma"]:
                return
            st["dma"] += 1
            waits = [wtok[b - NR][0], wtok[b - NR][1]] if b >= NR else []
            sp.dma(s_w[b % NR], wraw[:, b % NR, :, :], a["wst"][b], *waits)

        def w_split(b):
            if b >= NB or b != st["split"]:
                return
            st["split"] += 1
            raw, hi, lo = wraw[:, b % NR, :, :], whi[:, b % NH, :, :], wlo[:, b % NH, :, :]
            landed = (s_w[b % NR], 16 * (b // NR + 1))
            waits = [done[b - NH]] if b >= NH else []
            h = act.do(lambda e: e.activation(hi, raw, ACT.Copy), landed, *waits)
            l = pool.do(lambda e: e.tensor_tensor(lo, raw, bc(hi), ALU.subtract), landed, h, *waits)
            wtok[b] = (h, l)
            w_dma(b + NR)

        def w_next(key):
            s = len(order)
            order.append(key)
            b = s // 8
            if s % 8 == 0:
                w_split(b + NH - 1)
                pe.wait(*wtok[b])
            return b, whi[:, b % NH, s % 8, :], wlo[:, b % NH, s % 8, :]

        def mm(o, l, r, start, stop, *tokens, skip=False):
            return pe.do(lambda e: e.matmul(o, l, r, start=start, stop=stop, skip_group_check=skip), *tokens)

        def mmq(o, l, r, start, stop, *tokens, skip=False):
            pe.quiet(lambda e: e.matmul(o, l, r, start=start, stop=stop, skip_group_check=skip), *tokens)

        def linear(name, m, kts, groups, step=2):
            tok = None
            for i, k in enumerate(kts):
                b, hi, lo = w_next((name, m, k))
                for o, xs in groups:
                    xh, xl, need = xs[i]
                    mmq(o, hi, xh, i == 0, False, need)
                    mmq(o, hi, xl, False, False)
                    tok = mm(o, lo, xh, False, i == len(kts) - 1)
                done[b] = tok
                if i % step == step - 1:
                    yield
            return tok

        def split(src, hi, lo, *need):
            h = act.do(lambda e: e.activation(hi, src, ACT.Copy), *need)
            l = dve.do(lambda e: e.tensor_tensor(lo, src, bc(hi), ALU.subtract), h, *need)
            return [h, l]

        def split_pages(src, *need):
            H, L = pages.take(), pages.take()
            t = split(src.f, H.r, L.r, H.after, L.after, *need)
            pages.give(src, *t)
            return (H, L, t)

        def xk(pairs):
            return [(H.r, L.r, t) for H, L, t in pairs]

        def give_pairs(pairs, *tokens):
            for H, L, _ in pairs:
                pages.give(H, *tokens)
                pages.give(L, *tokens)

        def rsqrt(vps, width, scale, *need):
            v, r, t = pages.take(), pages.take(), pages.take()
            vf, rf, tf = v.f[:, 0:width], r.f[:, 0:width], t.f[:, 0:width]
            a0 = act.do(lambda e: e.activation(rf, vps, ACT.Ln, scale=scale, bias=col("eps")), r.after, *need)
            a1 = act.do(lambda e: e.activation(rf, rf, ACT.Exp, scale=-0.5), a0)
            d0 = dve.do(lambda e: e.tensor_scalar(vf, vps, scale, EPS, ALU.mult, ALU.add), v.after, a0)
            d1 = dve.do(lambda e: e.tensor_tensor(tf, rf, rf, ALU.mult), a1, t.after)
            d2 = dve.do(lambda e: e.scalar_tensor_tensor(tf, tf, -0.5, vf, ALU.mult, ALU.mult), d1, d0)
            d3 = dve.do(lambda e: e.scalar_tensor_tensor(rf, tf, 1.5, rf, ALU.add, ALU.mult), d2)
            pages.give(v, d2)
            pages.give(t, d3)
            return r, d3, d0

        class Squares:

            def __init__(self, width=T):
                self.w, self.acc, self.tok = width, None, None

            def add(self, ap, need):
                q = pages.take()
                qf = q.f[:, 0:self.w]
                s = act.do(lambda e: e.activation(qf, ap, ACT.Square), q.after, need)
                if self.acc is None:
                    self.acc, self.tok = q, s
                    return
                af = self.acc.f[:, 0:self.w]
                self.tok = dve.do(lambda e: e.tensor_tensor(af, af, qf, ALU.add), s, self.tok)
                pages.give(q, self.tok)

            def product(self, mat, bks):
                p = bks.take()
                m = mm(p.f[:, 0:self.w], mat, self.acc.f[:, 0:self.w], True, True, self.tok, p.after)
                pages.give(self.acc, m)
                return p, m

            def rstd(self, n, mat, bks, early=None):
                p, m = early if early is not None else self.product(mat, bks)
                r, rt, d0 = rsqrt(p.f[:, 0:self.w], self.w, 1.0 / n, m)
                bks.give(p, d0)
                return r, rt

        def rstd_of(tiles, width, n, mat, bks):
            q = Squares(width)
            for ap, need in tiles:
                q.add(ap, need)
            return q.rstd(n, mat, bks)

        t_prm = load(prm[:, :], a["prm"])
        t_cc = load(ccol[:, :, :], a["ccol"])
        t_cst = load(cst[:, :, :], a["cst"])
        X = []
        for k in range(8):
            p = pages.take()
            p.w = [load(p.f, a["xT"][:, k, :], p.after)]
            p.rd = []
            X.append(p)
        XC = []
        for k in range(4):
            p = pages.take()
            XC.append((p, load(p.f, a["cT"][:, k, :], p.after)))
        w_dma(0)

        def mod_load(i):
            p = pages.take()
            return p, load(p.f, a["wmod"][i], p.after)

        modp = [mod_load(i) for i in range(32)]
        t_wal = load(wal[:, :, :], a["wal"])
        t_tab = load(tabG[:, :], a["tabG"])
        for b in range(1, NR):
            w_dma(b)

        def ctx_tile(k):
            p, t = XC[k // 2]
            return p.f[:, 256 * (k % 2):256 * (k % 2) + 256], t

        act.wait(t_prm)
        t_cs = act.do(lambda e: e.activation(csil[:, :, :], ccol[:, :, :], ACT.Silu), t_cc)
        sqx, sqc = Squares(T), Squares(TC)
        for k in range(8):
            sqx.add(X[k].f, X[k].w)
        for k in range(8):
            sqc.add(*ctx_tile(k))
        pe.wait(t_cst)

        bm = mb.take()
        rows = {}
        pe.wait(bm.after, t_cs)
        for c in range(5):
            if c < 4:
                b = sbk.take()
                pe.wait(b.after)
                for k in range(8):
                    p, land = modp[8 * c + k]
                    t = mm(b.f[0:2, :], csil[:, k, :], p.f, k == 0, k == 7, land)
                    pages.give(p, t)
                rw = pages.take()
                rows[c] = (rw, act.do(lambda e, rw=rw, b=b: e.activation(rw.f[0:2, :], b.f[0:2, :], ACT.Copy), t,
                                      rw.after))
                sbk.give(b, rows[c][1])
            if c == 1:
                early_x = sqx.product(ones, mb)
                early_c = sqc.product(ones, mb)
            if c >= 1:
                rw, tr = rows[c - 1]
                for i in range(4):
                    m = 4 * (c - 1) + i
                    t = pe.do(lambda e, m=m, i=i, rw=rw: e.transpose(bm.f[:, 2 * m:2 * m + 2],
                                                                    rw.f[0:2, 128 * i:128 * i + 128],
                                                                    ident[0:2, 0:2]), tr)
                pages.give(rw, t)
        rx, rxt = sqx.rstd(1024, ones, mb, early_x)
        rc, rct = sqc.rstd(1024, ones, mb, early_c)
        bcast = col("b_mod", 0, 16).unsqueeze(2).broadcast_to([128, 16, 2])
        t_mod = dve.do(lambda e: e.tensor_tensor(modc[:, :, :], bm.f[:, 0:32].rearrange("p (m c) -> p m c", c=2),
                                                 bcast, ALU.add), t, t_prm)
        mb.give(bm, t_mod)
        n1 = col("norm1_g", 0, 8).unsqueeze(2).broadcast_to([128, 8, 2])
        t_A1 = dve.do(lambda e: e.scalar_tensor_tensor(A1[:, :, :], modc[:, 8:16, :], 1.0, n1, ALU.add, ALU.mult),
                      t_mod)

        w_split(0)
        w_split(1)
        H, HC = [], []
        for k in range(8):
            t, Hk, Lk = pages.take(), pages.take(), pages.take()
            d = dve.do(lambda e, k=k, t=t: e.scalar_tensor_tensor(t.f, X[k].f, A1[:, k, 0:1], rx.f, ALU.mult,
                                                                 ALU.mult), t.after, X[k].w, t_A1, rxt)
            d2 = dve.do(lambda e, k=k, t=t: e.tensor_scalar(t.f, t.f, modc[:, k, 0:1], None, ALU.add), d)
            s = act.do(lambda e, Hk=Hk, t=t: e.activation(Hk.r, t.f, ACT.Copy), d2, Hk.after)
            p = pool.do(lambda e, Hk=Hk, Lk=Lk, t=t: e.tensor_tensor(Lk.r, t.f, bc(Hk.r), ALU.subtract), s, Lk.after)
            pages.give(t, s, p)
            H.append((Hk, Lk, [s, p]))
            ap, _ = ctx_tile(k)
            t, h = pages.take(), pages.take()
            dc = dve.do(lambda e, k=k, t=t, ap=ap: e.scalar_tensor_tensor(
                t.f[:, 0:256], ap, A1[:, k, 1:2], rc.f[:, 0:256], ALU.mult, ALU.mult), t.after, XC[k // 2][1], rct)
            d2 = dve.do(lambda e, k=k, t=t: e.tensor_scalar(t.f[:, 0:256], t.f[:, 0:256], modc[:, k, 1:2], None,
                                                            ALU.add), dc)
            s = act.do(lambda e, h=h, t=t: e.activation(h.r[:, 0:256], t.f[:, 0:256], ACT.Copy), d2, h.after)
            p = pool.do(lambda e, h=h, t=t: e.tensor_tensor(h.r[:, 256:512], t.f[:, 0:256], bc(h.r[:, 0:256]),
                                                           ALU.subtract), s, h.after)
            pages.give(t, s, p)
            HC.append((h, [s, p]))
        pages.give(rx, d)
        pages.give(rc, dc)
        for p, _ in XC:
            pages.give(p, dc, act.now())

        R = {}
        hcur = [None, None]

        def proj(name, m, xs, ctx=None, step=2, k0=0, bks=mb):
            o = bks.take()
            pe.wait(o.after)
            groups = [(o.f, xs)]
            oc = None
            if ctx is not None:
                oc = bks.take()
                pe.wait(oc.after)
                groups.append((oc.f[:, 0:256], ctx))
            tok = yield from linear(name, m, range(k0, k0 + len(xs)), groups, step)
            return o, oc, tok

        def wide(items, xs, ctx=None, late=None):
            outs = []
            for name, m in items:
                o = mb.take()
                pe.wait(o.after)
                oc = None
                if ctx is not None:
                    oc = mb.take()
                    pe.wait(oc.after)
                outs.append([o, oc, None])
            n = len(xs)
            for k in range(n):
                for i, (name, m) in enumerate(items):
                    if late is not None and k == n - 1 and i == len(items) - 1:
                        late()
                    b, hi, lo = w_next((name, m, k))
                    for o, src in ((outs[i][0].f, xs), (ctx and outs[i][1].f[:, 0:256], ctx)):
                        if src is None:
                            continue
                        xh, xl, need = src[k]
                        mmq(o, hi, xh, k == 0, False, need)
                        mmq(o, hi, xl, False, False)
                        tok = mm(o, lo, xh, False, k == n - 1)
                    outs[i][2] = done[b] = tok
                    yield
            return outs

        hx = xk(H)
        hcx = [(h.r[:, 0:256], h.r[:, 256:512], s) for h, s in HC]

        def copy_act(dst, src, *need, **kw):
            return act.do(lambda e: e.activation(dst, src, ACT.Copy, **kw), *need)

        def to_tokens(src, offs, width, bks, *need):
            b = bks.take()
            pe.wait(b.after, *need)
            for j, o in enumerate(offs):
                tok = pe.do(lambda e, j=j, o=o: e.transpose(b.f[:, j * 128:(j + 1) * 128], src[:, o:o + 128], ident))
            p = pages.take()
            w = 128 * len(offs)
            c = copy_act(p.f[:, 0:w], b.f[:, 0:w], tok, p.after)
            bks.give(b, c)
            return p, c, tok

        def main_gla():
            first = yield from wide([("w_lr", 0), ("wk_g", 0)], hx, hcx)
            o, oc, t = first[0]
            z = pages.take()
            zc = pages.take()
            c1 = copy_act(z.f[0:32, :], o.f[0:32, :], t, z.after)
            c2 = copy_act(zc.f[0:32, 0:256], oc.f[0:32, 0:256], t, zc.after)
            mb.give(o, c1)
            mb.give(oc, c2)
            R["z"] = (z, zc, [c1, c2])
            for m in range(2):
                o, oc, t = first[1] if m == 0 else (yield from proj("wk_g", m, hx, hcx))
                R["kg", m] = rope_gla(o, t)
                kc = pages.take()
                c = copy_act(kc.f[:, 0:256], oc.f[:, 0:256], t, kc.after)
                mb.give(oc, c)
                R["kgc", m] = (kc, c)
                o, oc, t = yield from proj("wq_g", m, hx)
                R["qg", m] = rope_gla(o, t)
                for h in (2 * m, 2 * m + 1):
                    o, oc, t = yield from proj("wv_g", h, hx, hcx)
                    v, vc = pages.take(), pages.take()
                    c1 = copy_act(v.f, o.f, t, v.after)
                    c2 = copy_act(vc.f[:, 0:256], oc.f[:, 0:256], t, vc.after)
                    mb.give(o, c1)
                    mb.give(oc, c2)
                    V, tv, r1 = to_tokens(v.f, [0, 128, 256, 384], 512, mb, c1)
                    VC, tvc, r2 = to_tokens(vc.f, [0, 128], 256, mb, c2)
                    pages.give(v, r1)
                    pages.give(vc, r2)
                    R["vg", h] = (V, VC, [tv, tvc])

        def rope_gla(o, t):
            p, q = pages.take(), pages.take()
            d1 = dve.do(lambda e: e.tensor_tensor(p.f, o.f, gcos, ALU.mult), t, p.after, t_tab)
            dve.wait(q.after)
            for a_ in range(4):
                s, d = 32 * (a_ ^ 1), 32 * a_
                d2 = dve.do(lambda e, s=s, d=d: e.tensor_tensor(q.f[d:d + 32, :], o.f[s:s + 32, :],
                                                                gsin[s:s + 32, :], ALU.mult))
            d3 = dve.do(lambda e: e.tensor_tensor(p.f, p.f, q.f, ALU.add), d1, d2)
            mb.give(o, d2)
            pages.give(q, d3)
            return (p, d3)

        def side_gla():
            while "z" not in R:
                yield
            z, zc, tz = R["z"]
            for m in range(2):
                while ("kg", m) not in R:
                    yield
                dirs = []
                for dr in range(2):
                    b1, b2 = sbk.take(), sbk.take()
                    lh = wal[:, dr, 128 * m:128 * m + 128]
                    mmq(b1.f, lh, z.f[0:32, :], True, True, tz, b1.after, t_wal)
                    t = mm(b2.f[:, 0:256], lh, zc.f[0:32, 0:256], True, True, b2.after)
                    la, lac = pages.take(), pages.take()
                    bcol = col("b_alpha", 2 * dr + m)
                    d1 = dve.do(lambda e, la=la, b1=b1, bcol=bcol: e.tensor_scalar(
                        la.f, b1.f, bcol, -20.0, ALU.add, ALU.max), t, la.after)
                    d2 = dve.do(lambda e, lac=lac, b2=b2, bcol=bcol: e.tensor_scalar(
                        lac.f[:, 0:256], b2.f[:, 0:256], bcol, -20.0, ALU.add, ALU.max), lac.after)
                    sbk.give(b1, d1)
                    sbk.give(b2, d2)
                    e1 = act.do(lambda e, la=la: e.activation(la.f, la.f, ACT.Exp, scale=-1.0), d1)
                    e2 = act.do(lambda e, lac=lac: e.activation(lac.f[:, 0:256], lac.f[:, 0:256], ACT.Exp,
                                                                scale=-1.0), d2)
                    dirs.append([la, lac, e1, e2])
                yield
                for dr in range(2):
                    la, lac, e1, e2 = dirs[dr]
                    l1 = act.do(lambda e, la=la: e.activation(la.f, la.f, ACT.Ln, bias=col("one")), e1)
                    l2 = act.do(lambda e, lac=lac: e.activation(lac.f[:, 0:256], lac.f[:, 0:256], ACT.Ln,
                                                                bias=col("one")), e2)
                    d1 = dve.do(lambda e, la=la: e.tensor_scalar(la.f, la.f, -1.0 / 16, -1.0, ALU.mult, ALU.max),
                                l1)
                    d2 = dve.do(lambda e, lac=lac: e.tensor_scalar(lac.f[:, 0:256], lac.f[:, 0:256], -1.0 / 16,
                                                                   -1.0, ALU.mult, ALU.max), l2)
                    P, PC = pages.take(), pages.take()
                    d3 = dve.do(lambda e, la=la, P=P: e.tensor_tensor_scan(P.f, smask[:, 0:512], la.f, 0.0,
                                                                           ALU.mult, ALU.add), d1, P.after, t_tab)
                    d4 = dve.do(lambda e, lac=lac, PC=PC: e.tensor_tensor_scan(
                        PC.f[:, 0:256], smask[:, 512:768], lac.f[:, 0:256], 0.0, ALU.mult, ALU.add), d2, PC.after)
                    dirs[dr] = [la, lac, P, PC, d3, d4]
                yield
                k, tk = R["kg", m]
                q, tq = R["qg", m] if ("qg", m) in R else (None, None)
                while q is None:
                    yield
                    if ("qg", m) in R:
                        q, tq = R["qg", m]
                kc, tkc = R["kgc", m]
                work = []
                for dr in range(2):
                    la, lac, P, PC, d3, d4 = dirs[dr]
                    v3 = P.f.rearrange("p (c t) -> p c t", t=64)
                    o8 = 8 * (2 * m + dr)
                    dec = smal[:, o8:o8 + 8]
                    te = act.do(lambda e, dec=dec, v3=v3: e.activation(dec, v3[:, :, 63], ACT.Exp), d3)
                    if dr == 0:
                        aw = act.do(lambda e, lac=lac, PC=PC: e.activation(
                            lac.f[:, 0:256], PC.f[:, 0:256], ACT.Exp, scale=-1.0, bias=PC.f[:, 255:256]), d4)
                        B, tB = P, d3
                        pages.give(la, d3)
                    else:
                        x1 = dve.do(lambda e, la=la, P=P: e.tensor_tensor(la.f, la.f, P.f, ALU.subtract), d3)
                        tot = v3[:, :, 63:64].broadcast_to([128, 8, 64])
                        tB = dve.do(lambda e, la=la, tot=tot: e.tensor_tensor(
                            la.f.rearrange("p (c t) -> p c t", t=64), la.f.rearrange("p (c t) -> p c t", t=64),
                            tot, ALU.add), x1)
                        x2 = dve.do(lambda e, lac=lac, PC=PC: e.tensor_tensor(
                            lac.f[:, 0:256], PC.f[:, 0:256], lac.f[:, 0:256], ALU.subtract), d4)
                        aw = act.do(lambda e, lac=lac: e.activation(lac.f[:, 0:256], lac.f[:, 0:256], ACT.Exp), x2)
                        pages.give(P, tB, te)
                        B = la
                    E1 = pages.take()
                    a1 = act.do(lambda e, E1=E1, B=B: e.activation(E1.f, B.f, ACT.Exp), tB, E1.after)
                    a2 = act.do(lambda e, B=B: e.activation(B.f, B.f, ACT.Exp, scale=-1.0), a1, te)
                    qd = dve.do(lambda e, E1=E1: e.scalar_tensor_tensor(E1.f, q.f, 0.125, E1.f, ALU.mult,
                                                                        ALU.mult), a1, tq)
                    ki = dve.do(lambda e, B=B: e.tensor_tensor(B.f, k.f, B.f, ALU.mult), a2, tk)
                    KE = pages.take()
                    ke = dve.do(lambda e, KE=KE, B=B, dec=dec: e.tensor_tensor(
                        KE.f.rearrange("p (c t) -> p c t", t=64), B.f.rearrange("p (c t) -> p c t", t=64),
                        dec.unsqueeze(2).broadcast_to([128, 8, 64]), ALU.mult), ki, te, KE.after)
                    kw = dve.do(lambda e, lac=lac: e.tensor_tensor(lac.f[:, 0:256], kc.f[:, 0:256],
                                                                   lac.f[:, 0:256], ALU.mult), aw, tkc)
                    pages.give(PC, aw, x2 if dr else aw)
                    work.append((E1, qd, B, ki, KE, ke, lac, kw, dec, te))
                    yield
                pages.give(k, dve.now())
                pages.give(q, dve.now())
                pages.give(kc, dve.now())
                while ("vg", 2 * m + 1) not in R:
                    yield
                states = []
                for dr in range(2):
                    E1, qd, B, ki, KE, ke, lac, kw, dec, te = work[dr]
                    KT, tkt, r1 = to_tokens(KE.f, [0, 128, 256, 384], 512, sbk, ke)
                    pages.give(KE, r1)
                    WT, twt, r2 = to_tokens(lac.f, [0, 128], 256, sbk, kw)
                    pages.give(lac, r2)
                    yield
                    S = [pages.take(), pages.take()]

                    def sview(c, S=S):
                        return S[c // 4].f[:, 128 * (c % 4):128 * (c % 4) + 128]

                    b0 = sbk.take()
                    for hp in range(2):
                        V, VC, tv = R["vg", 2 * m + hp]
                        for j in range(2):
                            t = mm(b0.f[64 * hp:64 * hp + 64, 0:128], WT.f[:, 128 * j + 64 * hp:128 * j + 64 * hp + 64],
                                   VC.f[:, 128 * j:128 * j + 128], j == 0, j == 1, twt, tv, b0.after)
                    pages.give(WT, t)
                    c0 = 7 if dr else 0
                    s_t = dve.do(lambda e, c0=c0, sview=sview, b0=b0: e.tensor_copy(sview(c0), b0.f[:, 0:128]), t,
                                 S[0].after, S[1].after)
                    sbk.give(b0, s_t)
                    yield
                    ub = [sbk.take(), sbk.take()]
                    for par in range(2):
                        pe.wait(ub[par].after)
                        for i in range(4):
                            for hp in range(2):
                                V, _, tv = R["vg", 2 * m + hp]
                                l = KT.f[64 * par:64 * par + 64, 128 * i + 64 * hp:128 * i + 64 * hp + 64]
                                r = V.f[64 * par:64 * par + 64, 128 * i:128 * i + 128]
                                t = mm(ub[par].f[64 * hp:64 * hp + 64, 128 * i:128 * i + 128], l, r, True, True,
                                       tkt, tv)
                    pages.give(KT, t)
                    dve.wait(t)
                    for i in range(7):
                        c = 7 - i if dr else i
                        n = c - 1 if dr else c + 1
                        u = ub[c % 2].f[:, 128 * (c // 2):128 * (c // 2) + 128]
                        s_t = dve.do(lambda e, c=c, n=n, u=u, dec=dec, sview=sview: e.scalar_tensor_tensor(
                            sview(n), sview(c), dec[:, c:c + 1], u, ALU.mult, ALU.add), s_t)
                    sbk.give(ub[0], s_t)
                    sbk.give(ub[1], s_t)
                    states.append((S, sview, s_t))
                    yield
                for hp in range(2):
                    rows = slice(64 * hp, 64 * hp + 64)
                    V, VC, tv = R["vg", 2 * m + hp]
                    atts = []
                    for dr in range(2):
                        E1, qd, B, ki, *_ = work[dr]
                        ab = sbk.take()
                        pe.wait(ab.after, qd, ki)
                        for j in range(4):
                            sl = slice(128 * j, 128 * j + 128)
                            t = mm(ab.f[:, sl], B.f[rows, sl], E1.f[rows, sl], True, True)
                        am = pages.take()
                        msk = (maskF, maskB)[dr].unsqueeze(1).broadcast_to([128, 4, 128])
                        d = dve.do(lambda e, am=am, ab=ab, msk=msk: e.tensor_tensor(
                            am.f.rearrange("p (j n) -> p j n", j=4), ab.f.rearrange("p (j n) -> p j n", j=4), msk,
                            ALU.mult), t, am.after)
                        sbk.give(ab, d)
                        atts.append((am, d))
                    yield
                    ob = sbk.take()
                    pe.wait(ob.after, tv)
                    for dr in range(2):
                        am, d = atts[dr]
                        for j in range(4):
                            sl = slice(128 * j, 128 * j + 128)
                            t = mm(ob.f[:, sl], V.f[:, sl], am.f[:, sl], dr == 0 and j == 0, False, d, skip=True)
                        pages.give(am, t)
                    for dr in range(2):
                        E1 = work[dr][0]
                        S, sview, s_t = states[dr]
                        for c in range(8):
                            t = mm(ob.f[:, 64 * c:64 * c + 64], sview(c)[rows, :], E1.f[rows, 64 * c:64 * c + 64],
                                   False, dr == 1 and c == 7, s_t, skip=True)
                    og = pages.take()
                    c = copy_act(og.f, ob.f, t, og.after)
                    sbk.give(ob, c)
                    pages.give(V, t)
                    pages.give(VC, t)
                    R["og_raw", 2 * m + hp] = (og, c)
                    yield
                for dr in range(2):
                    pages.give(work[dr][0], t)
                    pages.give(work[dr][2], t)
                    pages.give(states[dr][0][0], t)
                    pages.give(states[dr][0][1], t)
            pages.give(z, pe.now())
            pages.give(zc, pe.now())
            for h in range(4):
                while ("og", h) not in R:
                    yield
                o, to = R["og_raw", h]
                r, rt = rstd_of([(o.f, to)], T, 128, ones, sbk)
                yield
                d = dve.do(lambda e, o=o, r=r: e.scalar_tensor_tensor(o.f, o.f, col("gla_norm_g"), r.f, ALU.mult,
                                                                     ALU.mult), rt, to, act.now())
                g, tg = R["og", h]
                d2 = dve.do(lambda e, o=o, g=g: e.scalar_tensor_tensor(o.f, o.f, 0.5, g.f, ALU.mult, ALU.mult),
                            d, tg)
                pages.give(r, d)
                pages.give(g, d2)
                R["o_gla", h] = split_pages(o, d2)
                yield

        def perm(ap):
            return ap.rearrange("p (r c) -> p c r", c=64)

        def inperm(ap):
            return ap.rearrange("p (c r) -> p c r", r=8)

        def na_norm(o, t, g, width, tag, natural):
            raw = pages.take()
            c = copy_act(raw.f[:, 0:width], o.f[:, 0:width], t, raw.after)
            mb.give(o, c)
            r, rt = rstd_of([(raw.f[:, 0:width], c)], width, 64, bones, mb)
            q = pages.take()
            if natural:
                d = dve.do(lambda e: e.scalar_tensor_tensor(q.f[:, 0:width], raw.f[:, 0:width], g,
                                                            r.f[:, 0:width], ALU.mult, ALU.mult), rt, q.after)
            else:
                d = dve.do(lambda e: e.scalar_tensor_tensor(perm2(q.f), rc3(raw.f), g, rc3(r.f), ALU.mult,
                                                            ALU.mult), rt, q.after)
            pages.give(raw, d)
            pages.give(r, d)
            R[tag] = (q, d)

        def rc3(ap):
            return ap.rearrange("p (r c) -> p r c", c=64)

        def perm2(ap):
            return ap.rearrange("p (c r) -> p r c", r=8)

        gq = smal[:, 64:65]
        t_gq = dve.do(lambda e: e.tensor_scalar(gq, col("na_q_g"), 0.125, None, ALU.mult), t_prm)

        def main_na():
            dve.wait(t_gq)
            for m in range(4):
                o, oc, t = yield from proj("wk_na", m, hx, hcx)
                na_norm(o, t, col("na_k_g"), 512, ("kn", m), False)
                na_norm(oc, t, col("na_k_g"), 256, ("knc", m), True)
                o, oc, t = yield from proj("wv_na", m, hx, hcx)
                v, vc = pages.take(), pages.take()
                c1 = copy_act(perm2(v.f), rc3(o.f), t, v.after)
                c2 = copy_act(vc.f[:, 0:256], oc.f[:, 0:256], t, vc.after)
                mb.give(o, c1)
                mb.give(oc, c2)
                V, tv, r0 = to_tokens(v.f, [0, 128, 256, 384], 512, mb, c1)
                VS, ts, r1 = to_tokens(v.f, [64, 192, 320], 384, mb, c1)
                VC, tc, r2 = to_tokens(vc.f, [0, 128], 256, mb, c2)
                pages.give(v, r1)
                pages.give(vc, r2)
                R["vn", m] = (V, VS, VC, [tv, ts, tc])
                o, oc, t = yield from proj("wq_na", m, hx)
                na_norm(o, t, gq, 512, ("qn", m), False)

        def softmax(b, t, col0):
            nm, sm, rc_ = smal[:, col0:col0 + 1], smal[:, col0 + 1:col0 + 2], smal[:, col0 + 2:col0 + 3]
            d = dve.do(lambda e: e.tensor_reduce(nm, b.f, AX, ALU.max, negate=True), t)
            P = pages.take()
            x = act.do(lambda e: e.activation(P.f, b.f, ACT.Exp, bias=nm, accum_out=sm), d, P.after)
            sbk.give(b, x)
            d2 = dve.do(lambda e: e.reciprocal(rc_, sm), x)
            d3 = dve.do(lambda e: e.tensor_scalar(P.f, P.f, rc_, None, ALU.mult), d2)
            return P, d3

        def attention(jobs, scores, values, finish, ready):
            a_, b_ = {}, {}
            n = len(jobs)
            for i in range(n + 2):
                if i < n:
                    while not ready(jobs[i]):
                        yield
                    b = sbk.take()
                    t = scores(jobs[i], b)
                    a_[i] = softmax(b, t, 80 + 4 * (i % 8))
                    yield
                if 1 <= i <= n:
                    P, d = a_.pop(i - 1)
                    PT, tp, r = to_tokens(P.f, [0, 128, 256, 384], 512, sbk, d)
                    pages.give(P, r)
                    b_[i - 1] = (PT, tp)
                    yield
                if i >= 2:
                    PT, tp = b_.pop(i - 2)
                    t = values(jobs[i - 2], PT, tp)
                    pages.give(PT, t)
                    finish(jobs[i - 2], t)
                    yield

        def side_na():
            cur = {}
            bias = {}

            def bias_load(h, hf):
                if h < 8 and (h, hf) not in bias:
                    p = pages.take()
                    bias[h, hf] = (p, load(p.f.rearrange("p (q k) -> p q k", q=2), a["bias"][2 * h + hf], p.after))

            bias_load(0, 0)
            bias_load(0, 1)

            def scores(job, b):
                h, qt = job
                m, hp = h // 2, h % 2
                if qt % 2 == 0:
                    nh, nf = (h, 1) if qt == 0 else (h + 1, 0)
                    bias_load(nh, nf)
                q, tq = R["qn", m]
                k, tk = R["kn", m]
                kc, tkc = R["knc", m]
                rows = slice(64 * hp, 64 * hp + 64)
                k0 = NA_K0[qt]
                ql = q.f[rows, 128 * qt:128 * qt + 128]
                pe.wait(b.after, tq, tk, tkc)
                mmq(b.f[:, 0:256], ql, k.f[rows, k0:k0 + 256], True, False, skip=True)
                mmq(b.f[:, 256:512], ql, kc.f[rows, 0:256], False, False, skip=True)
                p, tb = bias[h, qt // 2]
                t = mm(b.f[:, 0:256], ident, p.f[:, 256 * (qt % 2):256 * (qt % 2) + 256], False, True, tb, skip=True)
                if qt % 2 == 1:
                    pages.give(p, t)
                return t

            def values(job, PT, tp):
                h, qt = job
                m, hp = h // 2, h % 2
                if m not in cur:
                    cur[m] = sbk.take()
                    pe.wait(cur[m].after)
                V, VS, VC, tv = R["vn", m]
                f = slice(64 * hp, 64 * hp + 64)

                def vt(page, j):
                    return page.f[:, 128 * j + 64 * hp:128 * j + 64 * hp + 64]

                loc = {0: (V, 0), 1: (VS, 0), 2: (VS, 1), 3: (V, 2)}[qt]
                ls = [vt(loc[0], loc[1]), vt(loc[0], loc[1] + 1), vt(VC, 0), vt(VC, 1)]
                for j in range(4):
                    t = mm(cur[m].f[f, 128 * qt:128 * qt + 128], ls[j], PT.f[:, 128 * j:128 * j + 128], j == 0,
                           j == 3, tp, tv)
                return t

            def finish(job, t):
                h, qt = job
                m = h // 2
                if h % 2 == 1 and qt == 3:
                    o = pages.take()
                    b = cur.pop(m)
                    c = act.do(lambda e: e.activation(rc3(o.f), perm2(b.f), ACT.Copy), t, o.after)
                    sbk.give(b, c)
                    R["o_na", m] = split_pages(o, c)
                    for key in (("qn", m), ("kn", m), ("knc", m)):
                        pages.give(R[key][0], pe.now())
                    for p in R["vn", m][0:3]:
                        pages.give(p, pe.now())

            jobs = [(h, qt) for h in range(8) for qt in range(4)]
            yield from attention(jobs, scores, values, finish, lambda job: ("qn", job[0] // 2) in R)

        def tanh_gate(o, t, bks):
            g = pages.take()
            c = act.do(lambda e: e.activation(g.f, o.f, ACT.Tanh, scale=0.5), t, g.after)
            bks.give(o, c)
            return g, c

        def main_og():
            for h in range(4):
                o, _, t = yield from proj("w_og", h, hx)
                g = pages.take()
                c = act.do(lambda e, g=g, o=o: e.activation(g.f, o.f, ACT.Tanh, scale=0.5), t, g.after)
                d = dve.do(lambda e, g=g, o=o: e.scalar_tensor_tensor(g.f, g.f, 1.0, o.f, ALU.add, ALU.mult), c)
                mb.give(o, d)
                R["og", h] = (g, d)

        def side_mod():
            while ("vg", 0) not in R:
                yield
            nxt = [mod_load(32), mod_load(33)]
            for c in range(8):
                acc = pages.take()
                for k in range(8):
                    p, land = nxt.pop(0)
                    i = 8 * c + k
                    w = csil[:, k, 0:1]
                    if k == 0:
                        d = dve.do(lambda e, p=p, w=w, acc=acc: e.tensor_scalar(acc.f, p.f, w, None, ALU.mult), land,
                                   acc.after, t_cs)
                    else:
                        d = dve.do(lambda e, p=p, w=w, acc=acc: e.scalar_tensor_tensor(acc.f, p.f, w, acc.f, ALU.mult,
                                                                                      ALU.add), land, d)
                    pages.give(p, d)
                    if i + 2 < 64:
                        nxt.append(mod_load(34 + i))
                    yield
                b = sbk.take()
                for j in range(4):
                    t = mm(b.f[:, j:j + 1], acc.f[:, 128 * j:128 * j + 128], ones[:, 0:1], True, True, d, b.after)
                pages.give(acc, t)
                o = modr[:, 4 * c:4 * c + 4]
                d = dve.do(lambda e, b=b, o=o, c=c: e.tensor_tensor(o, b.f[:, 0:4], col("b_mod", 16 + 4 * c, 4),
                                                                   ALU.add), t)
                sbk.give(b, d)
                yield
            d = dve.do(lambda e: e.scalar_tensor_tensor(A2[:, :], modr[:, 16:24], 1.0, col("norm2_g", 0, 8),
                                                        ALU.add, ALU.mult), d)
            d = dve.do(lambda e: e.tensor_scalar(modr[:, 0:8], modr[:, 0:8], 0.5, None, ALU.mult), d)
            R["mod"] = d

        def main_gates1():
            for m in range(8):
                for nm in ("w_ma", "w_mb"):
                    o, _, t = yield from proj(nm, m, hx)
                    R[nm, m] = tanh_gate(o, t, mb)

        def chain(*gens):
            for g in gens:
                yield from g

        def room(n):
            for _ in range(1000):
                if len(pages.free) >= n:
                    return
                yield
            raise ValueError("no room")

        def ready(*keys):
            for _ in range(1000):
                if all(k in R for k in keys):
                    return
                yield
            raise ValueError(f"never ready: {keys}")

        def branch(merged, gate, gm, w, xs, gates=None, final=None):
            for m in range(8):
                if gates is None:
                    yield from room(3)
                    o, _, t = yield from proj(gate, gm + m, hcur[0])
                    g, tg = hcur[1](o, t)
                else:
                    g, tg = gates[m]
                o, _, t = yield from proj(w, m, xs)
                d = dve.do(lambda e, g=g, o=o: e.scalar_tensor_tensor(g.f, g.f, 1.0, o.f, ALU.add, ALU.mult), tg, t)
                mb.give(o, d)
                if m not in merged:
                    merged[m] = (g, d)
                else:
                    acc, tok = merged[m]
                    tok = dve.do(lambda e, g=g, acc=acc: e.tensor_tensor(acc.f, acc.f, g.f, ALU.add), d, tok)
                    pages.give(g, tok)
                    merged[m] = (acc, tok)
                if final is not None:
                    final.append(split_pages(*merged[m]))

        def free_context():
            for h, _ in HC:
                pages.give(h, pe.now())
            yield

        mains1 = chain(main_gla(), main_og(), main_na(), free_context(), main_gates1())
        weave(mains1, [chain(side_gla(), side_na()), side_mod()], 1)
        give_pairs(H, pe.now())

        def run(gen):
            for _ in gen:
                pass

        def main_merge1():
            merged = {}
            yield from ready("mod")
            for key, w in (("o_gla", "w_branch_gla"), ("o_na", "w_branch_na")):
                pairs = [R.pop((key, m)) for m in range(4)]
                gates = [R.pop(({"o_na": "w_ma", "o_gla": "w_mb"}[key], m)) for m in range(8)]
                yield from branch(merged, None, 0, w, xk(pairs), gates, M if key == "o_na" else None)
                give_pairs(pairs, pe.now())

        M = []
        run(main_merge1())
        sq = Squares()

        def main_out1():
            xm = xk(M)
            for m in range(8):
                o, _, t = yield from proj("w_out", m, xm)
                d = dve.do(lambda e, m=m, o=o: e.scalar_tensor_tensor(X[m].f, o.f, modr[:, m:m + 1], X[m].f, ALU.mult,
                                                                      ALU.add), t, X[m].rd, R["mod"])
                mb.give(o, d)
                X[m].w, X[m].rd = [d], []
                sq.add(X[m].f, d)

        run(main_out1())
        give_pairs(M, pe.now())

        def norm_x2():
            r, rt = sq.rstd(1024, ones, sbk)
            res = []
            last = []
            for k in range(9):
                if k < 8:
                    t, Hk, Lk = pages.take(), pages.take(), pages.take()
                    d = dve.do(lambda e, k=k, t=t: e.scalar_tensor_tensor(t.f, X[k].f, A2[:, k:k + 1], r.f, ALU.mult,
                                                                         ALU.mult), t.after, rt)
                    X[k].rd = [d]
                    d2 = dve.do(lambda e, k=k, t=t: e.tensor_scalar(t.f, t.f, modr[:, 8 + k:9 + k], None, ALU.add), d)
                    h = act.do(lambda e, Hk=Hk, t=t: e.activation(Hk.r, t.f, ACT.Copy), d2, Hk.after)
                    last.append((t, Hk, Lk, h))
                if k > 0:
                    t_, H_, L_, h_ = last.pop(0)
                    lo = dve.do(lambda e, t_=t_, H_=H_, L_=L_: e.tensor_tensor(L_.r, t_.f, bc(H_.r), ALU.subtract),
                                h_, L_.after)
                    pages.give(t_, lo)
                    res.append((H_, L_, [h_, lo]))
            pages.give(r, d)
            return res

        def times(page, src, r, *need):
            return dve.do(lambda e: e.tensor_tensor(page.f, src, r.f, ALU.mult), page.after, *need)

        def main_ffn(sfx, Hf, on_out, rs=None):
            xh = xk(Hf)
            for hf in range(2):
                pairs = []
                for j in range(FH * hf, FH * hf + FH):
                    bks = mb
                    if j == 0:
                        first = yield from wide([(n + sfx, i) for i in range(2) for n in ("ffn_gate", "ffn_up")],
                                                xh, None, rs and (lambda: input_rms(rs)))
                    if j < 2:
                        (og, _, tg), (ou, _, tu) = first[2 * j:2 * j + 2]
                    else:
                        bks = sbk if rs is not None and j == 2 else mb
                        og, _, tg = yield from proj("ffn_gate" + sfx, j, xh, bks=bks)
                        ou, _, tu = yield from proj("ffn_up" + sfx, j, xh, bks=bks)
                    s = pages.take()
                    if rs is None:
                        c = act.do(lambda e, s=s, og=og: e.activation(s.f, og.f, ACT.Silu), tg, s.after)
                        bks.give(og, c)
                    else:
                        d = times(s, og.f, rs.r, tg, rs.rt)
                        bks.give(og, d)
                        c = act.do(lambda e, s=s: e.activation(s.f, s.f, ACT.Silu), d)
                    d = dve.do(lambda e, s=s, ou=ou: e.tensor_tensor(s.f, s.f, ou.f, ALU.mult), c, tu)
                    bks.give(ou, d)
                    if rs is not None:
                        d = dve.do(lambda e, s=s: e.tensor_tensor(s.f, s.f, rs.r.f, ALU.mult), d)
                    pairs.append(split_pages(s, d))
                if hf == 1:
                    give_pairs(Hf, pe.now())
                    if rs is not None:
                        pages.give(rs.r, d)
                for m in range(8):
                    o, _, t = yield from proj("ffn_down" + sfx, m, xk(pairs), None, 2, FH * hf)
                    on_out(hf, m, o, t)
                give_pairs(pairs, pe.now())

        H2 = norm_x2()

        def out_x(hf, m, o, t):
            d = dve.do(lambda e: e.scalar_tensor_tensor(X[m].f, o.f, modr[:, 24 + m:25 + m], X[m].f, ALU.mult,
                                                        ALU.add), t, X[m].rd, X[m].w)
            mb.give(o, d)
            X[m].w, X[m].rd = [d], []
            if hf == 1:
                input_hi(v0, m)

        class Input:

            def __init__(self, gain):
                self.gain, self.sq, self.pairs, self.hi, self.r, self.rt = gain, Squares(), [], [], None, None

        def input_hi(v, m):
            H_, L_, q = pages.take(), pages.take(), pages.take()
            h = act.do(lambda e: e.activation(H_.r, X[m].f, ACT.Copy, scale=col(v.gain, m)), X[m].w, H_.after)
            s = act.do(lambda e: e.activation(q.f, X[m].f, ACT.Square), q.after)
            v.hi.append((m, H_, L_, h, q, s))
            if m > 0:
                input_lo(v, *v.hi.pop(0))
            if m == 7:
                input_lo(v, *v.hi.pop(0))

        def input_lo(v, m, H_, L_, h, q, s):
            lo = dve.do(lambda e: e.scalar_tensor_tensor(L_.r, X[m].f, col(v.gain, m), bc(H_.r), ALU.mult,
                                                         ALU.subtract), h, L_.after)
            X[m].rd = [h, lo, s]
            v.pairs.append((H_, L_, [h, lo]))
            if m == 0:
                v.sq.acc, v.sq.tok = q, s
            else:
                acc = v.sq.acc
                v.sq.tok = pool.do(lambda e: e.tensor_tensor(acc.f, acc.f, q.f, ALU.add), s, v.sq.tok)
                pages.give(q, v.sq.tok)

        def input_rms(v):
            v.r, v.rt = v.sq.rstd(1024, ones, sbk)

        lg = smal[:, 128:144]

        def side_tables():
            R["tabA"] = load(tabA[:, :], a["tabA"], dve.now())
            pi = pages.take()
            tp = load(pi.f.bitcast(I32), a["pos"], pi.after)
            pf = pages.take()
            d0 = dve.do(lambda e: e.tensor_copy(pf.f, pi.f.bitcast(I32)), tp, pf.after)
            pages.give(pi, d0)
            yield
            for key, inv, sgn in (("m", "inv_m", "sgn_m"), ("r", "inv_r", "sgn_r")):
                an, kk = pages.take(), pages.take()
                d = dve.do(lambda e, an=an, inv=inv: e.tensor_scalar(an.f, pf.f, col(inv), None, ALU.mult), d0,
                           an.after)
                d = dve.do(lambda e, an=an, kk=kk: e.tensor_scalar(kk.f, an.f, 1 / (2 * np.pi), ROUND, ALU.mult,
                                                                   ALU.add), d, kk.after)
                d = dve.do(lambda e, kk=kk: e.tensor_scalar(kk.f, kk.f, -ROUND, None, ALU.add), d)
                for cc in (C1, C2, C3):
                    d = dve.do(lambda e, an=an, kk=kk, cc=cc: e.scalar_tensor_tensor(an.f, kk.f, -cc, an.f, ALU.mult,
                                                                                    ALU.add), d)
                d = dve.do(lambda e, an=an: e.tensor_scalar(an.f, an.f, -PI_IN, PI_IN, ALU.max, ALU.min), d)
                s1 = act.do(lambda e, an=an, kk=kk: e.activation(kk.f, an.f, ACT.Sin), d)
                d = act.do(lambda e, an=an: e.activation(an.f, an.f, ACT.Abs), s1)
                s2 = act.do(lambda e, an=an: e.activation(an.f, an.f, ACT.Sin, scale=-1.0, bias=col("halfpi")), d)
                d = dve.do(lambda e, kk=kk, sgn=sgn: e.tensor_scalar(kk.f, kk.f, col(sgn), None, ALU.mult), s1)
                R["cos", key], R["sin", key] = an, kk
                R["trig", key] = [s2, d]
                yield
            pages.give(pf, d)
            x = col("decay", 0, 16)
            s = [smal[:, 144 + 16 * i:160 + 16 * i] for i in range(2)]
            d = act.do(lambda e: e.activation(s[0], x, ACT.Abs))
            t = act.do(lambda e: e.activation(s[0], s[0], ACT.Exp, scale=-1.0), d)
            t = act.do(lambda e: e.activation(s[0], s[0], ACT.Ln, bias=col("one")), t)
            d = dve.do(lambda e: e.tensor_scalar(s[1], x, 0.0, None, ALU.min))
            R["lg"] = dve.do(lambda e: e.tensor_tensor(lg, s[1], s[0], ALU.subtract), t, d)
            yield

        v0 = Input("mix_pre0")
        weave(main_ffn("", H2, out_x), [side_tables()], 4)

        MSC = float(96 ** -0.5)
        RSC = float(128 ** -0.5)

        def layer(l, rs):
            L = str(l)
            Hl = rs.pairs
            xh = xk(Hl)
            big = {}
            qns = smal[:, 176 + 2 * l:178 + 2 * l]
            t_qn = dve.do(lambda e: e.tensor_scalar(qns, col("q_norm" + L, 0, 2), MSC, None, ALU.mult))
            cosM, sinM, trM = R["cos", "m"], R["sin", "m"], R["trig", "m"]
            cosR, sinR, trR = R["cos", "r"], R["sin", "r"], R["trig", "r"]

            def rope96(o, dst, t, *need):
                q = pages.take()
                d1 = dve.do(lambda e: e.tensor_tensor(dst.f[64:96, :], o.f[64:96, :], cosM.f[64:96, :], ALU.mult),
                            t, trM, dst.after, *need)
                d2 = dve.do(lambda e: e.tensor_tensor(q.f[64:96, :], o.f[96:128, :], sinM.f[96:128, :], ALU.mult),
                            q.after)
                d3 = dve.do(lambda e: e.tensor_tensor(dst.f[64:96, :], dst.f[64:96, :], q.f[64:96, :], ALU.add),
                            d1, d2)
                pages.give(q, d3)
                return d3

            def rope128(o, t):
                cos, sin, tr = big["rope"]
                p, q = pages.take(), pages.take()
                d1 = dve.do(lambda e: e.tensor_tensor(p.f, o.f, cos.f, ALU.mult), t, tr, p.after)
                dve.wait(q.after)
                for s, d in ((0, 64), (64, 0)):
                    d2 = dve.do(lambda e, s=s, d=d: e.tensor_tensor(q.f[d:d + 64, :], o.f[s:s + 64, :],
                                                                    sin.f[s:s + 64, :], ALU.mult))
                d3 = dve.do(lambda e: e.tensor_tensor(p.f, p.f, q.f, ALU.add), d1, d2)
                mb.give(o, d2)
                pages.give(q, d3)
                return p, d3

            def scaled(o, t, bks=mb):
                p = pages.take()
                d = times(p, o.f, rs.r, t, rs.rt)
                bks.give(o, d)
                return p, d

            def tanh_scaled(o, t, bks=mb):
                p, d = scaled(o, t, bks)
                return p, act.do(lambda e: e.activation(p.f, p.f, ACT.Tanh, scale=0.5), d)

            def main_mla():
                first = yield from wide([("w_kv" + L, 0), ("w_cq" + L, 0), ("w_cq" + L, 1), ("w_kpe" + L, 0)], xh,
                                        None, lambda: input_rms(rs))
                kv, tkv = scaled(first[0][0], first[0][2])
                cq = [scaled(o, t) for o, _, t in first[1:3]]
                raw, tr = scaled(first[3][0], first[3][2])
                kp = pages.take()
                d = rope96(raw, kp, tr)
                pages.give(raw, d)
                R["kpe"] = (kp, d)
                c, s = pages.take(), pages.take()
                d = times(c, cosR.f, rs.r, trR)
                d = times(s, sinR.f, rs.r)
                big["rope"] = (c, s, d)
                R["down"] = (kv, tkv, cq)

            def side_mla():
                while "down" not in R:
                    yield
                (kv, tkv, cq), (kp, tkp) = R.pop("down"), R.pop("kpe")
                s1, s2 = Squares(), Squares()
                s1.add(kv.f, tkv)
                for p, c in cq:
                    s2.add(p.f, c)
                yield
                r, rt = s1.rstd(128, ones, sbk)
                yield
                d = dve.do(lambda e: e.scalar_tensor_tensor(kv.f, kv.f, col("kv_norm" + L), r.f, ALU.mult, ALU.mult),
                           rt)
                pages.give(r, d)
                xkv = [split_pages(kv, d)]
                r, rt = s2.rstd(256, ones, sbk)
                yield
                xq = []
                for m, (p, c) in enumerate(cq):
                    d = dve.do(lambda e, p=p, m=m: e.scalar_tensor_tensor(p.f, p.f, qns[:, m:m + 1], r.f, ALU.mult,
                                                                         ALU.mult), rt, t_qn)
                    xq.append(split_pages(p, d))
                pages.give(r, d)
                yield
                made = {}

                def make(j):
                    o, _, t = yield from proj("w_kn" + L, j, xk(xkv))
                    ks = []
                    for hp in range(2):
                        p = pages.take()
                        c1 = copy_act(p.f[0:64, :], o.f[64 * hp:64 * hp + 64, :], t, p.after)
                        c2 = dve.do(lambda e, p=p: e.tensor_copy(p.f[64:96, :], kp.f[64:96, :]), tkp, p.after)
                        ks.append((p, [c1, c2]))
                    mb.give(o, c1)
                    yield
                    o, _, t = yield from proj("w_v" + L, j, xk(xkv))
                    v = pages.take()
                    c = copy_act(v.f, o.f, t, v.after)
                    mb.give(o, c)
                    yield
                    qs = []
                    for hp in range(2):
                        o, _, t = yield from proj("w_uq" + L, 2 * j + hp, xk(xq))
                        p = pages.take()
                        d = rope96(o, p, t)
                        c1 = copy_act(p.f[0:64, :], o.f[0:64, :], t, p.after, d)
                        mb.give(o, c1)
                        qs.append((p, [c1, d]))
                        yield
                    V, tv, r = to_tokens(v.f, [0, 128, 256, 384], 512, mb, c)
                    pages.give(v, r)
                    made[j] = (ks, qs, V, tv)

                yield from make(0)
                cur = {}

                def scores(job, b):
                    h, qt = job
                    ks, qs, V, tv = made[h // 2]
                    (q, tq), (k, tk) = qs[h % 2], ks[h % 2]
                    return mm(b.f, q.f[0:96, 128 * qt:128 * qt + 128], k.f[0:96, :], True, True, b.after, tq, tk)

                def values(job, PT, tp):
                    h, qt = job
                    j, hp = h // 2, h % 2
                    if j not in cur:
                        cur[j] = sbk.take()
                        pe.wait(cur[j].after)
                    V, tv = made[j][2:4]
                    for i in range(4):
                        t = mm(cur[j].f[64 * hp:64 * hp + 64, 128 * qt:128 * qt + 128],
                               V.f[:, 128 * i + 64 * hp:128 * i + 64 * hp + 64], PT.f[:, 128 * i:128 * i + 128],
                               i == 0, i == 3, tp, tv)
                    return t

                def finish(job, t):
                    h, qt = job
                    j = h // 2
                    if h % 2 == 1 and qt == 3:
                        o, b = pages.take(), cur.pop(j)
                        c = copy_act(o.f, b.f, t, o.after)
                        sbk.give(b, c)
                        R["o_mla", j] = split_pages(o, c)
                        ks, qs, V, tv = made.pop(j)
                        for p, _ in ks + qs:
                            pages.give(p, pe.now())
                        pages.give(V, pe.now())

                def maker():
                    for j in range(1, 4):
                        yield from make(j)
                        while j in made and len(made) > 1:
                            yield
                    give_pairs(xq, pe.now())
                    give_pairs(xkv, pe.now())
                    pages.give(kp, dve.now())

                mk = maker()
                jobs = [(h, qt) for h in range(8) for qt in range(4)]
                n = 0
                att = attention(jobs, scores, values, finish, lambda job: job[0] // 2 in made)
                started = {0}
                for _ in att:
                    n += 1
                    next(mk, None)
                    yield
                for _ in mk:
                    yield

            def main_conv():
                for m in range(4):
                    bks = sbk if m == 0 else mb
                    o1, _, t1 = yield from proj("w_cg" + L, m, xh, bks=bks)
                    g, tg = tanh_scaled(o1, t1, bks)
                    o2, _, t2 = yield from proj("w_ca" + L, m, xh, bks=bks)
                    p, d = scaled(o2, t2, bks)
                    d = dve.do(lambda e, g=g, p=p: e.scalar_tensor_tensor(g.f, g.f, 1.0, p.f, ALU.add, ALU.mult),
                               tg, d)
                    pages.give(p, d)
                    R["ca", m] = (g, d)

            def side_conv():
                while ("ca", 3) not in R:
                    yield
                ca = [R.pop(("ca", m)) for m in range(4)]
                acc = [pages.take() for _ in range(4)]
                tok = [None] * 4
                for j in [15] + [i for i in range(31) if i != 15]:
                    s = j - 15
                    lo, hi = max(0, -s), min(T, T - s)
                    for m in range(4):
                        w = col("w_dw" + L, 31 * m + j)
                        src, A = ca[m][0].f[:, lo + s:hi + s], acc[m].f[:, lo:hi]
                        if j == 15:
                            tok[m] = dve.do(lambda e, A=A, src=src, w=w: e.tensor_scalar(A, src, w, None, ALU.mult),
                                            ca[m][1], acc[m].after)
                        else:
                            tok[m] = dve.do(lambda e, A=A, src=src, w=w: e.scalar_tensor_tensor(
                                A, src, w, A, ALU.mult, ALU.add), tok[m])
                        yield
                for m in range(4):
                    pages.give(ca[m][0], tok[m])
                    tok[m] = dve.do(lambda e, m=m: e.tensor_scalar(acc[m].f, acc[m].f, 0.5, col("b_dw" + L, m),
                                                                   ALU.mult, ALU.add), tok[m])
                R["conv"] = (acc, tok)
                yield

            def centred(ps, toks, n):
                b = sbk.take()
                pe.wait(b.after)
                for i, (p, t) in enumerate(zip(ps, toks)):
                    mt = mm(b.f, ones, p.f, i == 0, i == len(ps) - 1, t)
                ds = []
                for p in ps:
                    ds.append(dve.do(lambda e, p=p: e.scalar_tensor_tensor(p.f, b.f, -1.0 / n, p.f, ALU.mult,
                                                                           ALU.add), mt))
                sbk.give(b, ds[-1])
                return ds

            def side_conv_norm():
                while "conv" not in R:
                    yield
                acc, tok = R.pop("conv")
                ds = centred(acc, tok, 512)
                yield
                r, rt = rstd_of([(p.f, d) for p, d in zip(acc, ds)], T, 512, ones, sbk)
                yield
                for m in range(4):
                    d = dve.do(lambda e, m=m: e.scalar_tensor_tensor(acc[m].f, acc[m].f, col("cln_g" + L, m), r.f,
                                                                     ALU.mult, ALU.mult), rt)
                    c = act.do(lambda e, m=m: e.activation(acc[m].f, acc[m].f, ACT.Silu, bias=col("cln_b" + L, m)),
                               d)
                    R["o_conv", m] = split_pages(acc[m], c)
                    yield
                pages.give(r, d)

            def main_ret(h):
                yield from room(14)
                vs = []
                for e_ in range(2):
                    o, _, t = yield from proj("w_rv" + L, 2 * h + e_, xh)
                    vs.append(scaled(o, t))
                for nm in ("rk", "rq"):
                    o, _, t = yield from proj("w_" + nm + L, h, xh)
                    R[nm, h] = rope128(o, t)
                    v, tv = vs.pop(0)
                    V, tv, r = to_tokens(v.f, [0, 128, 256, 384], 512, mb, tv)
                    pages.give(v, r)
                    R["rv", h, 1 - len(vs)] = (V, tv)
                for e_ in range(2):
                    o, _, t = yield from proj("w_rg" + L, 2 * h + e_, xh)
                    p, ta = scaled(o, t)
                    g = pages.take()
                    c = act.do(lambda e, g=g, p=p: e.activation(g.f, p.f, ACT.Tanh, scale=0.5), ta, g.after)
                    d = dve.do(lambda e, g=g, p=p: e.scalar_tensor_tensor(g.f, g.f, 1.0, p.f, ALU.add, ALU.mult), c)
                    pages.give(p, d)
                    R["rg", h, e_] = (g, d)

            def side_ret():
                for h in range(4):
                    while ("rg", h, 1) not in R:
                        yield
                    lf, lb = (lg[:, 8 * l + 4 * x + h:8 * l + 4 * x + h + 1] for x in range(2))
                    d = dve.do(lambda e, lf=lf: e.tensor_scalar(tabD, rA1, lf, None, ALU.mult), R["tabA"], R["lg"],
                               R["Dfree"])
                    d = dve.do(lambda e, lb=lb: e.scalar_tensor_tensor(tabD, rA2, lb, tabD, ALU.mult, ALU.add), d)
                    tD = act.do(lambda e: e.activation(tabD, tabD, ACT.Exp), d)
                    yield
                    (q, tq), (k, tk) = R.pop(("rq", h)), R.pop(("rk", h))
                    ats = []
                    for j in range(4):
                        b, at = sbk.take(), pages.take()
                        t = mm(b.f, k.f[:, 128 * j:128 * j + 128], q.f, True, True, b.after, tq, tk)
                        o0 = 384 - 128 * j
                        d = dve.do(lambda e, b=b, at=at, o0=o0: e.scalar_tensor_tensor(
                            at.f, b.f, RSC, tabD[:, o0:o0 + 512], ALU.mult, ALU.mult), t, tD, at.after)
                        sbk.give(b, d)
                        ats.append((at, d))
                        if j % 2:
                            yield
                    R["Dfree"] = [d]
                    pages.give(q, t)
                    pages.give(k, t)
                    os_, ots = [], []
                    for e_ in range(2):
                        V, tv = R.pop(("rv", h, e_))
                        b = sbk.take()
                        pe.wait(b.after, tv)
                        for j, (at, d) in enumerate(ats):
                            t = mm(b.f, V.f[:, 128 * j:128 * j + 128], at.f, j == 0, j == 3, d)
                        pages.give(V, t)
                        o = pages.take()
                        c = copy_act(o.f, b.f, t, o.after)
                        sbk.give(b, c)
                        os_.append(o)
                        ots.append(c)
                        yield
                    for at, _ in ats:
                        pages.give(at, t)
                    ds = centred(os_, ots, 256)
                    yield
                    r, rt = rstd_of([(p.f, d) for p, d in zip(os_, ds)], T, 256, ones, sbk)
                    yield
                    for e_ in range(2):
                        o, (g, tg) = os_[e_], R.pop(("rg", h, e_))
                        d = dve.do(lambda e, o=o, e_=e_, h=h: e.scalar_tensor_tensor(
                            o.f, o.f, col("gn_g" + L, 2 * h + e_), r.f, ALU.mult, ALU.mult), rt)
                        d2 = dve.do(lambda e, o=o, g=g: e.scalar_tensor_tensor(o.f, o.f, 0.5, g.f, ALU.mult,
                                                                               ALU.mult), d, tg)
                        pages.give(g, d2)
                        R["o_ret", 2 * h + e_] = split_pages(o, d2)
                    pages.give(r, d)
                    yield

            merged = {}
            hcur[:] = [xh, tanh_scaled]
            M = []

            def main_branch(i, key, n, w):
                yield from ready(*[(key, m) for m in range(n)])
                pairs = [R.pop((key, m)) for m in range(n)]
                yield from branch(merged, "w_gate" + L, 8 * i, w + L, xk(pairs), None, M if i == 2 else None)
                give_pairs(pairs, pe.now())

            weave(chain(main_mla(), main_conv(), main_ret(0), main_ret(1), main_branch(0, "o_mla", 4, "w_mo"),
                        main_branch(1, "o_conv", 4, "w_pw"), main_ret(2), main_ret(3),
                        main_branch(2, "o_ret", 8, "w_ro")),
                  [chain(side_mla(), side_ret()), side_conv(), side_conv_norm()], 1)
            give_pairs(Hl, pe.now())
            pages.give(rs.r, dve.now())
            for p in big["rope"][0:2]:
                pages.give(p, dve.now())
            F = []
            sf = Squares()

            def main_out():
                for m in range(8):
                    o, _, t = yield from proj("w_out" + L, m, xk(M))
                    f = pages.take()
                    c = copy_act(f.f, o.f, t, f.after, scale=0.5)
                    mb.give(o, c)
                    sf.add(f.f, c)
                    F.append((f, c))

            run(main_out())
            give_pairs(M, pe.now())

            def post_norm(F, sf, g, each):
                r, rt = sf.rstd(1024, ones, mb)
                for m, (f, c) in enumerate(F):
                    d = dve.do(lambda e, f=f, m=m: e.scalar_tensor_tensor(f.f, f.f, col(g, m), r.f, ALU.mult,
                                                                         ALU.mult), rt)
                    d = dve.do(lambda e, f=f, m=m: e.tensor_tensor(X[m].f, X[m].f, f.f, ALU.add), d, X[m].rd)
                    X[m].w, X[m].rd = [d], []
                    pages.give(f, d)
                    each(m)
                pages.give(r, d)

            vf = Input("ffn_pre" + L)
            post_norm(F, sf, "mix_post" + L, lambda m: input_hi(vf, m))
            F2 = []
            sf2 = Squares()

            def out_f(hf, m, o, t):
                if hf == 0:
                    f = pages.take()
                    c = copy_act(f.f, o.f, t, f.after)
                    F2.append((f, c))
                else:
                    f, c0 = F2[m]
                    c = dve.do(lambda e: e.tensor_tensor(f.f, f.f, o.f, ALU.add), t, c0)
                    F2[m] = (f, c)
                    sf2.add(f.f, c)
                mb.give(o, c)

            run(main_ffn(L, vf.pairs, out_f, vf))
            if l == 0:
                nxt = Input("mix_pre1")
                post_norm(F2, sf2, "ffn_post" + L, lambda m: input_hi(nxt, m))
                return nxt
            post_norm(F2, sf2, "ffn_post" + L, lambda m: sp.dma(s_out, out[:, m, :], X[m].f, X[m].w))

        R["Dfree"] = []
        layer(1, layer(0, v0))
        sp.quiet(lambda e: e.wait_ge(s_out, 128))

        while len(order) % 8:
            order.append(None)
        if probe:
            return

        block = ctx.enter_context(nc.Block())

        @block.sync
        def _(e):
            sp.play(e)

        @block.tensor
        def _(e):
            pe.play(e)

        @block.scalar
        def _(e):
            act.play(e)

        @block.vector
        def _(e):
            dve.play(e)

        @block.gpsimd
        def _(e):
            pool.play(e)


def columns(v):
    return np.ascontiguousarray(v.reshape(-1, 128).T)


def tables():
    i = np.arange(128)
    same = (i[:, None] // 64) == (i[None, :] // 64)
    cst = np.zeros((128, 5, 128), np.float32)
    cst[:, 0] = np.eye(128)
    cst[:, 1] = 1.0
    cst[:, 2] = same
    cst[:, 3] = same & (i[:, None] <= i[None, :])
    cst[:, 4] = same & (i[:, None] >= i[None, :])
    freqs = (np.float32(10000.0) ** (-np.arange(16, dtype=np.float32) / np.float32(16))).astype(np.float32)
    t = np.arange(T)
    tabG = np.zeros((128, 1792), np.float32)
    for p in range(128):
        j, second = p % 32, (p % 64) >= 32
        pos = (t // 64 if j < 16 else t % 64).astype(np.float32)
        ang = (pos * freqs[j % 16]).astype(np.float32)
        tabG[p, 0:512] = np.cos(ang)
        tabG[p, 512:1024] = -np.sin(ang) if second else np.sin(ang)
    tabG[:, 1024:1536] = (t % 64 != 0)
    tabG[:, 1536:1792] = (np.arange(256) != 0)
    c = np.arange(896)
    diff = (c[None, :] - 384 - i[:, None]).astype(np.float32)
    tabA = np.concatenate([np.maximum(diff, 0), np.maximum(-diff, 0)], 1).astype(np.float32)
    return cst, tabG, tabA


def na_bias(rpb):
    out = np.full((8, 4, 128, 256), -1e30, np.float32)
    for qt in range(4):
        q = 128 * qt + np.arange(128)
        k = NA_K0[qt] + np.arange(256)
        qc, qr = (q // 8)[:, None], (q % 8)[:, None]
        kc, kr = (k // 8)[None, :], (k % 8)[None, :]
        st = np.clip(qc - 8, 0, 48)
        inside = (kc >= st) & (kc < st + 16)
        dc = np.clip(kc - qc, -15, 15) + 15
        got = rpb[:, kr - qr + 7, dc]
        out[:, qt] = np.where(inside[None], got, out[:, qt])
    return np.ascontiguousarray(out.reshape(16, 2, 128, 256).transpose(0, 2, 1, 3))


def weights(inp):
    w = inp["w_in"][0]
    o = np.cumsum([0, 512, 512, 512, 256, 256, 512, 512, 32, 1024, 1024])
    hp = np.concatenate([np.arange(0, 16), np.arange(32, 48), np.arange(16, 32), np.arange(48, 64)])
    gp = np.concatenate([64 * h + hp for h in range(4)])
    lr = np.zeros((1024, 128), np.float32)
    lr[:, 0:32] = w[:, o[7]:o[8]]
    m = {
        "wq_na": w[:, o[0]:o[1]], "wk_na": w[:, o[1]:o[2]], "wv_na": w[:, o[2]:o[3]],
        "wq_g": w[:, o[3]:o[4]][:, gp], "wk_g": w[:, o[4]:o[5]][:, gp], "wv_g": w[:, o[5]:o[6]],
        "w_og": w[:, o[6]:o[7]], "w_lr": lr, "w_ma": w[:, o[8]:o[9]], "w_mb": w[:, o[9]:o[10]],
        "w_branch_na": inp["w_branch_na"][0], "w_branch_gla": inp["w_branch_gla"][0], "w_out": inp["w_out"][0],
        "ffn_gate": inp["w_ffn_gate"][0], "ffn_up": inp["w_ffn_up"][0], "ffn_down": inp["w_ffn_down"][0],
    }
    o = np.cumsum([0, 256, 128, 32, 1024, 512, 512, 1024, 1024, 3072])
    swap = np.concatenate([np.arange(16, 32), np.arange(0, 16)])
    for l in range(2):
        L = str(l)
        w = inp["w_in_2"][l]
        pe_ = w[:, o[2]:o[3]]
        kpe = np.zeros((1024, 128), np.float32)
        kpe[:, 64:96], kpe[:, 96:128] = pe_, pe_[:, swap]
        uq = inp["mla_w_uq_2"][l].reshape(256, 8, 96)
        uq = np.concatenate([uq, uq[:, :, 64:][:, :, swap]], 2).reshape(256, 1024)
        ukv = inp["mla_w_ukv_2"][l].reshape(128, 8, 128)
        m.update({
            "w_cq" + L: w[:, o[0]:o[1]], "w_kv" + L: w[:, o[1]:o[2]], "w_kpe" + L: kpe,
            "w_ca" + L: w[:, o[3]:o[3] + 512], "w_cg" + L: w[:, o[3] + 512:o[4]],
            "w_rq" + L: w[:, o[4]:o[5]], "w_rk" + L: w[:, o[5]:o[6]], "w_rv" + L: w[:, o[6]:o[7]],
            "w_rg" + L: w[:, o[7]:o[8]], "w_gate" + L: w[:, o[8]:o[9]],
            "w_uq" + L: uq, "w_kn" + L: ukv[:, :, 0:64].reshape(128, 512), "w_v" + L: ukv[:, :, 64:].reshape(128, 512),
            "w_mo" + L: inp["mla_w_o_2"][l], "w_pw" + L: inp["conv_w_pw_2"][l], "w_ro" + L: inp["ret_w_o_2"][l],
            "w_out" + L: inp["w_out_2"][l], "ffn_gate" + L: inp["ffn_w_gate_2"][l],
            "ffn_up" + L: inp["ffn_w_up_2"][l], "ffn_down" + L: inp["ffn_w_down_2"][l],
        })
    return m


def stream(mats, order):
    out = np.zeros((NB, 128, 8, 128), np.float32)
    for s, key in enumerate(order):
        if key is not None:
            name, m, k = key
            out[s // 8, :, s % 8, :] = mats[name][128 * k:128 * k + 128, 128 * m:128 * m + 128]
    return out


def params(inp):
    hp = np.concatenate([np.arange(0, 16), np.arange(32, 48), np.arange(16, 32), np.arange(48, 64)])
    gp = np.concatenate([64 * h + hp for h in range(4)])
    prm = np.zeros((128, NPC), np.float32)

    def put(name, v):
        o, n = PCOL[name]
        prm[:, o:o + n] = v

    put("eps", EPS)
    put("one", 1.0)
    put("halfpi", np.pi / 2)
    put("b_mod", columns(inp["b_mod"][0]))
    put("norm1_g", columns(inp["norm1_g"][0]))
    put("norm2_g", columns(inp["norm2_g"][0]))
    put("na_q_g", columns(np.concatenate([inp["na_q_norm_g"][0]] * 2)))
    put("na_k_g", columns(np.concatenate([inp["na_k_norm_g"][0]] * 2)))
    put("b_alpha", columns(np.ascontiguousarray(inp["gla_b_alpha"][0][:, gp])))
    put("gla_norm_g", columns(inp["gla_norm_g"][0]))
    im = (np.float32(10000.0) ** (-np.arange(0, 32, 2, dtype=np.float32) / np.float32(32))).astype(np.float32)
    ir = (np.float32(10000.0) ** (-np.arange(0, 128, 2, dtype=np.float32) / np.float32(128))).astype(np.float32)
    put("inv_m", np.tile(im, 8)[:, None])
    put("sgn_m", np.tile(np.repeat(np.float32([-1, 1]), 16), 4)[:, None])
    put("inv_r", np.tile(ir, 2)[:, None])
    put("sgn_r", np.repeat(np.float32([1, -1]), 64)[:, None])
    put("decay", np.broadcast_to(inp["ret_decay_logits_2"].reshape(1, 16), (128, 16)))
    for l in range(2):
        L = str(l)
        for n, k in (("mix_pre", "ln_mix_pre_2"), ("mix_post", "ln_mix_post_2"), ("ffn_pre", "ln_ffn_pre_2"),
                     ("ffn_post", "ln_ffn_post_2"), ("q_norm", "mla_q_norm_2"), ("kv_norm", "mla_kv_norm_2"),
                     ("b_dw", "conv_b_dw_2"), ("cln_g", "conv_ln_g_2"), ("cln_b", "conv_ln_b_2"),
                     ("gn_g", "ret_gn_g_2")):
            put(n + L, columns(inp[k][l]))
        put("w_dw" + L, inp["conv_w_dw_2"][l].reshape(31, 4, 128).transpose(2, 1, 0).reshape(128, 124))
    return prm


SHAPES = {
    "wst": ((NB, 128, 8, 128), F32), "prm": ((128, NPC), F32), "ccol": ((128, 8, 2), F32),
    "wmod": ((96, 128, 512), F32), "xT": ((128, 8, 512), F32), "cT": ((128, 4, 512), F32),
    "cst": ((128, 5, 128), F32), "tabG": ((128, 1792), F32), "tabA": ((128, 1792), F32), "wal": ((32, 2, 256), F32),
    "bias": ((16, 128, 2, 256), F32), "pos": ((128, 512), I32),
}


def arrays(inp, order):
    cst, tabG, tabA = tables()
    gp = np.concatenate([64 * h + np.concatenate([np.arange(0, 16), np.arange(32, 48), np.arange(16, 32),
                                                  np.arange(48, 64)]) for h in range(4)])
    wal = np.zeros((32, 2, 256), np.float32)
    wal[0:16, 0] = inp["gla_w_alpha"][0, 0][:, gp]
    wal[16:32, 1] = inp["gla_w_alpha"][0, 1][:, gp]
    wm = inp["w_mod"][0].reshape(8, 128, 12, 512).transpose(2, 0, 1, 3).reshape(96, 128, 512)
    got = {
        "wst": stream(weights(inp), order), "prm": params(inp),
        "ccol": np.stack([columns(inp["c"][0]), columns(inp["c_ctx"])], 2),
        "wmod": wm, "xT": inp["x"][0].T.reshape(8, 128, 512).transpose(1, 0, 2),
        "cT": inp["ctx"][0].T.reshape(4, 2, 128, 256).transpose(2, 0, 1, 3).reshape(128, 4, 512),
        "cst": cst, "tabG": tabG, "tabA": tabA, "wal": wal, "bias": na_bias(inp["na_rpb"][0]),
        "pos": np.repeat(inp["positions_2"][0:1], 128, 0),
    }
    return {k: np.ascontiguousarray(v) for k, v in got.items()}


def kernel(**inputs):
    import concourse.bacc as _bacc
    from concourse.bass_utils import run_bass_kernel_spmd as _run

    inp = {k: np.asarray(v) for k, v in inputs.items()}
    nc = _bacc.Bacc("TRN2", target_bir_lowering=False, num_devices=1)
    aps = {k: nc.dram_tensor(f"in_{k}", s, dt, kind="ExternalInput").ap() for k, (s, dt) in SHAPES.items()}
    out = nc.dram_tensor("out_x", (128, 8, 512), F32, kind="ExternalOutput").ap()
    order = []
    program(nc, aps, out, order, False)
    assert len(order) == 8 * NB, len(order) / 8
    got = arrays(inp, order)
    r = _run(nc, [{f"in_{k}": v for k, v in got.items()}], core_ids=[0])
    y = r.results[0]["out_x"]
    return np.ascontiguousarray(y.transpose(1, 0, 2).reshape(1024, 512).T)[None]
```

```python
from contextlib import ExitStack

import numpy as np

import concourse.bass as bass
from concourse import mybir

F32 = mybir.dt.float32
F32R = mybir.dt.float32r
I32 = mybir.dt.int32
ACT = mybir.ActivationFunctionType
ALU = mybir.AluOpType
AX = mybir.AxisListType.X

T = 512
TC = 256
EPS = 1e-6
FT = 22
FH = 11
NB = 429
NPAGE = 70
ROUND = 12582912.0
C1 = 6.28125
C2 = float(np.floor((2 * np.pi - C1) * 2.0**20) / 2.0**20)
C3 = float(2 * np.pi - C1 - C2)
PI_IN = 3.1415925
NA_K0 = [0, 64, 192, 256]

PARAMS = [
    ("eps", 1), ("one", 1), ("halfpi", 1),
    ("b_mod", 48), ("norm1_g", 8), ("norm2_g", 8), ("na_q_g", 1), ("na_k_g", 1), ("b_alpha", 4),
    ("gla_norm_g", 1), ("inv_m", 1), ("sgn_m", 1), ("inv_r", 1), ("sgn_r", 1), ("decay", 16),
]
for _l in range(2):
    PARAMS += [(f"{n}{_l}", c) for n, c in (
        ("mix_pre", 8), ("mix_post", 8), ("ffn_pre", 8), ("ffn_post", 8), ("q_norm", 2), ("kv_norm", 1),
        ("w_dw", 124), ("b_dw", 4), ("cln_g", 4), ("cln_b", 4), ("gn_g", 8))]
PCOL = {}
NPC = 0
for _n, _c in PARAMS:
    PCOL[_n] = (NPC, _c)
    NPC += _c


class Note:

    def activation(self, *a, **k):
        return lambda e: e.activation(*a, **k)

    def tensor_tensor(self, *a, **k):
        return lambda e: e.tensor_tensor(*a, **k)

    def tensor_scalar(self, *a, **k):
        return lambda e: e.tensor_scalar(*a, **k)

    def scalar_tensor_tensor(self, *a, **k):
        return lambda e: e.scalar_tensor_tensor(*a, **k)

    def tensor_tensor_scan(self, *a, **k):
        return lambda e: e.tensor_tensor_scan(*a, **k)

    def tensor_reduce(self, *a, **k):
        return lambda e: e.tensor_reduce(*a, **k)

    def tensor_copy(self, *a, **k):
        return lambda e: e.tensor_copy(*a, **k)

    def reciprocal(self, *a, **k):
        return lambda e: e.reciprocal(*a, **k)

    def matmul(self, *a, **k):
        return lambda e: e.matmul(*a, **k)

    def transpose(self, *a, **k):
        return lambda e: e.transpose(*a, **k)

    def dma_start(self, *a, **k):
        return lambda e: e.dma_start(*a, **k)

    def wait_ge(self, *a, **k):
        return lambda e: e.wait_ge(*a, **k)


NOTE = Note()


class Lane:

    def __init__(self, sem):
        self.sem, self.ops, self.count, self.seen = sem, [], 0, {}

    def wait(self, *tokens):
        for t in tokens:
            if isinstance(t, list):
                self.wait(*t)
                continue
            sem, value = t
            if self.seen.get(id(sem), 0) < value:
                self.seen[id(sem)] = value
                self.ops.append(lambda e, s=sem, v=value: e.wait_ge(s, v))

    def do(self, fn, *tokens):
        self.wait(*tokens)
        self.count += 1
        op = fn(NOTE)
        self.ops.append(lambda e: op(e).then_inc(self.sem, 1))
        return (self.sem, self.count)

    def quiet(self, fn, *tokens):
        self.wait(*tokens)
        self.ops.append(fn(NOTE))

    def dma(self, sem, dst, src, *tokens):
        self.wait(*tokens)
        self.ops.append(lambda e: e.dma_start(dst, src).then_inc(sem, 16))

    def now(self):
        return (self.sem, self.count)

    def play(self, e):
        for op in self.ops:
            op(e)


class Page:
    def __init__(self, f, r):
        self.f, self.r, self.after = f, r, []


class Slots:

    def __init__(self, pages):
        self.free = list(pages)

    def take(self):
        return self.free.pop(0)

    def give(self, page, *tokens):
        page.after = list(tokens)
        self.free.append(page)


def weave(main, sides, every):
    sides = [s for s in sides]
    n = 0
    for _ in main:
        n += 1
        if n % every == 0:
            sides = [s for s in sides if next(s, "end") != "end"]
    for _ in range(100000):
        sides = [s for s in sides if next(s, "end") != "end"]
        if not sides:
            return
    raise ValueError("a side waits for what is never queued")


def program(nc, a, out, order):
    with ExitStack() as ctx:
        def sb(name, shape, dt=F32):
            return ctx.enter_context(nc.sbuf_tensor(name, shape, dt))

        def sem(name):
            return ctx.enter_context(nc.semaphore(name))

        both = []
        for i in range(NPAGE):
            with nc.sbuf_tensor(f"pageF{i}", [128, 512], F32) as pf:
                pass
            both.append((pf, sb(f"pageR{i}", [128, 512], F32R)))
        NR, NH = 3, 4
        wraw = sb("wraw", [128, NR, 8, 128])
        whi = sb("whi", [128, NH, 8, 128], F32R)
        wlo = sb("wlo", [128, NH, 8, 128], F32R)
        prm = sb("prm", [128, NPC])
        cst = sb("cst", [128, 5, 128])
        with nc.sbuf_tensor("tabG", [128, 1792], F32) as tabG:
            pass
        tabA = sb("tabA", [128, 1792])
        wal = sb("wal", [32, 2, 256])
        csil = sb("csil", [128, 8, 2])
        ccol = sb("ccol", [128, 8, 2])
        modc = sb("modc", [128, 16, 2])
        modr = sb("modr", [128, 32])
        A1 = sb("A1", [128, 8, 2])
        A2 = sb("A2", [128, 8])
        smal = sb("smal", [128, 256])
        banks = [ctx.enter_context(nc.psum_tensor(f"bank{i}", [128, 512], F32)) for i in range(8)]

        pe, act, dve, pool, sp = (Lane(sem(n)) for n in ("s_pe", "s_act", "s_dve", "s_pool", "s_sp"))
        s_w = [sem(f"s_w{i}") for i in range(NR)]
        s_pg = [sem(f"s_pg{i}") for i in range(132)]
        s_out = sem("s_out")

        pages = Slots([Page(f[:, :], r[:, :]) for f, r in both])
        mb = Slots([Page(b, None) for b in banks[0:4]])
        sbk = Slots([Page(b, None) for b in banks[4:8]])
        for p in mb.free + sbk.free:
            p.f = p.f[:, :]

        ident, ones, bones = cst[:, 0, :], cst[:, 1, :], cst[:, 2, :]
        maskF, maskB = cst[:, 3, :], cst[:, 4, :]
        gcos, gsin, smask = tabG[:, 0:512], tabG[:, 512:1024], tabG[:, 1024:1792]
        rA1, rA2 = tabA[:, 0:896], tabA[:, 896:1792]
        tabD = sb("tabD", [128, 896])[:, :]

        def col(name, i=0, n=1):
            o = PCOL[name][0] + i
            return prm[:, o:o + n]

        def bc(ap):
            return ap.bitcast(F32)

        dma_n = [0]

        def load(dst, src, *tokens):
            n = dma_n[0]
            dma_n[0] += 1
            s = s_pg[n % len(s_pg)]
            sp.dma(s, dst, src, *tokens)
            return (s, 16 * (n // len(s_pg) + 1))

        st = {"n": 0, "dma": 0, "split": 0}
        wtok = {}
        done = {}

        def w_dma(b):
            if b >= NB or b != st["dma"]:
                return
            st["dma"] += 1
            waits = [wtok[b - NR][0], wtok[b - NR][1]] if b >= NR else []
            sp.dma(s_w[b % NR], wraw[:, b % NR, :, :], a["wst"][b], *waits)

        def w_split(b):
            if b >= NB or b != st["split"]:
                return
            st["split"] += 1
            raw, hi, lo = wraw[:, b % NR, :, :], whi[:, b % NH, :, :], wlo[:, b % NH, :, :]
            landed = (s_w[b % NR], 16 * (b // NR + 1))
            waits = [done[b - NH]] if b >= NH else []
            h = act.do(lambda e: e.activation(hi, raw, ACT.Copy), landed, *waits)
            l = pool.do(lambda e: e.tensor_tensor(lo, raw, bc(hi), ALU.subtract), landed, h, *waits)
            wtok[b] = (h, l)
            w_dma(b + NR)

        def w_next(key):
            s = len(order)
            order.append(key)
            b = s // 8
            if s % 8 == 0:
                w_split(b + NH - 1)
                pe.wait(*wtok[b])
            return b, whi[:, b % NH, s % 8, :], wlo[:, b % NH, s % 8, :]

        def pause(n):
            for _ in range(n):
                yield

        def mm(o, l, r, start, stop, *tokens, skip=False):
            return pe.do(lambda e: e.matmul(o, l, r, start=start, stop=stop, skip_group_check=skip), *tokens)

        def mmq(o, l, r, start, stop, *tokens, skip=False):
            pe.quiet(lambda e: e.matmul(o, l, r, start=start, stop=stop, skip_group_check=skip), *tokens)

        def linear(name, m, kts, groups, step=2):
            tok = None
            for i, k in enumerate(kts):
                b, hi, lo = w_next((name, m, k))
                for o, xs in groups:
                    xh, xl, need = xs[i]
                    mmq(o, hi, xh, i == 0, False, need)
                    mmq(o, hi, xl, False, False)
                    tok = mm(o, lo, xh, False, i == len(kts) - 1)
                done[b] = tok
                if i % step == step - 1:
                    yield
            return tok

        def split_pages(src, *need, lane=dve):
            H, L = pages.take(), pages.take()
            h = act.do(lambda e: e.activation(H.r, src.f, ACT.Copy), H.after, *need)
            l = lane.do(lambda e: e.tensor_tensor(L.r, src.f, bc(H.r), ALU.subtract), h, L.after, *need)
            pages.give(src, h, l)
            return (H, L, [h, l])

        def xk(pairs):
            return [(H.r, L.r, t) for H, L, t in pairs]

        def give_pairs(pairs, *tokens):
            for H, L, _ in pairs:
                pages.give(H, *tokens)
                pages.give(L, *tokens)

        def rsqrt_act(vps, width, scale, *need):
            v, r = pages.take(), pages.take()
            vf, rf = v.f[:, 0:width], r.f[:, 0:width]
            a0 = act.do(lambda e: e.activation(rf, vps, ACT.Ln, scale=scale, bias=col("eps")), r.after, *need)
            a1 = act.do(lambda e: e.activation(rf, rf, ACT.Exp, scale=-0.5), a0)
            a2 = act.do(lambda e: e.activation(vf, vps, ACT.Identity, scale=scale, bias=col("eps")), v.after)
            return v, r, a1, a2

        def rsqrt_dve(width, v, r, a1, a2):
            t = pages.take()
            vf, rf, tf = v.f[:, 0:width], r.f[:, 0:width], t.f[:, 0:width]
            d1 = dve.do(lambda e: e.tensor_tensor(tf, rf, rf, ALU.mult), a1, t.after)
            d2 = dve.do(lambda e: e.scalar_tensor_tensor(tf, tf, -0.5, vf, ALU.mult, ALU.mult), d1, a2)
            d3 = dve.do(lambda e: e.scalar_tensor_tensor(rf, tf, 1.5, rf, ALU.add, ALU.mult), d2)
            pages.give(v, d2)
            pages.give(t, d3)
            return r, d3

        class Squares:

            def __init__(self, width=T):
                self.w, self.acc, self.tok, self.last = width, None, None, None

            def add(self, ap, need, scale=1.0, last=False):
                q = pages.take()
                qf = q.f[:, 0:self.w]
                s = act.do(lambda e: e.activation(qf, ap, ACT.Square, scale=scale), q.after, need)
                if last:
                    self.last = (q, s)
                    return
                if self.acc is None:
                    self.acc, self.tok = q, s
                    return
                af = self.acc.f[:, 0:self.w]
                self.tok = dve.do(lambda e: e.tensor_tensor(af, af, qf, ALU.add), s, self.tok)
                pages.give(q, self.tok)

            def product(self, mat, bks, warm=False):
                if warm:
                    act.do(lambda e: e.activation(smal[:, 255:256], col("one"), ACT.Ln))
                p = bks.take()
                m = mm(p.f[:, 0:self.w], mat, self.acc.f[:, 0:self.w], True, self.last is None, self.tok, p.after)
                pages.give(self.acc, m)
                if self.last is not None:
                    q, s = self.last
                    m = mm(p.f[:, 0:self.w], mat, q.f[:, 0:self.w], False, True, s)
                    pages.give(q, m)
                return p, m

            def rstd(self, n, mat, bks, early=None, warm=False):
                p, m = early if early is not None else self.product(mat, bks, warm)
                st_ = rsqrt_act(p.f[:, 0:self.w], self.w, 1.0 / n, m)
                bks.give(p, st_[3])
                return rsqrt_dve(self.w, *st_)

            def rstd_steps(self, n, mat, bks):
                p, m = self.product(mat, bks)
                st_ = rsqrt_act(p.f[:, 0:self.w], self.w, 1.0 / n, m)
                bks.give(p, st_[3])
                yield from pause(2)
                return rsqrt_dve(self.w, *st_)

        t_prm = load(prm[:, :], a["prm"])
        t_cc = load(ccol[:, :, :], a["ccol"])
        t_cst = load(cst[:, :, :], a["cst"])

        def mod_load(i):
            p = pages.take()
            return p, load(p.f, a["wmod"][i], p.after)

        modp = {(0, k): mod_load(k) for k in range(8)}
        X = []
        for k in range(8):
            p = pages.take()
            p.w = [load(p.f, a["xT"][:, k, :], p.after)]
            p.rd = []
            X.append(p)
        modp.update({(2, k): mod_load(16 + k) for k in range(8)})
        XC = []
        for k in range(4):
            p = pages.take()
            XC.append((p, load(p.f, a["cT"][:, k, :], p.after)))
        w_dma(0)
        modp.update({(c, k): mod_load(8 * c + k) for c in (1, 3) for k in range(8)})
        t_wal = load(wal[:, :, :], a["wal"])
        t_tab = load(tabG[:, :], a["tabG"])
        for b in range(1, NR):
            w_dma(b)

        def ctx_tile(k):
            p, t = XC[k // 2]
            return p.f[:, 256 * (k % 2):256 * (k % 2) + 256], t

        act.wait(t_prm)
        t_cs = act.do(lambda e: e.activation(csil[:, :, :], ccol[:, :, :], ACT.Silu), t_cc)
        sqx, sqc = Squares(T), Squares(TC)
        for k in range(8):
            sqx.add(X[k].f, X[k].w)
        for k in range(8):
            sqc.add(*ctx_tile(k))
        pe.wait(t_cst)

        pe.wait(t_cs)

        def mod_rows(c):
            b = sbk.take()
            pe.wait(b.after)
            for k in range(8):
                p, land = modp[c, k]
                t = mm(b.f[0:2, :], csil[:, k, :], p.f, k == 0, k == 7, land)
                pages.give(p, t)
            rw = pages.take()
            tr = act.do(lambda e: e.activation(rw.f[0:2, :], b.f[0:2, :], ACT.Copy), t, rw.after)
            sbk.give(b, tr)
            return rw, tr

        def mod_columns(half, part, rw, tr):
            b = mb.take()
            pe.wait(b.after)
            for i in range(4):
                t = pe.do(lambda e, i=i: e.transpose(b.f[:, 2 * i:2 * i + 2], rw.f[0:2, 128 * i:128 * i + 128],
                                                     ident[0:2, 0:2]), tr)
            pages.give(rw, t)
            sl = slice(8 * part + 4 * half, 8 * part + 4 * half + 4)
            bcast = col("b_mod", sl.start, 4).unsqueeze(2).broadcast_to([128, 4, 2])
            t = dve.do(lambda e: e.tensor_tensor(
                modc[:, sl, :], b.f[:, 0:8].rearrange("p (m c) -> p m c", c=2), bcast, ALU.add), t, t_prm)
            mb.give(b, t)
            if part == 1:
                n1 = col("norm1_g", 4 * half, 4).unsqueeze(2).broadcast_to([128, 4, 2])
                t = dve.do(lambda e: e.scalar_tensor_tensor(A1[:, 4 * half:4 * half + 4, :], modc[:, sl, :], 1.0, n1,
                                                            ALU.add, ALU.mult), t)
            return t

        r0 = mod_rows(0)
        early_x = sqx.product(ones, sbk)
        r2 = mod_rows(2)
        mod_columns(0, 0, *r0)
        early_c = sqc.product(ones, sbk)
        rx, rxt = sqx.rstd(1024, ones, sbk, early_x)
        r1 = mod_rows(1)
        t_A = [mod_columns(0, 1, *r2)]
        rc, rct = sqc.rstd(1024, ones, sbk, early_c)
        r3 = mod_rows(3)
        mod_columns(1, 0, *r1)
        H, HC = [], []

        w_split(0)
        w_split(1)
        w_split(2)
        for k in range(8):
            if k == 4:
                t_A.append(mod_columns(1, 1, *r3))
            t, Hk, Lk = pages.take(), pages.take(), pages.take()
            d = dve.do(lambda e, k=k, t=t: e.scalar_tensor_tensor(t.f, X[k].f, A1[:, k, 0:1], rx.f, ALU.mult,
                                                                 ALU.mult), t.after, X[k].w, t_A[k // 4], rxt)
            d2 = dve.do(lambda e, k=k, t=t: e.tensor_scalar(t.f, t.f, modc[:, k, 0:1], None, ALU.add), d)
            s = act.do(lambda e, Hk=Hk, t=t: e.activation(Hk.r, t.f, ACT.Copy), d2, Hk.after)
            p = pool.do(lambda e, Hk=Hk, Lk=Lk, t=t: e.tensor_tensor(Lk.r, t.f, bc(Hk.r), ALU.subtract), s, Lk.after)
            pages.give(t, s, p)
            H.append((Hk, Lk, [s, p]))
            ap, _ = ctx_tile(k)
            t, h = pages.take(), pages.take()
            dc = dve.do(lambda e, k=k, t=t, ap=ap: e.scalar_tensor_tensor(
                t.f[:, 0:256], ap, A1[:, k, 1:2], rc.f[:, 0:256], ALU.mult, ALU.mult), t.after, XC[k // 2][1], rct)
            d2 = dve.do(lambda e, k=k, t=t: e.tensor_scalar(t.f[:, 0:256], t.f[:, 0:256], modc[:, k, 1:2], None,
                                                            ALU.add), dc)
            s = act.do(lambda e, h=h, t=t: e.activation(h.r[:, 0:256], t.f[:, 0:256], ACT.Copy), d2, h.after)
            p = pool.do(lambda e, h=h, t=t: e.tensor_tensor(h.r[:, 256:512], t.f[:, 0:256], bc(h.r[:, 0:256]),
                                                           ALU.subtract), s, h.after)
            pages.give(t, s, p)
            HC.append((h, [s, p]))
        pages.give(rx, d)
        pages.give(rc, dc)
        for p, _ in XC:
            pages.give(p, dc, act.now())

        R = {}
        hcur = [None, None]

        def proj(name, m, xs, ctx=None, step=2, k0=0, bks=mb):
            o = bks.take()
            pe.wait(o.after)
            groups = [(o.f, xs)]
            oc = None
            if ctx is not None:
                oc = bks.take()
                pe.wait(oc.after)
                groups.append((oc.f[:, 0:256], ctx))
            tok = yield from linear(name, m, range(k0, k0 + len(xs)), groups, step)
            return o, oc, tok

        def wide(items, pairs, ctx=None, late=None, feed=()):
            feed = iter(feed)
            for _ in range(3):
                next(feed, None)
            outs = []
            for name, m in items:
                o = mb.take()
                pe.wait(o.after)
                oc = None
                if ctx is not None:
                    oc = mb.take()
                    pe.wait(oc.after)
                outs.append([o, oc, None])
            n = 8
            for k in range(n):
                next(feed, None)
                for i, (name, m) in enumerate(items):
                    b, hi, lo = w_next((name, m, k))
                    H_, L_, th = pairs[k]
                    for o, src in ((outs[i][0].f, (H_.r, L_.r, th)), (ctx and outs[i][1].f[:, 0:256], ctx and ctx[k])):
                        if src is None:
                            continue
                        xh, xl, need = src
                        mmq(o, hi, xh, k == 0, False, need)
                        mmq(o, hi, xl, False, False)
                        tok = mm(o, lo, xh, False, k == n - 1)
                    outs[i][2] = done[b] = tok
                    yield
            if late is not None:
                late()
            return outs

        hx = xk(H)
        hcx = [(h.r[:, 0:256], h.r[:, 256:512], s) for h, s in HC]

        def copy_act(dst, src, *need, **kw):
            return act.do(lambda e: e.activation(dst, src, ACT.Copy, **kw), *need)

        def to_tokens(src, offs, width, bks, *need):
            b = bks.take()
            pe.wait(b.after, *need)
            for j, o in enumerate(offs):
                tok = pe.do(lambda e, j=j, o=o: e.transpose(b.f[:, j * 128:(j + 1) * 128], src[:, o:o + 128], ident))
            p = pages.take()
            w = 128 * len(offs)
            c = copy_act(p.f[:, 0:w], b.f[:, 0:w], tok, p.after)
            bks.give(b, c)
            return p, c, tok

        def main_gla():
            first = yield from wide([("w_lr", 0), ("wk_g", 0)], H, hcx)
            o, oc, t = first[0]
            z = pages.take()
            zc = pages.take()
            c1 = copy_act(z.f[0:32, :], o.f[0:32, :], t, z.after)
            c2 = copy_act(zc.f[0:32, 0:256], oc.f[0:32, 0:256], t, zc.after)
            mb.give(o, c1)
            mb.give(oc, c2)
            R["z"] = (z, zc, [c1, c2])
            for m in range(2):
                o, oc, t = first[1] if m == 0 else (yield from proj("wk_g", m, hx, hcx))
                R["kg", m] = rope_gla(o, t)
                kc = pages.take()
                c = copy_act(kc.f[:, 0:256], oc.f[:, 0:256], t, kc.after)
                mb.give(oc, c)
                R["kgc", m] = (kc, c)
                o, oc, t = yield from proj("wq_g", m, hx)
                R["qg", m] = rope_gla(o, t)
                vals = []
                for h in (2 * m, 2 * m + 1):
                    o, oc, t = yield from proj("wv_g", h, hx, hcx)
                    v, vc = pages.take(), pages.take()
                    c1 = copy_act(v.f, o.f, t, v.after)
                    c2 = copy_act(vc.f[:, 0:256], oc.f[:, 0:256], t, vc.after)
                    mb.give(o, c1)
                    mb.give(oc, c2)
                    vals.append((v, vc, c1, c2))
                    if len(vals) == 2:
                        gla_values(h - 1, *vals[0])
                yield
                gla_values(2 * m + 1, *vals[1])

        def gla_values(h, v, vc, c1, c2):
            V, tv, r1 = to_tokens(v.f, [0, 128, 256, 384], 512, mb, c1)
            VC, tvc, r2 = to_tokens(vc.f, [0, 128], 256, mb, c2)
            pages.give(v, r1)
            pages.give(vc, r2)
            R["vg", h] = (V, VC, [tv, tvc])

        def rope_gla(o, t):
            p, q = pages.take(), pages.take()
            d1 = dve.do(lambda e: e.tensor_tensor(p.f, o.f, gcos, ALU.mult), t, p.after, t_tab)
            dve.wait(q.after)
            for a_ in range(4):
                s, d = 32 * (a_ ^ 1), 32 * a_
                d2 = dve.do(lambda e, s=s, d=d: e.tensor_tensor(q.f[d:d + 32, :], o.f[s:s + 32, :],
                                                                gsin[s:s + 32, :], ALU.mult))
            d3 = dve.do(lambda e: e.tensor_tensor(p.f, p.f, q.f, ALU.add), d1, d2)
            mb.give(o, d2)
            pages.give(q, d3)
            return (p, d3)

        def side_gla():
            while "z" not in R:
                yield
            z, zc, tz = R["z"]
            for m in range(2):
                while ("kg", m) not in R:
                    yield
                dirs = []
                for dr in range(2):
                    b1, b2 = sbk.take(), sbk.take()
                    lh = wal[:, dr, 128 * m:128 * m + 128]
                    mmq(b1.f, lh, z.f[0:32, :], True, True, tz, b1.after, t_wal)
                    t = mm(b2.f[:, 0:256], lh, zc.f[0:32, 0:256], True, True, b2.after)
                    la, lac = pages.take(), pages.take()
                    bcol = col("b_alpha", 2 * dr + m)
                    d1 = dve.do(lambda e, la=la, b1=b1, bcol=bcol: e.tensor_scalar(
                        la.f, b1.f, bcol, -20.0, ALU.add, ALU.max), t, la.after)
                    d2 = dve.do(lambda e, lac=lac, b2=b2, bcol=bcol: e.tensor_scalar(
                        lac.f[:, 0:256], b2.f[:, 0:256], bcol, -20.0, ALU.add, ALU.max), lac.after)
                    sbk.give(b1, d1)
                    sbk.give(b2, d2)
                    e1 = act.do(lambda e, la=la: e.activation(la.f, la.f, ACT.Exp, scale=-1.0), d1)
                    e2 = act.do(lambda e, lac=lac: e.activation(lac.f[:, 0:256], lac.f[:, 0:256], ACT.Exp,
                                                                scale=-1.0), d2)
                    dirs.append([la, lac, e1, e2])
                yield
                for dr in range(2):
                    la, lac, e1, e2 = dirs[dr]
                    l1 = act.do(lambda e, la=la: e.activation(la.f, la.f, ACT.Ln, bias=col("one")), e1)
                    l2 = act.do(lambda e, lac=lac: e.activation(lac.f[:, 0:256], lac.f[:, 0:256], ACT.Ln,
                                                                bias=col("one")), e2)
                    d1 = dve.do(lambda e, la=la: e.tensor_scalar(la.f, la.f, -1.0 / 16, -1.0, ALU.mult, ALU.max),
                                l1)
                    d2 = dve.do(lambda e, lac=lac: e.tensor_scalar(lac.f[:, 0:256], lac.f[:, 0:256], -1.0 / 16,
                                                                   -1.0, ALU.mult, ALU.max), l2)
                    P, PC = pages.take(), pages.take()
                    d3 = dve.do(lambda e, la=la, P=P: e.tensor_tensor_scan(P.f, smask[:, 0:512], la.f, 0.0,
                                                                           ALU.mult, ALU.add), d1, P.after, t_tab)
                    d4 = dve.do(lambda e, lac=lac, PC=PC: e.tensor_tensor_scan(
                        PC.f[:, 0:256], smask[:, 512:768], lac.f[:, 0:256], 0.0, ALU.mult, ALU.add), d2, PC.after)
                    dirs[dr] = [la, lac, P, PC, d3, d4]
                yield
                k, tk = R["kg", m]
                q, tq = R["qg", m] if ("qg", m) in R else (None, None)
                while q is None:
                    yield
                    if ("qg", m) in R:
                        q, tq = R["qg", m]
                kc, tkc = R["kgc", m]
                work = []
                for dr in range(2):
                    la, lac, P, PC, d3, d4 = dirs[dr]
                    v3 = P.f.rearrange("p (c t) -> p c t", t=64)
                    o8 = 8 * (2 * m + dr)
                    dec = smal[:, o8:o8 + 8]
                    te = act.do(lambda e, dec=dec, v3=v3: e.activation(dec, v3[:, :, 63], ACT.Exp), d3)
                    if dr == 0:
                        aw = act.do(lambda e, lac=lac, PC=PC: e.activation(
                            lac.f[:, 0:256], PC.f[:, 0:256], ACT.Exp, scale=-1.0, bias=PC.f[:, 255:256]), d4)
                        B, tB = P, d3
                        pages.give(la, d3)
                    else:
                        x1 = dve.do(lambda e, la=la, P=P: e.tensor_tensor(la.f, la.f, P.f, ALU.subtract), d3)
                        tot = v3[:, :, 63:64].broadcast_to([128, 8, 64])
                        tB = dve.do(lambda e, la=la, tot=tot: e.tensor_tensor(
                            la.f.rearrange("p (c t) -> p c t", t=64), la.f.rearrange("p (c t) -> p c t", t=64),
                            tot, ALU.add), x1)
                        x2 = dve.do(lambda e, lac=lac, PC=PC: e.tensor_tensor(
                            lac.f[:, 0:256], PC.f[:, 0:256], lac.f[:, 0:256], ALU.subtract), d4)
                        aw = act.do(lambda e, lac=lac: e.activation(lac.f[:, 0:256], lac.f[:, 0:256], ACT.Exp), x2)
                        pages.give(P, tB, te)
                        B = la
                    E1 = pages.take()
                    a1 = act.do(lambda e, E1=E1, B=B: e.activation(E1.f, B.f, ACT.Exp), tB, E1.after)
                    a2 = act.do(lambda e, B=B: e.activation(B.f, B.f, ACT.Exp, scale=-1.0), a1, te)
                    qd = dve.do(lambda e, E1=E1: e.scalar_tensor_tensor(E1.f, q.f, 0.125, E1.f, ALU.mult,
                                                                        ALU.mult), a1, tq)
                    ki = dve.do(lambda e, B=B: e.tensor_tensor(B.f, k.f, B.f, ALU.mult), a2, tk)
                    KE = pages.take()
                    ke = dve.do(lambda e, KE=KE, B=B, dec=dec: e.tensor_tensor(
                        KE.f.rearrange("p (c t) -> p c t", t=64), B.f.rearrange("p (c t) -> p c t", t=64),
                        dec.unsqueeze(2).broadcast_to([128, 8, 64]), ALU.mult), ki, te, KE.after)
                    kw = dve.do(lambda e, lac=lac: e.tensor_tensor(lac.f[:, 0:256], kc.f[:, 0:256],
                                                                   lac.f[:, 0:256], ALU.mult), aw, tkc)
                    pages.give(PC, aw, x2 if dr else aw)
                    work.append((E1, qd, B, ki, KE, ke, lac, kw, dec, te))
                    yield from pause(3)
                pages.give(k, dve.now())
                pages.give(q, dve.now())
                pages.give(kc, dve.now())
                while ("vg", 2 * m + 1) not in R:
                    yield
                states = []
                for dr in range(2):
                    E1, qd, B, ki, KE, ke, lac, kw, dec, te = work[dr]
                    yield from pause(0 if dr else 3)
                    KT, tkt, r1 = to_tokens(KE.f, [0, 128, 256, 384], 512, sbk, ke)
                    pages.give(KE, r1)
                    WT, twt, r2 = to_tokens(lac.f, [0, 128], 256, sbk, kw)
                    pages.give(lac, r2)
                    yield
                    S = [pages.take(), pages.take()]

                    def sview(c, S=S):
                        return S[c // 4].f[:, 128 * (c % 4):128 * (c % 4) + 128]

                    b0 = sbk.take()
                    for hp in range(2):
                        V, VC, tv = R["vg", 2 * m + hp]
                        for j in range(2):
                            t = mm(b0.f[64 * hp:64 * hp + 64, 0:128], WT.f[:, 128 * j + 64 * hp:128 * j + 64 * hp + 64],
                                   VC.f[:, 128 * j:128 * j + 128], j == 0, j == 1, twt, tv, b0.after)
                    pages.give(WT, t)
                    c0 = 7 if dr else 0
                    s_t = dve.do(lambda e, c0=c0, sview=sview, b0=b0: e.tensor_copy(sview(c0), b0.f[:, 0:128]), t,
                                 S[0].after, S[1].after)
                    sbk.give(b0, s_t)
                    yield
                    ub = [sbk.take(), sbk.take()]
                    for par in range(2):
                        pe.wait(ub[par].after)
                        for i in range(4):
                            for hp in range(2):
                                V, _, tv = R["vg", 2 * m + hp]
                                l = KT.f[64 * par:64 * par + 64, 128 * i + 64 * hp:128 * i + 64 * hp + 64]
                                r = V.f[64 * par:64 * par + 64, 128 * i:128 * i + 128]
                                t = mm(ub[par].f[64 * hp:64 * hp + 64, 128 * i:128 * i + 128], l, r, True, True,
                                       tkt, tv)
                    pages.give(KT, t)
                    dve.wait(t)
                    for i in range(7):
                        c = 7 - i if dr else i
                        n = c - 1 if dr else c + 1
                        u = ub[c % 2].f[:, 128 * (c // 2):128 * (c // 2) + 128]
                        s_t = dve.do(lambda e, c=c, n=n, u=u, dec=dec, sview=sview: e.scalar_tensor_tensor(
                            sview(n), sview(c), dec[:, c:c + 1], u, ALU.mult, ALU.add), s_t)
                    sbk.give(ub[0], s_t)
                    sbk.give(ub[1], s_t)
                    states.append((S, sview, s_t))
                    yield
                for hp in range(2):
                    rows = slice(64 * hp, 64 * hp + 64)
                    V, VC, tv = R["vg", 2 * m + hp]
                    atts = []
                    for dr in range(2):
                        E1, qd, B, ki, *_ = work[dr]
                        ab = sbk.take()
                        pe.wait(ab.after, qd, ki)
                        for j in range(4):
                            sl = slice(128 * j, 128 * j + 128)
                            t = mm(ab.f[:, sl], B.f[rows, sl], E1.f[rows, sl], True, True)
                        am = pages.take()
                        msk = (maskF, maskB)[dr].unsqueeze(1).broadcast_to([128, 4, 128])
                        d = dve.do(lambda e, am=am, ab=ab, msk=msk: e.tensor_tensor(
                            am.f.rearrange("p (j n) -> p j n", j=4), ab.f.rearrange("p (j n) -> p j n", j=4), msk,
                            ALU.mult), t, am.after)
                        sbk.give(ab, d)
                        atts.append((am, d))
                    yield
                    ob = sbk.take()
                    pe.wait(ob.after, tv)
                    for dr in range(2):
                        am, d = atts[dr]
                        for j in range(4):
                            sl = slice(128 * j, 128 * j + 128)
                            t = mm(ob.f[:, sl], V.f[:, sl], am.f[:, sl], dr == 0 and j == 0, False, d, skip=True)
                        pages.give(am, t)
                    for dr in range(2):
                        E1 = work[dr][0]
                        S, sview, s_t = states[dr]
                        for c in range(8):
                            t = mm(ob.f[:, 64 * c:64 * c + 64], sview(c)[rows, :], E1.f[rows, 64 * c:64 * c + 64],
                                   False, dr == 1 and c == 7, s_t, skip=True)
                    og = pages.take()
                    c = copy_act(og.f, ob.f, t, og.after)
                    sbk.give(ob, c)
                    pages.give(V, t)
                    pages.give(VC, t)
                    R["og_raw", 2 * m + hp] = (og, c)
                    yield
                for dr in range(2):
                    pages.give(work[dr][0], t)
                    pages.give(work[dr][2], t)
                    pages.give(states[dr][0][0], t)
                    pages.give(states[dr][0][1], t)
            pages.give(z, pe.now())
            pages.give(zc, pe.now())
            sqs = {}
            for i in range(6):
                if i < 4:
                    sqs[i] = Squares()
                    sqs[i].add(R["og_raw", i][0].f, R["og_raw", i][1])
                    yield from pause(2)
                if 1 <= i < 5:
                    sqs[i - 1] = yield from sqs[i - 1].rstd_steps(128, ones, sbk)
                    yield
                if i >= 2:
                    h = i - 2
                    while ("og", h) not in R:
                        yield
                    o, to = R["og_raw", h]
                    r, rt = sqs.pop(h)
                    d = dve.do(lambda e, o=o, r=r: e.scalar_tensor_tensor(o.f, o.f, col("gla_norm_g"), r.f, ALU.mult,
                                                                         ALU.mult), rt, to)
                    g, tg = R["og", h]
                    d2 = dve.do(lambda e, o=o, g=g: e.scalar_tensor_tensor(o.f, o.f, 0.5, g.f, ALU.mult, ALU.mult),
                                d, tg)
                    pages.give(r, d)
                    pages.give(g, d2)
                    R["o_gla", h] = split_pages(o, d2, lane=pool)
                    yield

        def na_raw(o, t, width, tag):
            raw = pages.take()
            c = copy_act(raw.f[:, 0:width], o.f[:, 0:width], t, raw.after)
            mb.give(o, c)
            R["raw", tag] = (raw, c)

        def side_na_norm():
            dve.wait(t_gq)
            for m in range(4):
                for tag, g, width in ((("kn", m), col("na_k_g"), 512), (("knc", m), col("na_k_g"), 256),
                                      (("qn", m), gq, 512)):
                    while ("raw", tag) not in R:
                        yield
                    raw, c = R.pop(("raw", tag))
                    sq = Squares(width)
                    sq.add(raw.f[:, 0:width], c)
                    yield from pause(2)
                    r, rt = yield from sq.rstd_steps(64, bones, sbk)
                    yield
                    q = pages.take()
                    if width == 256:
                        d = dve.do(lambda e, q=q, raw=raw, g=g, r=r: e.scalar_tensor_tensor(
                            q.f[:, 0:256], raw.f[:, 0:256], g, r.f[:, 0:256], ALU.mult, ALU.mult), rt, q.after)
                    else:
                        d = dve.do(lambda e, q=q, raw=raw, g=g, r=r: e.scalar_tensor_tensor(
                            perm2(q.f), rc3(raw.f), g, rc3(r.f), ALU.mult, ALU.mult), rt, q.after)
                    pages.give(raw, d)
                    pages.give(r, d)
                    R[tag] = (q, d)
                    yield

        def rc3(ap):
            return ap.rearrange("p (r c) -> p r c", c=64)

        def perm2(ap):
            return ap.rearrange("p (c r) -> p r c", r=8)

        gq = smal[:, 64:65]
        t_gq = dve.do(lambda e: e.tensor_scalar(gq, col("na_q_g"), 0.125, None, ALU.mult), t_prm)

        def main_na():
            for m in range(4):
                yield from room(10)
                o, oc, t = yield from proj("wk_na", m, hx, hcx)
                na_raw(o, t, 512, ("kn", m))
                na_raw(oc, t, 256, ("knc", m))
                if m:
                    na_values(m - 1, *vals)
                o, oc, t = yield from proj("wv_na", m, hx, hcx)
                v, vc = pages.take(), pages.take()
                c1 = copy_act(perm2(v.f), rc3(o.f), t, v.after)
                c2 = copy_act(vc.f[:, 0:256], oc.f[:, 0:256], t, vc.after)
                mb.give(o, c1)
                mb.give(oc, c2)
                vals = (v, vc, c1, c2)
                o, oc, t = yield from proj("wq_na", m, hx)
                na_raw(o, t, 512, ("qn", m))
            yield
            yield
            na_values(3, *vals)

        def na_values(m, v, vc, c1, c2):
            V, tv, r0 = to_tokens(v.f, [0, 128, 256, 384], 512, mb, c1)
            VS, ts, r1 = to_tokens(v.f, [64, 192, 320], 384, mb, c1)
            VC, tc, r2 = to_tokens(vc.f, [0, 128], 256, mb, c2)
            pages.give(v, r1)
            pages.give(vc, r2)
            R["vn", m] = (V, VS, VC, [tv, ts, tc])

        def attention(jobs, scores, values, finish, ready, adjust=None):
            S, P_, D, V_ = {}, {}, {}, {}
            n = len(jobs)

            def cols(i):
                o = 80 + 4 * (i % 8)
                return [smal[:, o + x:o + x + 1] for x in range(3)]

            for i in range(n + 3):
                if i < n:
                    while not ready(jobs[i]):
                        yield
                    b = sbk.take()
                    S[i] = (b, scores(jobs[i], b))
                if 1 <= i <= n:
                    P, x = P_.pop(i - 1)
                    nm, sm, rc_ = cols(i - 1)
                    d = dve.do(lambda e, sm=sm, rc_=rc_: e.reciprocal(rc_, sm), x)
                    D[i - 1] = (P, dve.do(lambda e, P=P, rc_=rc_: e.tensor_scalar(P.f, P.f, rc_, None, ALU.mult), d))
                yield
                if i < n:
                    b, t = S.pop(i)
                    nm, sm, rc_ = cols(i)
                    if adjust is not None:
                        t = adjust(jobs[i], b, t)
                    d = dve.do(lambda e, nm=nm, b=b: e.tensor_reduce(nm, b.f, AX, ALU.max, negate=True), t)
                    P = pages.take()
                    x = act.do(lambda e, P=P, b=b, nm=nm, sm=sm: e.activation(P.f, b.f, ACT.Exp, bias=nm,
                                                                             accum_out=sm), d, P.after)
                    sbk.give(b, x)
                    P_[i] = (P, x)
                if 2 <= i < n + 2:
                    P, d = D.pop(i - 2)
                    PT, tp, r = to_tokens(P.f, [0, 128, 256, 384], 512, sbk, d)
                    pages.give(P, r)
                    V_[i - 2] = (PT, tp)
                yield
                if i >= 3:
                    PT, tp = V_.pop(i - 3)
                    t = values(jobs[i - 3], PT, tp)
                    pages.give(PT, t)
                    finish(jobs[i - 3], t)
                yield

        bias = {}

        def bias_load(h, hf):
            if h < 8 and (h, hf) not in bias:
                p = pages.take()
                bias[h, hf] = (p, load(p.f.rearrange("p (q k) -> p q k", q=2), a["bias"][2 * h + hf], p.after))

        def side_na():
            cur = {}

            def scores(job, b):
                h, qt = job
                m, hp = h // 2, h % 2
                if qt % 2 == 0:
                    nh, nf = (h, 1) if qt == 0 else (h + 1, 0)
                    bias_load(nh, nf)
                q, tq = R["qn", m]
                k, tk = R["kn", m]
                kc, tkc = R["knc", m]
                rows = slice(64 * hp, 64 * hp + 64)
                k0 = NA_K0[qt]
                ql = q.f[rows, 128 * qt:128 * qt + 128]
                pe.wait(b.after, tq, tk, tkc)
                mmq(b.f[:, 0:256], ql, k.f[rows, k0:k0 + 256], True, True)
                return mm(b.f[:, 256:512], ql, kc.f[rows, 0:256], True, True)

            def adjust(job, b, t):
                h, qt = job
                p, tb = bias[h, qt // 2]
                d = dve.do(lambda e: e.tensor_tensor(b.f[:, 0:256], b.f[:, 0:256],
                                                     p.f[:, 256 * (qt % 2):256 * (qt % 2) + 256], ALU.add), t, tb)
                if qt % 2 == 1:
                    pages.give(p, d)
                return d

            def values(job, PT, tp):
                h, qt = job
                m, hp = h // 2, h % 2
                if m not in cur:
                    cur[m] = sbk.take()
                    pe.wait(cur[m].after)
                V, VS, VC, tv = R["vn", m]
                f = slice(64 * hp, 64 * hp + 64)

                def vt(page, j):
                    return page.f[:, 128 * j + 64 * hp:128 * j + 64 * hp + 64]

                loc = {0: (V, 0), 1: (VS, 0), 2: (VS, 1), 3: (V, 2)}[qt]
                ls = [vt(loc[0], loc[1]), vt(loc[0], loc[1] + 1), vt(VC, 0), vt(VC, 1)]
                for j in range(4):
                    t = mm(cur[m].f[f, 128 * qt:128 * qt + 128], ls[j], PT.f[:, 128 * j:128 * j + 128], j == 0,
                           j == 3, tp, tv)
                return t

            def finish(job, t):
                h, qt = job
                m = h // 2
                if h % 2 == 1 and qt == 3:
                    o = pages.take()
                    b = cur.pop(m)
                    c = act.do(lambda e: e.activation(rc3(o.f), perm2(b.f), ACT.Copy), t, o.after)
                    sbk.give(b, c)
                    R["o_na", m] = split_pages(o, c, lane=pool)
                    for key in (("qn", m), ("kn", m), ("knc", m)):
                        pages.give(R[key][0], pe.now())
                    for p in R["vn", m][0:3]:
                        pages.give(p, pe.now())

            jobs = [(h, qt) for h in range(8) for qt in range(4)]
            yield from attention(jobs, scores, values, finish, lambda job: ("qn", job[0] // 2) in R and ("vn", job[0] // 2) in R,
                                 adjust)

        def tanh_gate(o, t, bks):
            g = pages.take()
            c = act.do(lambda e: e.activation(g.f, o.f, ACT.Tanh, scale=0.5), t, g.after)
            bks.give(o, c)
            return g, c

        def main_og():
            bias_load(0, 0)
            bias_load(0, 1)
            for h in range(4):
                o, _, t = yield from proj("w_og", h, hx)
                g = pages.take()
                c = act.do(lambda e, g=g, o=o: e.activation(g.f, o.f, ACT.Tanh, scale=0.5), t, g.after)
                d = dve.do(lambda e, g=g, o=o: e.scalar_tensor_tensor(g.f, g.f, 1.0, o.f, ALU.add, ALU.mult), c)
                mb.give(o, d)
                R["og", h] = (g, d)

        def side_mod():
            while ("vg", 0) not in R:
                yield
            nxt = [mod_load(32), mod_load(33)]
            for c in range(8):
                acc = pages.take()
                for k in range(8):
                    p, land = nxt.pop(0)
                    i = 8 * c + k
                    w = csil[:, k, 0:1]
                    if k == 0:
                        d = dve.do(lambda e, p=p, w=w, acc=acc: e.tensor_scalar(acc.f, p.f, w, None, ALU.mult), land,
                                   acc.after, t_cs)
                    else:
                        d = dve.do(lambda e, p=p, w=w, acc=acc: e.scalar_tensor_tensor(acc.f, p.f, w, acc.f, ALU.mult,
                                                                                      ALU.add), land, d)
                    pages.give(p, d)
                    if i + 2 < 64:
                        nxt.append(mod_load(34 + i))
                    yield
                b = sbk.take()
                for j in range(4):
                    t = mm(b.f[:, j:j + 1], acc.f[:, 128 * j:128 * j + 128], ones[:, 0:1], True, True, d, b.after)
                pages.give(acc, t)
                o = modr[:, 4 * c:4 * c + 4]
                d = dve.do(lambda e, b=b, o=o, c=c: e.tensor_tensor(o, b.f[:, 0:4], col("b_mod", 16 + 4 * c, 4),
                                                                   ALU.add), t)
                sbk.give(b, d)
                yield
            d = dve.do(lambda e: e.scalar_tensor_tensor(A2[:, :], modr[:, 16:24], 1.0, col("norm2_g", 0, 8),
                                                        ALU.add, ALU.mult), d)
            d = dve.do(lambda e: e.tensor_scalar(modr[:, 0:8], modr[:, 0:8], 0.5, None, ALU.mult), d)
            R["mod"] = d

        def main_gates1():
            for m in range(8):
                for nm in ("w_ma", "w_mb"):
                    o, _, t = yield from proj(nm, m, hx)
                    R[nm, m] = tanh_gate(o, t, mb)

        def chain(*gens):
            for g in gens:
                yield from g

        def room(n):
            for _ in range(1000):
                if len(pages.free) >= n:
                    return
                yield
            raise ValueError("no room")

        def ready(*keys):
            for _ in range(1000):
                if all(k in R for k in keys):
                    return
                yield
            raise ValueError(f"never ready: {keys}")

        def branch(merged, gate, gm, w, xs, gates, final=None):
            for m in range(8):
                if m not in gates:
                    yield from room(3)
                    o, _, t = yield from proj(gate, gm + m, hcur[0])
                    g, tg = hcur[1](o, t)
                else:
                    g, tg = gates[m]
                o, _, t = yield from proj(w, m, xs)
                d = dve.do(lambda e, g=g, o=o: e.scalar_tensor_tensor(g.f, g.f, 1.0, o.f, ALU.add, ALU.mult), tg, t)
                mb.give(o, d)
                if m not in merged:
                    merged[m] = (g, d)
                else:
                    acc, tok = merged[m]
                    tok = dve.do(lambda e, g=g, acc=acc: e.tensor_tensor(acc.f, acc.f, g.f, ALU.add), d, tok)
                    pages.give(g, tok)
                    merged[m] = (acc, tok)
                if final is not None:
                    final.append(split_pages(*merged[m]))

        def free_context():
            for h, _ in HC:
                pages.give(h, pe.now())
            yield

        mains1 = chain(main_gla(), main_og(), main_na(), free_context(), main_gates1())
        weave(mains1, [chain(side_gla(), side_na()), side_na_norm(), side_mod()], 1)
        give_pairs(H, pe.now())

        def run(gen):
            for _ in gen:
                pass

        def main_merge1():
            merged = {}
            yield from ready("mod")
            for key, w in (("o_gla", "w_branch_gla"), ("o_na", "w_branch_na")):
                pairs = [R.pop((key, m)) for m in range(4)]
                gates = {m: R.pop(({"o_na": "w_ma", "o_gla": "w_mb"}[key], m)) for m in range(8)}
                yield from branch(merged, None, 0, w, xk(pairs), gates, M if key == "o_na" else None)
                give_pairs(pairs, pe.now())

        M = []
        run(main_merge1())
        sq = Squares()

        def main_out1():
            xm = xk(M)
            for m in range(8):
                o, _, t = yield from proj("w_out", m, xm)
                d = dve.do(lambda e, m=m, o=o: e.scalar_tensor_tensor(X[m].f, o.f, modr[:, m:m + 1], X[m].f, ALU.mult,
                                                                      ALU.add), t, X[m].rd, R["mod"])
                mb.give(o, d)
                X[m].w, X[m].rd = [d], []
                sq.add(X[m].f, d, last=m == 7)

        run(main_out1())
        give_pairs(M, pe.now())

        H2 = []

        def norm_x2():
            r, rt = sq.rstd(1024, ones, sbk, warm=True)
            last = []
            for k in range(9):
                if k < 8:
                    t, Hk, Lk = pages.take(), pages.take(), pages.take()
                    d = dve.do(lambda e, k=k, t=t: e.scalar_tensor_tensor(t.f, X[k].f, A2[:, k:k + 1], r.f, ALU.mult,
                                                                         ALU.mult), t.after, rt)
                    X[k].rd = [d]
                    d2 = dve.do(lambda e, k=k, t=t: e.tensor_scalar(t.f, t.f, modr[:, 8 + k:9 + k], None, ALU.add), d)
                    h = act.do(lambda e, Hk=Hk, t=t: e.activation(Hk.r, t.f, ACT.Copy), d2, Hk.after)
                    last.append((t, Hk, Lk, h))
                if k > 0:
                    t_, H_, L_, h_ = last.pop(0)
                    lo = dve.do(lambda e, t_=t_, H_=H_, L_=L_: e.tensor_tensor(L_.r, t_.f, bc(H_.r), ALU.subtract),
                                h_, L_.after)
                    pages.give(t_, lo)
                    H2.append((H_, L_, [h_, lo]))
                if k < 7:
                    yield
            pages.give(r, d)

        def times(page, src, r, *need):
            return dve.do(lambda e: e.tensor_tensor(page.f, src, r.f, ALU.mult), page.after, *need)

        def main_ffn(sfx, Hf, on_out, feed, rs=None):
            for hf in range(2):
                pairs = []
                for j in range(FH * hf, FH * hf + FH):
                    bks = mb
                    if j == 0:
                        first = yield from wide([(n + sfx, i) for i in range(2) for n in ("ffn_gate", "ffn_up")],
                                                Hf, None, rs and (lambda: input_rms(rs)), feed)
                        xh = xk(Hf)
                    if j < 2:
                        (og, _, tg), (ou, _, tu) = first[2 * j:2 * j + 2]
                    else:
                        bks = sbk if rs is not None and j == 2 else mb
                        og, _, tg = yield from proj("ffn_gate" + sfx, j, xh, bks=bks)
                        ou, _, tu = yield from proj("ffn_up" + sfx, j, xh, bks=bks)
                    s = pages.take()
                    if rs is None:
                        c = act.do(lambda e, s=s, og=og: e.activation(s.f, og.f, ACT.Silu), tg, s.after)
                        bks.give(og, c)
                    else:
                        d = times(s, og.f, rs.r, tg, rs.rt)
                        bks.give(og, d)
                        c = act.do(lambda e, s=s: e.activation(s.f, s.f, ACT.Silu), d)
                    d = dve.do(lambda e, s=s, ou=ou: e.tensor_tensor(s.f, s.f, ou.f, ALU.mult), c, tu)
                    bks.give(ou, d)
                    if rs is not None:
                        d = dve.do(lambda e, s=s: e.tensor_tensor(s.f, s.f, rs.r.f, ALU.mult), d)
                    pairs.append(split_pages(s, d))
                if hf == 1:
                    give_pairs(Hf, pe.now())
                    if rs is not None:
                        pages.give(rs.r, d)
                for m in range(8):
                    o, _, t = yield from proj("ffn_down" + sfx, m, xk(pairs), None, 2, FH * hf)
                    on_out(hf, m, o, t)
                give_pairs(pairs, pe.now())


        def out_x(hf, m, o, t):
            d = dve.do(lambda e: e.scalar_tensor_tensor(X[m].f, o.f, modr[:, 24 + m:25 + m], X[m].f, ALU.mult,
                                                        ALU.add), t, X[m].rd, X[m].w)
            mb.give(o, d)
            X[m].w, X[m].rd = [d], []
            if hf == 1:
                input_hi(v0, m)

        class Input:

            def __init__(self, gain):
                self.gain, self.sq, self.pairs, self.hi, self.r, self.rt = gain, Squares(), [], [], None, None

        def input_hi(v, m):
            H_, L_, q = pages.take(), pages.take(), pages.take()
            h = act.do(lambda e: e.activation(H_.r, X[m].f, ACT.Copy, scale=col(v.gain, m)), X[m].w, H_.after)
            s = act.do(lambda e: e.activation(q.f, X[m].f, ACT.Square), q.after)
            v.hi.append((m, H_, L_, h, q, s))
            if m > 0:
                input_lo(v, *v.hi.pop(0))
            if m == 7:
                input_lo(v, *v.hi.pop(0))

        def input_lo(v, m, H_, L_, h, q, s):
            lo = dve.do(lambda e: e.scalar_tensor_tensor(L_.r, X[m].f, col(v.gain, m), bc(H_.r), ALU.mult,
                                                         ALU.subtract), h, L_.after)
            X[m].rd = [h, lo, s]
            v.pairs.append((H_, L_, [h, lo]))
            if m == 0:
                v.sq.acc, v.sq.tok = q, s
            else:
                acc = v.sq.acc
                adder = dve if m in (2, 5, 7) else pool
                v.sq.tok = adder.do(lambda e: e.tensor_tensor(acc.f, acc.f, q.f, ALU.add), s, v.sq.tok)
                pages.give(q, v.sq.tok)

        def input_rms(v):
            v.r, v.rt = v.sq.rstd(1024, ones, sbk)

        lg = smal[:, 128:144]

        def side_tables():
            pi = pages.take()
            tp = load(pi.f.bitcast(I32), a["pos"], pi.after)
            R["tabA"] = load(tabA[:, :], a["tabA"], dve.now())
            yield from pause(6)
            pf = pages.take()
            d0 = dve.do(lambda e: e.tensor_copy(pf.f, pi.f.bitcast(I32)), tp, pf.after)
            pages.give(pi, d0)
            yield
            for key, inv, sgn in (("m", "inv_m", "sgn_m"), ("r", "inv_r", "sgn_r")):
                an, kk = pages.take(), pages.take()
                d = dve.do(lambda e, an=an, inv=inv: e.tensor_scalar(an.f, pf.f, col(inv), None, ALU.mult), d0,
                           an.after)
                d = dve.do(lambda e, an=an, kk=kk: e.tensor_scalar(kk.f, an.f, 1 / (2 * np.pi), ROUND, ALU.mult,
                                                                   ALU.add), d, kk.after)
                d = dve.do(lambda e, kk=kk: e.tensor_scalar(kk.f, kk.f, -ROUND, None, ALU.add), d)
                for cc in (C1, C2, C3):
                    d = dve.do(lambda e, an=an, kk=kk, cc=cc: e.scalar_tensor_tensor(an.f, kk.f, -cc, an.f, ALU.mult,
                                                                                    ALU.add), d)
                d = dve.do(lambda e, an=an: e.tensor_scalar(an.f, an.f, -PI_IN, PI_IN, ALU.max, ALU.min), d)
                s1 = act.do(lambda e, an=an, kk=kk: e.activation(kk.f, an.f, ACT.Sin), d)
                d = act.do(lambda e, an=an: e.activation(an.f, an.f, ACT.Abs), s1)
                s2 = act.do(lambda e, an=an: e.activation(an.f, an.f, ACT.Sin, scale=-1.0, bias=col("halfpi")), d)
                d = dve.do(lambda e, kk=kk, sgn=sgn: e.tensor_scalar(kk.f, kk.f, col(sgn), None, ALU.mult), s1)
                R["cos", key], R["sin", key] = an, kk
                R["trig", key] = [s2, d]
                yield
            pages.give(pf, d)
            x = col("decay", 0, 16)
            s = [smal[:, 144 + 16 * i:160 + 16 * i] for i in range(2)]
            d = act.do(lambda e: e.activation(s[0], x, ACT.Abs))
            t = act.do(lambda e: e.activation(s[0], s[0], ACT.Exp, scale=-1.0), d)
            t = act.do(lambda e: e.activation(s[0], s[0], ACT.Ln, bias=col("one")), t)
            d = dve.do(lambda e: e.tensor_scalar(s[1], x, 0.0, None, ALU.min))
            R["lg"] = dve.do(lambda e: e.tensor_tensor(lg, s[1], s[0], ALU.subtract), t, d)
            yield

        v0 = Input("mix_pre0")
        weave(main_ffn("", H2, out_x, norm_x2()), [side_tables()], 4)

        MSC = float(96 ** -0.5)
        RSC = float(128 ** -0.5)

        def layer(l, rs, feed):
            L = str(l)
            Hl = rs.pairs
            xh = []
            big = {}
            qns = smal[:, 176 + 2 * l:178 + 2 * l]
            t_qn = dve.do(lambda e: e.tensor_scalar(qns, col("q_norm" + L, 0, 2), MSC, None, ALU.mult))
            cosM, sinM, trM = R["cos", "m"], R["sin", "m"], R["trig", "m"]
            cosR, sinR, trR = R["cos", "r"], R["sin", "r"], R["trig", "r"]

            def rope96(o, dst, t, *need):
                q = pages.take()
                d1 = dve.do(lambda e: e.tensor_tensor(dst.f[64:96, :], o.f[64:96, :], cosM.f[64:96, :], ALU.mult),
                            t, trM, dst.after, *need)
                d2 = dve.do(lambda e: e.tensor_tensor(q.f[64:96, :], o.f[96:128, :], sinM.f[96:128, :], ALU.mult),
                            q.after)
                d3 = dve.do(lambda e: e.tensor_tensor(dst.f[64:96, :], dst.f[64:96, :], q.f[64:96, :], ALU.add),
                            d1, d2)
                pages.give(q, d3)
                return d3

            def rope128(o, t):
                cos, sin, tr = big["rope"]
                p, q = pages.take(), pages.take()
                d1 = dve.do(lambda e: e.tensor_tensor(p.f, o.f, cos.f, ALU.mult), t, tr, p.after)
                dve.wait(q.after)
                for s, d in ((0, 64), (64, 0)):
                    d2 = dve.do(lambda e, s=s, d=d: e.tensor_tensor(q.f[d:d + 64, :], o.f[s:s + 64, :],
                                                                    sin.f[s:s + 64, :], ALU.mult))
                d3 = dve.do(lambda e: e.tensor_tensor(p.f, p.f, q.f, ALU.add), d1, d2)
                mb.give(o, d2)
                pages.give(q, d3)
                return p, d3

            def scaled(o, t, bks=mb):
                p = pages.take()
                d = times(p, o.f, rs.r, t, rs.rt)
                bks.give(o, d)
                return p, d

            def tanh_scaled(o, t, bks=mb):
                p, d = scaled(o, t, bks)
                return p, act.do(lambda e: e.activation(p.f, p.f, ACT.Tanh, scale=0.5), d)

            def main_mla():
                first = yield from wide([("w_kv" + L, 0), ("w_cq" + L, 0), ("w_cq" + L, 1), ("w_kpe" + L, 0)], Hl,
                                        None, lambda: input_rms(rs), feed)
                xh.extend(xk(Hl))
                kv, tkv = scaled(first[0][0], first[0][2])
                cq = [scaled(o, t) for o, _, t in first[1:3]]
                raw, tr = scaled(first[3][0], first[3][2])
                kp = pages.take()
                d = rope96(raw, kp, tr)
                pages.give(raw, d)
                R["kpe"] = (kp, d)
                c, s = pages.take(), pages.take()
                d = times(c, cosR.f, rs.r, trR)
                d = times(s, sinR.f, rs.r)
                big["rope"] = (c, s, d)
                R["down"] = (kv, tkv, cq)

            def side_mla():
                while "down" not in R:
                    yield
                (kv, tkv, cq), (kp, tkp) = R.pop("down"), R.pop("kpe")
                s1, s2 = Squares(), Squares()
                s1.add(kv.f, tkv)
                for p, c in cq:
                    s2.add(p.f, c)
                yield
                r, rt = yield from s1.rstd_steps(128, ones, sbk)
                yield
                d = dve.do(lambda e: e.scalar_tensor_tensor(kv.f, kv.f, col("kv_norm" + L), r.f, ALU.mult, ALU.mult),
                           rt)
                pages.give(r, d)
                xkv = [split_pages(kv, d, lane=pool)]
                r, rt = yield from s2.rstd_steps(256, ones, sbk)
                yield
                xq = []
                for m, (p, c) in enumerate(cq):
                    d = dve.do(lambda e, p=p, m=m: e.scalar_tensor_tensor(p.f, p.f, qns[:, m:m + 1], r.f, ALU.mult,
                                                                         ALU.mult), rt, t_qn)
                    xq.append(split_pages(p, d, lane=pool))
                pages.give(r, d)
                yield from pause(3)
                made = {}

                def make(j):
                    o, _, t = yield from proj("w_kn" + L, j, xk(xkv))
                    ks = []
                    for hp in range(2):
                        p = pages.take()
                        c1 = copy_act(p.f[0:64, :], o.f[64 * hp:64 * hp + 64, :], t, p.after)
                        c2 = dve.do(lambda e, p=p: e.tensor_copy(p.f[64:96, :], kp.f[64:96, :]), tkp, p.after)
                        ks.append((p, [c1, c2]))
                    mb.give(o, c1)
                    yield
                    o, _, t = yield from proj("w_v" + L, j, xk(xkv))
                    v = pages.take()
                    c = copy_act(v.f, o.f, t, v.after)
                    mb.give(o, c)
                    yield
                    qs = []
                    for hp in range(2):
                        o, _, t = yield from proj("w_uq" + L, 2 * j + hp, xk(xq))
                        p = pages.take()
                        d = rope96(o, p, t)
                        c1 = copy_act(p.f[0:64, :], o.f[0:64, :], t, p.after, d)
                        mb.give(o, c1)
                        qs.append((p, [c1, d]))
                        yield
                    V, tv, r = to_tokens(v.f, [0, 128, 256, 384], 512, mb, c)
                    pages.give(v, r)
                    made[j] = (ks, qs, V, tv)

                yield from make(0)
                cur = {}

                def scores(job, b):
                    h, qt = job
                    ks, qs, V, tv = made[h // 2]
                    (q, tq), (k, tk) = qs[h % 2], ks[h % 2]
                    return mm(b.f, q.f[0:96, 128 * qt:128 * qt + 128], k.f[0:96, :], True, True, b.after, tq, tk)

                def values(job, PT, tp):
                    h, qt = job
                    j, hp = h // 2, h % 2
                    if j not in cur:
                        cur[j] = sbk.take()
                        pe.wait(cur[j].after)
                    V, tv = made[j][2:4]
                    for i in range(4):
                        t = mm(cur[j].f[64 * hp:64 * hp + 64, 128 * qt:128 * qt + 128],
                               V.f[:, 128 * i + 64 * hp:128 * i + 64 * hp + 64], PT.f[:, 128 * i:128 * i + 128],
                               i == 0, i == 3, tp, tv)
                    return t

                def finish(job, t):
                    h, qt = job
                    j = h // 2
                    if h % 2 == 1 and qt == 3:
                        o, b = pages.take(), cur.pop(j)
                        c = copy_act(o.f, b.f, t, o.after)
                        sbk.give(b, c)
                        R["o_mla", j] = split_pages(o, c, lane=pool)
                        ks, qs, V, tv = made.pop(j)
                        for p, _ in ks + qs:
                            pages.give(p, pe.now())
                        pages.give(V, pe.now())

                def maker():
                    for j in range(1, 4):
                        yield from make(j)
                        while j in made and len(made) > 1:
                            yield
                    give_pairs(xq, pe.now())
                    give_pairs(xkv, pe.now())
                    pages.give(kp, dve.now())

                mk = maker()
                jobs = [(h, qt) for h in range(8) for qt in range(4)]
                att = attention(jobs, scores, values, finish, lambda job: job[0] // 2 in made)
                for _ in att:
                    next(mk, None)
                    yield
                for _ in mk:
                    yield

            def main_conv():
                for m in range(4):
                    bks = sbk if m == 0 else mb
                    o1, _, t1 = yield from proj("w_cg" + L, m, xh, bks=bks)
                    g, tg = tanh_scaled(o1, t1, bks)
                    o2, _, t2 = yield from proj("w_ca" + L, m, xh, bks=bks)
                    p, d = scaled(o2, t2, bks)
                    d = dve.do(lambda e, g=g, p=p: e.scalar_tensor_tensor(g.f, g.f, 1.0, p.f, ALU.add, ALU.mult),
                               tg, d)
                    pages.give(p, d)
                    R["ca", m] = (g, d)

            def taps(m):
                while ("ca", m) not in R:
                    yield
                ca, tca = R.pop(("ca", m))
                acc = pages.take()
                for n, j in enumerate([15] + [i for i in range(31) if i != 15]):
                    s = j - 15
                    lo, hi = max(0, -s), min(T, T - s)
                    w = col("w_dw" + L, 31 * m + j)
                    src, A = ca.f[:, lo + s:hi + s], acc.f[:, lo:hi]
                    if n == 0:
                        tok = dve.do(lambda e: e.tensor_scalar(A, src, w, None, ALU.mult), tca, acc.after)
                    elif m < 3:
                        tok = dve.do(lambda e: e.scalar_tensor_tensor(A, src, w, A, ALU.mult, ALU.add), tok)
                    else:
                        q = pages.take()
                        qf = q.f[:, 0:hi - lo]
                        c = act.do(lambda e: e.activation(qf, src, ACT.Copy, scale=w), q.after, tca)
                        tok = pool.do(lambda e: e.tensor_tensor(A, A, qf, ALU.add), c, tok)
                        pages.give(q, tok)
                    yield
                    if n % 3 or m == 3:
                        yield
                pages.give(ca, tok)
                tok = dve.do(lambda e: e.tensor_scalar(acc.f, acc.f, 0.5, col("b_dw" + L, m), ALU.mult, ALU.add), tok)
                R["conv", m] = (acc, tok)
                yield

            def side_conv_norm():
                yield from ready(*[("conv", m) for m in range(4)])
                acc, tok = zip(*[R.pop(("conv", m)) for m in range(4)])
                yield
                b = sbk.take()
                pe.wait(b.after)
                for m in range(4):
                    mt = mm(b.f, ones, acc[m].f, m == 0, m == 3, tok[m])
                sq = Squares()
                ds = [dve.do(lambda e, p=p: e.scalar_tensor_tensor(p.f, b.f, -1.0 / 512, p.f, ALU.mult, ALU.add), mt)
                      for p in acc]
                sbk.give(b, ds[-1])
                for p, d in zip(acc, ds):
                    sq.add(p.f, d)
                yield
                yield
                r, rt = yield from sq.rstd_steps(512, ones, sbk)
                yield
                for m in range(4):
                    d = dve.do(lambda e, m=m: e.scalar_tensor_tensor(acc[m].f, acc[m].f, col("cln_g" + L, m), r.f,
                                                                     ALU.mult, ALU.mult), rt)
                    c = act.do(lambda e, m=m: e.activation(acc[m].f, acc[m].f, ACT.Silu, bias=col("cln_b" + L, m)),
                               d)
                    R["o_conv", m] = split_pages(acc[m], c, lane=pool)
                    yield
                pages.give(r, d)

            def centre_values(h, v0_, v1_):
                s = [smal[:, 192 + 8 * (h % 2) + 4 * i:196 + 8 * (h % 2) + 4 * i] for i in range(2)]
                ds = []
                for i, (V, tv) in enumerate((v0_, v1_)):
                    ds.append(dve.do(lambda e, i=i, V=V: e.tensor_reduce(s[i], V.f.rearrange("p (j f) -> p j f", j=4),
                                                                         AX, ALU.add), tv))
                d = dve.do(lambda e: e.tensor_tensor(s[0], s[0], s[1], ALU.add), *ds)
                m = s[0].unsqueeze(2).broadcast_to([128, 4, 128])
                for i, (V, tv) in enumerate((v0_, v1_)):
                    v3 = V.f.rearrange("p (j f) -> p j f", j=4)
                    R["rv", h, i] = (V, dve.do(lambda e, v3=v3: e.scalar_tensor_tensor(v3, m, -1.0 / 256, v3,
                                                                                      ALU.mult, ALU.add), d))

            def main_ret(h):
                yield from room(17)
                vs, both_v = [], []
                for e_ in range(2):
                    o, _, t = yield from proj("w_rv" + L, 2 * h + e_, xh)
                    vs.append(scaled(o, t))
                for nm in ("rk", "rq"):
                    o, _, t = yield from proj("w_" + nm + L, h, xh)
                    R[nm, h] = rope128(o, t)
                    v, tv = vs.pop(0)
                    V, tv, r = to_tokens(v.f, [0, 128, 256, 384], 512, mb, tv)
                    pages.give(v, r)
                    both_v.append((V, tv))
                centre_values(h, *both_v)
                for e_ in range(2):
                    o, _, t = yield from proj("w_rg" + L, 2 * h + e_, xh)
                    p, ta = scaled(o, t)
                    g = pages.take()
                    c = act.do(lambda e, g=g, p=p: e.activation(g.f, p.f, ACT.Tanh, scale=0.5), ta, g.after)
                    d = dve.do(lambda e, g=g, p=p: e.scalar_tensor_tensor(g.f, g.f, 1.0, p.f, ALU.add, ALU.mult), c)
                    pages.give(p, d)
                    R["rg", h, e_] = (g, d)

            def side_ret():
                for h in range(4):
                    while ("rg", h, 1) not in R:
                        yield
                    lf, lb = (lg[:, 8 * l + 4 * x + h:8 * l + 4 * x + h + 1] for x in range(2))
                    d = dve.do(lambda e, lf=lf: e.tensor_scalar(tabD, rA1, lf, None, ALU.mult), R["tabA"], R["lg"],
                               R["Dfree"])
                    d = dve.do(lambda e, lb=lb: e.scalar_tensor_tensor(tabD, rA2, lb, tabD, ALU.mult, ALU.add), d)
                    tD = act.do(lambda e: e.activation(tabD, tabD, ACT.Exp), d)
                    yield
                    (q, tq), (k, tk) = R.pop(("rq", h)), R.pop(("rk", h))
                    ats = []
                    for j in range(4):
                        b, at = sbk.take(), pages.take()
                        t = mm(b.f, k.f[:, 128 * j:128 * j + 128], q.f, True, True, b.after, tq, tk)
                        o0 = 384 - 128 * j
                        d = dve.do(lambda e, b=b, at=at, o0=o0: e.scalar_tensor_tensor(
                            at.f, b.f, RSC, tabD[:, o0:o0 + 512], ALU.mult, ALU.mult), t, tD, at.after)
                        sbk.give(b, d)
                        ats.append((at, d))
                        if j % 2:
                            yield
                    R["Dfree"] = [d]
                    pages.give(q, t)
                    pages.give(k, t)
                    os_, ots = [], []
                    for e_ in range(2):
                        V, tv = R.pop(("rv", h, e_))
                        b = sbk.take()
                        pe.wait(b.after, tv)
                        for j, (at, d) in enumerate(ats):
                            t = mm(b.f, V.f[:, 128 * j:128 * j + 128], at.f, j == 0, j == 3, d)
                        pages.give(V, t)
                        o = pages.take()
                        c = copy_act(o.f, b.f, t, o.after)
                        sbk.give(b, c)
                        os_.append(o)
                        ots.append(c)
                        yield
                    for at, _ in ats:
                        pages.give(at, t)
                    sq = Squares()
                    for o, c in zip(os_, ots):
                        sq.add(o.f, c)
                    yield
                    yield
                    r, rt = yield from sq.rstd_steps(256, ones, sbk)
                    yield
                    yield
                    for e_ in range(2):
                        o, (g, tg) = os_[e_], R.pop(("rg", h, e_))
                        d = dve.do(lambda e, o=o, e_=e_, h=h: e.scalar_tensor_tensor(
                            o.f, o.f, col("gn_g" + L, 2 * h + e_), r.f, ALU.mult, ALU.mult), rt)
                        d2 = dve.do(lambda e, o=o, g=g: e.scalar_tensor_tensor(o.f, o.f, 0.5, g.f, ALU.mult,
                                                                               ALU.mult), d, tg)
                        pages.give(g, d2)
                        R["o_ret", 2 * h + e_] = split_pages(o, d2, lane=pool)
                    pages.give(r, d)
                    yield

            merged = {}
            hcur[:] = [xh, tanh_scaled]
            M = []

            def main_branch(i, key, n, w):
                gates = {}
                while not all((key, m) in R for m in range(n)) and len(gates) < 4 and len(pages.free) >= 8:
                    o, _, t = yield from proj("w_gate" + L, 8 * i + len(gates), xh)
                    gates[len(gates)] = tanh_scaled(o, t)
                yield from ready(*[(key, m) for m in range(n)])
                pairs = [R.pop((key, m)) for m in range(n)]
                yield from branch(merged, "w_gate" + L, 8 * i, w + L, xk(pairs), gates, M if i == 2 else None)
                give_pairs(pairs, pe.now())

            weave(chain(main_mla(), main_conv(), main_ret(0), main_ret(1), main_branch(0, "o_mla", 4, "w_mo"),
                        main_branch(1, "o_conv", 4, "w_pw"), main_ret(2), main_ret(3),
                        main_branch(2, "o_ret", 8, "w_ro")),
                  [chain(side_mla(), side_ret()), chain(taps(0), taps(1), taps(2)), taps(3), side_conv_norm()], 1)
            give_pairs(Hl, pe.now())
            pages.give(rs.r, dve.now())
            for p in big["rope"][0:2]:
                pages.give(p, dve.now())
            F = []
            sf = Squares()

            def main_out():
                for m in range(8):
                    o, _, t = yield from proj("w_out" + L, m, xk(M))
                    f = pages.take()
                    sf.add(o.f, t, 0.5, m == 7)
                    c = copy_act(f.f, o.f, t, f.after, scale=0.5)
                    mb.give(o, c)
                    F.append((f, c))

            run(main_out())
            give_pairs(M, pe.now())

            def post_norm(F, sf, g, each):
                r, rt = sf.rstd(1024, ones, mb, warm=True)
                for m, (f, c) in enumerate(F):
                    d = dve.do(lambda e, f=f, m=m: e.scalar_tensor_tensor(f.f, f.f, col(g, m), r.f, ALU.mult,
                                                                         ALU.mult), rt)
                    d = dve.do(lambda e, f=f, m=m: e.tensor_tensor(X[m].f, X[m].f, f.f, ALU.add), d, X[m].rd)
                    X[m].w, X[m].rd = [d], []
                    pages.give(f, d)
                    each(m)
                    if m == 7:
                        pages.give(r, d)
                    yield

            vf = Input("ffn_pre" + L)
            feed = post_norm(F, sf, "mix_post" + L, lambda m: input_hi(vf, m))
            F2 = []
            sf2 = Squares()

            def out_f(hf, m, o, t):
                if hf == 0:
                    f = pages.take()
                    c = copy_act(f.f, o.f, t, f.after)
                    F2.append((f, c))
                else:
                    f, c0 = F2[m]
                    c = dve.do(lambda e: e.tensor_tensor(f.f, f.f, o.f, ALU.add), t, c0)
                    F2[m] = (f, c)
                    sf2.add(f.f, c, last=m == 7)
                mb.give(o, c)

            run(main_ffn(L, vf.pairs, out_f, feed, vf))
            if l == 0:
                nxt = Input("mix_pre1")
                return nxt, post_norm(F2, sf2, "ffn_post" + L, lambda m: input_hi(nxt, m))
            run(post_norm(F2, sf2, "ffn_post" + L, lambda m: sp.dma(s_out, out[:, m, :], X[m].f, X[m].w)))

        R["Dfree"] = []
        layer(1, *layer(0, v0, ()))
        sp.quiet(lambda e: e.wait_ge(s_out, 128))

        while len(order) % 8:
            order.append(None)

        block = ctx.enter_context(nc.Block())

        @block.sync
        def _(e):
            sp.play(e)

        @block.tensor
        def _(e):
            pe.play(e)

        @block.scalar
        def _(e):
            act.play(e)

        @block.vector
        def _(e):
            dve.play(e)

        @block.gpsimd
        def _(e):
            pool.play(e)


def columns(v):
    return np.ascontiguousarray(v.reshape(-1, 128).T)


def tables():
    i = np.arange(128)
    same = (i[:, None] // 64) == (i[None, :] // 64)
    cst = np.zeros((128, 5, 128), np.float32)
    cst[:, 0] = np.eye(128)
    cst[:, 1] = 1.0
    cst[:, 2] = same
    cst[:, 3] = same & (i[:, None] <= i[None, :])
    cst[:, 4] = same & (i[:, None] >= i[None, :])
    freqs = (np.float32(10000.0) ** (-np.arange(16, dtype=np.float32) / np.float32(16))).astype(np.float32)
    t = np.arange(T)
    tabG = np.zeros((128, 1792), np.float32)
    for p in range(128):
        j, second = p % 32, (p % 64) >= 32
        pos = (t // 64 if j < 16 else t % 64).astype(np.float32)
        ang = (pos * freqs[j % 16]).astype(np.float32)
        tabG[p, 0:512] = np.cos(ang)
        tabG[p, 512:1024] = -np.sin(ang) if second else np.sin(ang)
    tabG[:, 1024:1536] = (t % 64 != 0)
    tabG[:, 1536:1792] = (np.arange(256) != 0)
    c = np.arange(896)
    diff = (c[None, :] - 384 - i[:, None]).astype(np.float32)
    tabA = np.concatenate([np.maximum(diff, 0), np.maximum(-diff, 0)], 1).astype(np.float32)
    return cst, tabG, tabA


def na_bias(rpb):
    out = np.full((8, 4, 128, 256), -1e30, np.float32)
    for qt in range(4):
        q = 128 * qt + np.arange(128)
        k = NA_K0[qt] + np.arange(256)
        qc, qr = (q // 8)[:, None], (q % 8)[:, None]
        kc, kr = (k // 8)[None, :], (k % 8)[None, :]
        st = np.clip(qc - 8, 0, 48)
        inside = (kc >= st) & (kc < st + 16)
        dc = np.clip(kc - qc, -15, 15) + 15
        got = rpb[:, kr - qr + 7, dc]
        out[:, qt] = np.where(inside[None], got, out[:, qt])
    return np.ascontiguousarray(out.reshape(16, 2, 128, 256).transpose(0, 2, 1, 3))


def weights(inp):
    w = inp["w_in"][0]
    o = np.cumsum([0, 512, 512, 512, 256, 256, 512, 512, 32, 1024, 1024])
    hp = np.concatenate([np.arange(0, 16), np.arange(32, 48), np.arange(16, 32), np.arange(48, 64)])
    gp = np.concatenate([64 * h + hp for h in range(4)])
    lr = np.zeros((1024, 128), np.float32)
    lr[:, 0:32] = w[:, o[7]:o[8]]
    m = {
        "wq_na": w[:, o[0]:o[1]], "wk_na": w[:, o[1]:o[2]], "wv_na": w[:, o[2]:o[3]],
        "wq_g": w[:, o[3]:o[4]][:, gp], "wk_g": w[:, o[4]:o[5]][:, gp], "wv_g": w[:, o[5]:o[6]],
        "w_og": w[:, o[6]:o[7]], "w_lr": lr, "w_ma": w[:, o[8]:o[9]], "w_mb": w[:, o[9]:o[10]],
        "w_branch_na": inp["w_branch_na"][0], "w_branch_gla": inp["w_branch_gla"][0], "w_out": inp["w_out"][0],
        "ffn_gate": inp["w_ffn_gate"][0], "ffn_up": inp["w_ffn_up"][0], "ffn_down": inp["w_ffn_down"][0],
    }
    o = np.cumsum([0, 256, 128, 32, 1024, 512, 512, 1024, 1024, 3072])
    swap = np.concatenate([np.arange(16, 32), np.arange(0, 16)])
    for l in range(2):
        L = str(l)
        w = inp["w_in_2"][l]
        pe_ = w[:, o[2]:o[3]]
        kpe = np.zeros((1024, 128), np.float32)
        kpe[:, 64:96], kpe[:, 96:128] = pe_, pe_[:, swap]
        uq = inp["mla_w_uq_2"][l].reshape(256, 8, 96)
        uq = np.concatenate([uq, uq[:, :, 64:][:, :, swap]], 2).reshape(256, 1024)
        ukv = inp["mla_w_ukv_2"][l].reshape(128, 8, 128)
        m.update({
            "w_cq" + L: w[:, o[0]:o[1]], "w_kv" + L: w[:, o[1]:o[2]], "w_kpe" + L: kpe,
            "w_ca" + L: w[:, o[3]:o[3] + 512], "w_cg" + L: w[:, o[3] + 512:o[4]],
            "w_rq" + L: w[:, o[4]:o[5]], "w_rk" + L: w[:, o[5]:o[6]], "w_rv" + L: w[:, o[6]:o[7]],
            "w_rg" + L: w[:, o[7]:o[8]], "w_gate" + L: w[:, o[8]:o[9]],
            "w_uq" + L: uq, "w_kn" + L: ukv[:, :, 0:64].reshape(128, 512), "w_v" + L: ukv[:, :, 64:].reshape(128, 512),
            "w_mo" + L: inp["mla_w_o_2"][l], "w_pw" + L: inp["conv_w_pw_2"][l], "w_ro" + L: inp["ret_w_o_2"][l],
            "w_out" + L: inp["w_out_2"][l], "ffn_gate" + L: inp["ffn_w_gate_2"][l],
            "ffn_up" + L: inp["ffn_w_up_2"][l], "ffn_down" + L: inp["ffn_w_down_2"][l],
        })
    return m


def stream(mats, order):
    out = np.zeros((NB, 128, 8, 128), np.float32)
    for s, key in enumerate(order):
        if key is not None:
            name, m, k = key
            out[s // 8, :, s % 8, :] = mats[name][128 * k:128 * k + 128, 128 * m:128 * m + 128]
    return out


def params(inp):
    hp = np.concatenate([np.arange(0, 16), np.arange(32, 48), np.arange(16, 32), np.arange(48, 64)])
    gp = np.concatenate([64 * h + hp for h in range(4)])
    prm = np.zeros((128, NPC), np.float32)

    def put(name, v):
        o, n = PCOL[name]
        prm[:, o:o + n] = v

    put("eps", EPS)
    put("one", 1.0)
    put("halfpi", np.pi / 2)
    put("b_mod", columns(inp["b_mod"][0]))
    put("norm1_g", columns(inp["norm1_g"][0]))
    put("norm2_g", columns(inp["norm2_g"][0]))
    put("na_q_g", columns(np.concatenate([inp["na_q_norm_g"][0]] * 2)))
    put("na_k_g", columns(np.concatenate([inp["na_k_norm_g"][0]] * 2)))
    put("b_alpha", columns(np.ascontiguousarray(inp["gla_b_alpha"][0][:, gp])))
    put("gla_norm_g", columns(inp["gla_norm_g"][0]))
    im = (np.float32(10000.0) ** (-np.arange(0, 32, 2, dtype=np.float32) / np.float32(32))).astype(np.float32)
    ir = (np.float32(10000.0) ** (-np.arange(0, 128, 2, dtype=np.float32) / np.float32(128))).astype(np.float32)
    put("inv_m", np.tile(im, 8)[:, None])
    put("sgn_m", np.tile(np.repeat(np.float32([-1, 1]), 16), 4)[:, None])
    put("inv_r", np.tile(ir, 2)[:, None])
    put("sgn_r", np.repeat(np.float32([1, -1]), 64)[:, None])
    put("decay", np.broadcast_to(inp["ret_decay_logits_2"].reshape(1, 16), (128, 16)))
    for l in range(2):
        L = str(l)
        for n, k in (("mix_pre", "ln_mix_pre_2"), ("mix_post", "ln_mix_post_2"), ("ffn_pre", "ln_ffn_pre_2"),
                     ("ffn_post", "ln_ffn_post_2"), ("q_norm", "mla_q_norm_2"), ("kv_norm", "mla_kv_norm_2"),
                     ("b_dw", "conv_b_dw_2"), ("cln_g", "conv_ln_g_2"), ("cln_b", "conv_ln_b_2"),
                     ("gn_g", "ret_gn_g_2")):
            put(n + L, columns(inp[k][l]))
        put("w_dw" + L, inp["conv_w_dw_2"][l].reshape(31, 4, 128).transpose(2, 1, 0).reshape(128, 124))
    return prm


SHAPES = {
    "wst": ((NB, 128, 8, 128), F32), "prm": ((128, NPC), F32), "ccol": ((128, 8, 2), F32),
    "wmod": ((96, 128, 512), F32), "xT": ((128, 8, 512), F32), "cT": ((128, 4, 512), F32),
    "cst": ((128, 5, 128), F32), "tabG": ((128, 1792), F32), "tabA": ((128, 1792), F32), "wal": ((32, 2, 256), F32),
    "bias": ((16, 128, 2, 256), F32), "pos": ((128, 512), I32),
}


def arrays(inp, order):
    cst, tabG, tabA = tables()
    gp = np.concatenate([64 * h + np.concatenate([np.arange(0, 16), np.arange(32, 48), np.arange(16, 32),
                                                  np.arange(48, 64)]) for h in range(4)])
    wal = np.zeros((32, 2, 256), np.float32)
    wal[0:16, 0] = inp["gla_w_alpha"][0, 0][:, gp]
    wal[16:32, 1] = inp["gla_w_alpha"][0, 1][:, gp]
    wm = inp["w_mod"][0].reshape(8, 128, 12, 512).transpose(2, 0, 1, 3).reshape(96, 128, 512)
    got = {
        "wst": stream(weights(inp), order), "prm": params(inp),
        "ccol": np.stack([columns(inp["c"][0]), columns(inp["c_ctx"])], 2),
        "wmod": wm, "xT": inp["x"][0].T.reshape(8, 128, 512).transpose(1, 0, 2),
        "cT": inp["ctx"][0].T.reshape(4, 2, 128, 256).transpose(2, 0, 1, 3).reshape(128, 4, 512),
        "cst": cst, "tabG": tabG, "tabA": tabA, "wal": wal, "bias": na_bias(inp["na_rpb"][0]),
        "pos": np.repeat(inp["positions_2"][0:1], 128, 0),
    }
    return {k: np.ascontiguousarray(v) for k, v in got.items()}


def kernel(**inputs):
    import concourse.bacc as _bacc
    from concourse.bass_utils import run_bass_kernel_spmd as _run

    inp = {k: np.asarray(v) for k, v in inputs.items()}
    nc = _bacc.Bacc("TRN2", target_bir_lowering=False, num_devices=1)
    aps = {k: nc.dram_tensor(f"in_{k}", s, dt, kind="ExternalInput").ap() for k, (s, dt) in SHAPES.items()}
    out = nc.dram_tensor("out_x", (128, 8, 512), F32, kind="ExternalOutput").ap()
    order = []
    program(nc, aps, out, order)
    assert len(order) == 8 * NB, len(order) / 8
    got = arrays(inp, order)
    r = _run(nc, [{f"in_{k}": v for k, v in got.items()}], core_ids=[0])
    y = r.results[0]["out_x"]
    return np.ascontiguousarray(y.transpose(1, 0, 2).reshape(1024, 512).T)[None]
```
